# Optimizing a Trainium2 kernel written in Bass

```python
import numpy as np
import jax
import jax.numpy as jnp
from jax import lax

D_MODEL = 1024
BATCH = 1
SEQ = 1024
DEPTH = 1

GLA_HEADS = 4
GLA_DK = D_MODEL // 2
GLA_DV = D_MODEL
GLA_HEAD_DK = GLA_DK // GLA_HEADS
GLA_HEAD_DV = GLA_DV // GLA_HEADS
GLA_RANK = 16
GLA_TAU = 16.0
GLA_CHUNK = 64

LRU_WIDTH = D_MODEL
LRU_BLOCKS = 8
LRU_BLOCK_W = LRU_WIDTH // LRU_BLOCKS
CONV_WIDTH = 4
LRU_C = 8.0

PEER_HEADS = 8
PEER_NKEYS = 128
PEER_EXPERTS = PEER_NKEYS * PEER_NKEYS
PEER_DKEY = 256
PEER_HALF = PEER_DKEY // 2
PEER_TOPK = 16
PEER_TOKEN_BLOCK = 128

EPS = 1e-6

SPLIT_SIZES = (GLA_DK, GLA_DK, GLA_DV, GLA_DV, GLA_RANK, LRU_WIDTH, LRU_WIDTH, D_MODEL, D_MODEL)
D_IN = 2 * GLA_DK + 2 * GLA_DV + GLA_RANK + 2 * LRU_WIDTH + 2 * D_MODEL

kernel_name = 'hybrid_gla_rglru_peer_block'

def rms_norm(x, gain):
    xf = x.astype(jnp.float32)
    y = xf * lax.rsqrt(jnp.mean(xf * xf, axis=-1, keepdims=True) + EPS)
    return y * gain.astype(jnp.float32)

def gla_branch(q, k, v, r, a_low, w_alpha, b_alpha, gla_norm):
    f32 = jnp.float32
    B, S, _ = q.shape
    n_chunks = S // GLA_CHUNK
    log_alpha = jax.nn.log_sigmoid((a_low @ w_alpha + b_alpha).astype(f32)) / GLA_TAU

    def to_chunks(t, d):
        return t.astype(f32).reshape(B, n_chunks, GLA_CHUNK, GLA_HEADS, d).transpose(1, 0, 3, 2, 4)

    qc = to_chunks(q, GLA_HEAD_DK) * (GLA_HEAD_DK ** -0.5)
    kc = to_chunks(k, GLA_HEAD_DK)
    vc = to_chunks(v, GLA_HEAD_DV)
    gc = to_chunks(log_alpha, GLA_HEAD_DK)
    causal = jnp.tril(jnp.ones((GLA_CHUNK, GLA_CHUNK), dtype=bool))[:, :, None]

    def chunk_step(state, inp):
        qb, kb, vb, gb = inp
        cum = jnp.cumsum(gb, axis=2)
        cum_last = cum[:, :, -1:, :]
        o_inter = jnp.einsum('bhtk,bhkv->bhtv', qb * jnp.exp(cum), state)
        rel = cum[:, :, :, None, :] - cum[:, :, None, :, :]
        decay = jnp.exp(jnp.where(causal, rel, -jnp.inf))
        scores = jnp.einsum('bhtk,bhsk,bhtsk->bhts', qb, kb, decay)
        o_intra = jnp.einsum('bhts,bhsv->bhtv', scores, vb)
        k_dec = kb * jnp.exp(cum_last - cum)
        state = jnp.exp(cum_last[:, :, 0, :])[..., None] * state + jnp.einsum('bhsk,bhsv->bhkv', k_dec, vb)
        return state, o_inter + o_intra

    state0 = jnp.zeros((B, GLA_HEADS, GLA_HEAD_DK, GLA_HEAD_DV), f32)
    _, o = lax.scan(chunk_step, state0, (qc, kc, vc, gc))
    o = o.transpose(1, 0, 3, 2, 4).reshape(B, S, GLA_HEADS, GLA_HEAD_DV)
    o = rms_norm(o, gla_norm.reshape(GLA_HEADS, GLA_HEAD_DV)).reshape(B, S, GLA_DV)
    return o * jax.nn.silu(r.astype(f32))

def rg_lru_branch(xl, xg, conv_w, conv_b, lru_w_a, lru_b_a, lru_w_x, lru_b_x, lru_lambda):
    f32 = jnp.float32
    B, S, W = xl.shape
    xc = lax.conv_general_dilated(
        xl.astype(f32), conv_w.astype(f32)[:, None, :], window_strides=(1,),
        padding=[(CONV_WIDTH - 1, 0)], dimension_numbers=('NWC', 'WIO', 'NWC'),
        feature_group_count=W) + conv_b.astype(f32)
    xb = xc.reshape(B, S, LRU_BLOCKS, LRU_BLOCK_W)
    gate_r = jax.nn.sigmoid(jnp.einsum('bsni,nij->bsnj', xb, lru_w_a.astype(f32)) + lru_b_a.astype(f32)).reshape(B, S, W)
    gate_i = jax.nn.sigmoid(jnp.einsum('bsni,nij->bsnj', xb, lru_w_x.astype(f32)) + lru_b_x.astype(f32)).reshape(B, S, W)
    log_a = -LRU_C * gate_r * jax.nn.softplus(-lru_lambda.astype(f32))
    a = jnp.exp(log_a)
    u = jnp.sqrt(jnp.maximum(-jnp.expm1(2.0 * log_a), 0.0)) * (gate_i * xc)

    def combine(left, right):
        a_l, h_l = left
        a_r, h_r = right
        return a_l * a_r, a_r * h_l + h_r

    _, h = lax.associative_scan(combine, (a, u), axis=1)
    return h * jax.nn.gelu(xg.astype(f32))

def token_mixers(h, w_in, w_alpha, b_alpha, gla_norm, conv_w, conv_b, lru_w_a, lru_b_a,
                 lru_w_x, lru_b_x, lru_lambda, w_out):
    proj = h @ w_in
    offsets = np.cumsum(SPLIT_SIZES)[:-1].tolist()
    q, k, v, r, a_low, xl, xg, g_a, g_b = jnp.split(proj, offsets, axis=-1)
    y_gla = gla_branch(q, k, v, r, a_low, w_alpha, b_alpha, gla_norm)
    y_lru = rg_lru_branch(xl, xg, conv_w, conv_b, lru_w_a, lru_b_a, lru_w_x, lru_b_x, lru_lambda)
    merged = (jax.nn.sigmoid(g_a.astype(jnp.float32)) * y_gla
              + jax.nn.sigmoid(g_b.astype(jnp.float32)) * y_lru)
    return merged.astype(h.dtype) @ w_out

def peer_tokens(xt, w_query, sub_keys, u_table, v_table):
    f32 = jnp.float32
    T = xt.shape[0]
    qry = (xt @ w_query).astype(f32).reshape(T, PEER_HEADS, 2, PEER_HALF)
    sub_scores = jnp.einsum('thpd,hpnd->thpn', qry, sub_keys.astype(f32))
    top_s, top_i = lax.top_k(sub_scores, PEER_TOPK)
    cand_s = (top_s[:, :, 0, :, None] + top_s[:, :, 1, None, :]).reshape(T, PEER_HEADS, PEER_TOPK * PEER_TOPK)
    cand_i = (top_i[:, :, 0, :, None] * PEER_NKEYS + top_i[:, :, 1, None, :]).reshape(T, PEER_HEADS, PEER_TOPK * PEER_TOPK)
    best_s, best_pos = lax.top_k(cand_s, PEER_TOPK)
    expert_idx = jnp.take_along_axis(cand_i, best_pos, axis=-1)
    gates = jax.nn.softmax(best_s, axis=-1)
    u_sel = jnp.take(u_table, expert_idx, axis=0)
    act = jax.nn.gelu(jnp.einsum('td,thkd->thk', xt, u_sel).astype(f32))
    v_sel = jnp.take(v_table, expert_idx, axis=0)
    return jnp.einsum('thk,thkd->td', (gates * act).astype(v_sel.dtype), v_sel)

def peer_ffn(h, w_query, sub_keys, u_table, v_table):
    B, S, D = h.shape
    blocks = h.reshape(-1, PEER_TOKEN_BLOCK, D)
    out = lax.map(lambda xt: peer_tokens(xt, w_query, sub_keys, u_table, v_table), blocks)
    return out.reshape(B, S, D)

def hybrid_layer(x, c, w_ada, b_ada, norm_pre_mix, norm_post_mix, w_in, w_alpha, b_alpha, gla_norm,
                 conv_w, conv_b, lru_w_a, lru_b_a, lru_w_x, lru_b_x, lru_lambda, w_out,
                 norm_pre_ffn, norm_post_ffn, peer_w_query, peer_sub_keys, peer_u, peer_v):
    f32 = jnp.float32
    mod = jax.nn.silu(c.astype(f32)) @ w_ada.astype(f32) + b_ada.astype(f32)
    shift1, scale1, gate1, shift2, scale2, gate2 = jnp.split(mod[:, None, :], 6, axis=-1)
    h = rms_norm(x, norm_pre_mix) * (1.0 + scale1) + shift1
    y = token_mixers(h, w_in, w_alpha, b_alpha, gla_norm, conv_w, conv_b, lru_w_a, lru_b_a,
                     lru_w_x, lru_b_x, lru_lambda, w_out)
    x = x + (gate1 * rms_norm(y, norm_post_mix)).astype(x.dtype)
    h = rms_norm(x, norm_pre_ffn) * (1.0 + scale2) + shift2
    y = peer_ffn(h, peer_w_query, peer_sub_keys, peer_u, peer_v)
    x = x + (gate2 * rms_norm(y, norm_post_ffn)).astype(x.dtype)
    return x

def setup_inputs(seed: int = 0) -> dict:
    key = jax.random.key(seed)
    ks = jax.random.split(key, 26)
    D = D_MODEL
    nrm = jax.random.normal

    def gain(k, n):
        return 1.0 + 0.05 * nrm(k, (DEPTH, n), jnp.float32)

    lam_u = jax.random.uniform(ks[17], (DEPTH, LRU_WIDTH), jnp.float32, minval=0.9, maxval=0.999)
    lam_p = lam_u ** (1.0 / LRU_C)
    return {
        'x': nrm(ks[0], (BATCH, SEQ, D), jnp.float32),
        'c': nrm(ks[1], (BATCH, D), jnp.float32),
        'w_ada': 0.5 * D ** -0.5 * nrm(ks[2], (DEPTH, D, 6 * D), jnp.float32),
        'b_ada': 0.02 * nrm(ks[3], (DEPTH, 6 * D), jnp.float32),
        'norm_pre_mix': gain(ks[4], D),
        'norm_post_mix': gain(ks[5], D),
        'w_in': D ** -0.5 * nrm(ks[6], (DEPTH, D, D_IN), jnp.float32),
        'w_alpha': GLA_RANK ** -0.5 * nrm(ks[7], (DEPTH, GLA_RANK, GLA_DK), jnp.float32),
        'b_alpha': 0.1 * nrm(ks[8], (DEPTH, GLA_DK), jnp.float32),
        'gla_norm': gain(ks[9], GLA_DV),
        'conv_w': CONV_WIDTH ** -0.5 * nrm(ks[10], (DEPTH, CONV_WIDTH, LRU_WIDTH), jnp.float32),
        'conv_b': 0.02 * nrm(ks[11], (DEPTH, LRU_WIDTH), jnp.float32),
        'lru_w_a': LRU_BLOCK_W ** -0.5 * nrm(ks[12], (DEPTH, LRU_BLOCKS, LRU_BLOCK_W, LRU_BLOCK_W), jnp.float32),
        'lru_b_a': 0.02 * nrm(ks[13], (DEPTH, LRU_BLOCKS, LRU_BLOCK_W), jnp.float32),
        'lru_w_x': LRU_BLOCK_W ** -0.5 * nrm(ks[14], (DEPTH, LRU_BLOCKS, LRU_BLOCK_W, LRU_BLOCK_W), jnp.float32),
        'lru_b_x': 0.02 * nrm(ks[15], (DEPTH, LRU_BLOCKS, LRU_BLOCK_W), jnp.float32),
        'lru_lambda': jnp.log(lam_p) - jnp.log1p(-lam_p),
        'w_out': D ** -0.5 * nrm(ks[16], (DEPTH, D, D), jnp.float32),
        'norm_pre_ffn': gain(ks[18], D),
        'norm_post_ffn': gain(ks[19], D),
        'peer_w_query': D ** -0.5 * nrm(ks[20], (DEPTH, D, PEER_HEADS * PEER_DKEY), jnp.float32),
        'peer_sub_keys': PEER_HALF ** -0.5 * nrm(ks[21], (DEPTH, PEER_HEADS, 2, PEER_NKEYS, PEER_HALF), jnp.float32),
        'peer_u': D ** -0.5 * nrm(ks[22], (DEPTH, PEER_EXPERTS, D), jnp.float32),
        'peer_v': D ** -0.5 * nrm(ks[23], (DEPTH, PEER_EXPERTS, D), jnp.float32),
    }

def reference(x, c, w_ada, b_ada, norm_pre_mix, norm_post_mix, w_in, w_alpha, b_alpha, gla_norm,
              conv_w, conv_b, lru_w_a, lru_b_a, lru_w_x, lru_b_x, lru_lambda, w_out,
              norm_pre_ffn, norm_post_ffn, peer_w_query, peer_sub_keys, peer_u, peer_v):
    for l in range(DEPTH):
        x = hybrid_layer(x, c, w_ada[l], b_ada[l], norm_pre_mix[l], norm_post_mix[l], w_in[l],
                         w_alpha[l], b_alpha[l], gla_norm[l], conv_w[l], conv_b[l], lru_w_a[l],
                         lru_b_a[l], lru_w_x[l], lru_b_x[l], lru_lambda[l], w_out[l],
                         norm_pre_ffn[l], norm_post_ffn[l], peer_w_query[l], peer_sub_keys[l],
                         peer_u[l], peer_v[l])
    return x


_drawn_inputs = setup_inputs


def setup_inputs(seed=0):
    import zlib

    import numpy as np

    out = dict(_drawn_inputs(seed))
    spreads = {}
    factors = {'lru_b_a': 6.464, 'lru_b_x': 4.186, 'norm_post_ffn': 3.994}
    for name, (base, spread) in spreads.items():
        noise = np.random.default_rng([zlib.crc32(name.encode()), seed]).standard_normal(out[name].shape)
        drawn = base * np.exp(spread * noise) if base else spread * noise
        out[name] = jnp.asarray(drawn.astype(out[name].dtype))
    for name, factor in factors.items():
        out[name] = (out[name] * factor).astype(out[name].dtype)
    return out
```

```python
from contextlib import ExitStack

import concourse.bass as bass
from concourse import mybir

F32 = mybir.dt.float32
U32 = mybir.dt.uint32
ALU = mybir.AluOpType
ACT = mybir.ActivationFunctionType
AX = mybir.AxisListType

P = 128
D = 1024
T = 1024
KC = D // P
TC = T // P
HALF = 512
EPS = 1e-6
HEADS, DK, DV, RANK = 4, 128, 256, 16
TAU = 16.0
LEVELS = 7
NPAR = 8
SCAN_C = 8.0
GELU_A, GELU_B = 0.044715, 0.7978845608028654
MODS = 6
PH, NK, TOPK = 8, 128, 16
SLOTS = PH * TOPK
NEG = -3.0e38


class Chain:

    def __init__(self, eng, sem, base=0):
        self.eng, self.sem, self.base, self.n, self.outer = eng, sem, base, 0, []

    def __call__(self, ins):
        self.n += 1
        ins.then_inc(self.sem, 1)
        self.eng.wait_ge(self.sem, self.base + self.n)

    def loop(self, i, per):
        self.outer.append((self.base, self.n, per))
        self.base, self.n = self.base + self.n + i * per, 0

    def end(self, count):
        base, n, per = self.outer.pop()
        assert self.n == per, (self.n, per)
        self.base, self.n = base, n + count * per


def conditioning_and_lru(nc, ctx, keep, a):
    hT, merged, mod, ident = keep["hT"], keep["merged"], keep["mod"], keep["ident"]
    with ExitStack() as scope:
        def sb(name, shape, dt=F32):
            return scope.enter_context(nc.sbuf_tensor(name, shape, dt))

        def sem(name):
            return ctx.enter_context(nc.semaphore(name))

        ps_xl = scope.enter_context(nc.psum_tensor("ps_xl", [P, T], F32))
        ps_xg = scope.enter_context(nc.psum_tensor("ps_xg", [P, T], F32))
        ps_gb = scope.enter_context(nc.psum_tensor("ps_gb", [P, T], F32))
        ps_gate = scope.enter_context(nc.psum_tensor("ps_gate", [P, T], F32))

        mod1 = sb("mod1", [P, 2 * D])
        ada = sb("ada", [P, KC, HALF])
        ada_bias = sb("ada_bias", [P, HALF])
        ada_sum = sb("ada_sum", [P, HALF])
        ones = sb("ones1", [P, P])
        cT = sb("cT", [P, KC])
        eps = sb("eps1", [P, 1])
        cact = sb("cact", [P, KC])
        gain = sb("gain1", [P, KC])
        A1 = sb("A1", [P, KC])
        S1 = sb("S1", [P, KC])
        par = sb("par", [P, KC * NPAR])
        ptmp = sb("ptmp", [P, 5, KC])
        diag = sb("diag1", [P, D])
        xt = sb("xt", [P, 2, D])
        xn = sb("xn", [P, D])
        junk = sb("junk1", [P, D])
        ss = sb("ss1", [P, 1])
        rstd = sb("rstd1", [P, 1])
        wt = sb("wt", [P, 3, KC, P])
        wgate = sb("wgate", [P, 2, P])
        parj = sb("parj", [P, NPAR])
        xlp = sb("xlp", [P, 3 + T])
        xc = sb("xc", [P, T])
        xg = sb("xg", [P, T])
        pin = sb("pin", [P, T])
        tg = sb("tg", [P, T])
        tb = sb("tb", [P, T])
        tr = sb("tr", [P, T])
        ti = sb("ti", [P, T])
        av = sb("av", [P, T])
        th = sb("th", [P, T])
        mu = sb("mu", [P, T])

        small_in = sem("small_in")
        ada_in = sem("ada_in")
        ada_used = sem("ada_used")
        ada_ready = sem("ada_ready")
        ada_done = sem("ada_done")
        mod_out = sem("mod_out")
        c_tanh = sem("c_tanh")
        c_ready = sem("c_ready")
        par_abs = sem("par_abs")
        par_exp = sem("par_exp")
        consts = sem("consts1")
        x_in = [sem("x_in0"), sem("x_in1")]
        x_sq = sem("x_sq")
        x_rstd = sem("x_rstd")
        x_root = sem("x_root")
        x_scaled = sem("x_scaled")
        x_turned = sem("x_turned")
        hT_out = sem("hT_out")
        w_in = [sem(f"w_in{i}") for i in range(3)]
        wg_in = sem("wg_in")
        p_xl, p_xg, p_gb = sem("p_xl"), sem("p_xg"), sem("p_gb")
        p_gr, p_gi = sem("p_gr"), sem("p_gi")
        xl_out, xg_out, tb_out, tr_out, ti_out = (sem(n) for n in ("xl_out", "xg_out", "tb_out", "tr_out", "ti_out"))
        xc_ready, pin_ready, nla_ready = sem("xc_ready"), sem("pin_ready"), sem("nla_ready")
        parj_ready = sem("parj_ready")
        tg_out, a_out, th_out = sem("tg_out"), sem("a_out"), sem("th_out")
        lru_out = sem("lru_out")
        mu2_ready, mu_root = sem("mu2_ready"), sem("mu_root")
        dve_step = sem("dve_step1")
        act_step = sem("act_step1")

        block = scope.enter_context(nc.Block())

        @block.sync
        def _(sp):
            sp.dma_start(cT[:], a["cT"]).then_inc(small_in, 16)
            sp.dma_start(gain[:], a["gain1"]).then_inc(small_in, 16)
            sp.dma_start(par[:], a["lru_par"]).then_inc(small_in, 16)
            sp.dma_start(ident[:], a["ident"]).then_inc(small_in, 16)
            with sp.Fori(0, 4) as n:
                sp.wait_ge(ada_used, n)
                sp.wait_ge(mod_out, n)
                sp.dma_start(ada[:], a["w_ada"][bass.ds(n, 1)].rearrange("o p k c -> p (o k) c")).then_inc(ada_in, 16)
                sp.dma_start(ada_bias[:], a["b_ada"][bass.ds(n, 1), :].broadcast_to([P, HALF])).then_inc(ada_in, 16)
            for i in range(3):
                sp.dma_start(wt[:, i], a["w_lru"][0, i]).then_inc(w_in[i], 16)
            sp.dma_start(wgate[:], a["lru_w"][0]).then_inc(wg_in, 16)
            with sp.Fori(0, KC - 1) as j:
                sp.wait_ge(ada_used, j + 4)
                sp.wait_ge(mod_out, j + 4)
                sp.dma_start(ada[:], a["w_ada"][bass.ds(j + 4, 1)].rearrange("o p k c -> p (o k) c")).then_inc(ada_in, 16)
                sp.dma_start(ada_bias[:], a["b_ada"][bass.ds(j + 4, 1), :].broadcast_to([P, HALF])).then_inc(ada_in, 16)
                for i, done in enumerate((p_xl, p_xg, p_gb)):
                    sp.wait_ge(done, j + 1)
                    sp.dma_start(wt[:, i], a["w_lru"][bass.ds(j + 1, 1), i].rearrange("o p k c -> p (o k) c")).then_inc(w_in[i], 16)
                sp.wait_ge(p_gi, j + 1)
                sp.dma_start(wgate[:], a["lru_w"][bass.ds(j + 1, 1)].rearrange("o p g c -> p (o g) c")).then_inc(wg_in, 16)
            sp.wait_ge(ada_used, 11)
            sp.wait_ge(mod_out, 11)
            sp.dma_start(ada[:], a["w_ada"][11]).then_inc(ada_in, 16)
            sp.dma_start(ada_bias[:], a["b_ada"][11:12, :].broadcast_to([P, HALF])).then_inc(ada_in, 16)

        @block.gpsimd
        def _(pool):
            nc.gpsimd.memset(ones[:], 1.0).then_inc(consts, 1)
            nc.gpsimd.memset(xlp[:, 0:3], 0.0).then_inc(consts, 1)
            nc.gpsimd.memset(eps[:], EPS).then_inc(consts, 1)
            for s in range(2):
                pool.dma_start(xt[:, s], a["x"][s]).then_inc(x_in[s], 16)
            with pool.Fori(0, TC // 2 - 1) as g:
                for s in range(2):
                    pool.wait_ge(x_scaled, 2 * g + s + 1)
                    pool.dma_start(xt[:, s], a["x"][bass.ds(2 * g + s + 2, 1)].rearrange("o p d -> (o p) d")).then_inc(x_in[s], 16)

        @block.scalar
        def _(act):
            step = Chain(act, act_step)
            act.wait_ge(small_in, 64)
            nc.scalar.activation(cact[:], cT[:], ACT.Tanh, scale=0.5).then_inc(c_tanh, 1)
            act.wait_ge(par_abs, 1)
            nc.scalar.activation(ptmp[:, 1], ptmp[:, 0], ACT.Exp, scale=-1.0).then_inc(par_exp, 1)
            act.wait_ge(consts, 3)
            with act.Fori(0, TC // 2) as g:
                for s in range(2):
                    act.wait_ge(x_in[s], 16 * (g + 1))
                    act.wait_ge(x_rstd, 2 * g + s)
                    nc.scalar.activation(junk[:], xt[:, s], ACT.Square, scale=D ** -0.5, accum_out=ss[:]).then_inc(x_sq, 1)
                    act.wait_ge(x_sq, 2 * g + s + 1)
                    nc.scalar.activation(ss[:], ss[:], ACT.Sqrt, bias=eps[:]).then_inc(x_root, 1)
                    act.wait_ge(x_rstd, 2 * g + s + 1)
                    act.wait_ge(x_turned, 2 * g + s)
                    nc.scalar.activation(xn[:], xt[:, s], ACT.Copy, scale=rstd[:]).then_inc(x_scaled, 1)
            with act.Fori(0, KC) as j:
                act.wait_ge(p_xl, j + 1)
                act.wait_ge(xc_ready, j)
                act.wait_ge(consts, 3)
                nc.scalar.activation(xlp[:, 3:3 + T], ps_xl[:], ACT.Copy).then_inc(xl_out, 1)
                act.wait_ge(p_xg, j + 1)
                act.wait_ge(lru_out, j)
                nc.scalar.activation(xg[:], ps_xg[:], ACT.Copy).then_inc(xg_out, 1)
                act.wait_ge(pin_ready, j + 1)
                nc.scalar.activation(tg[:], pin[:], ACT.Tanh, scale=GELU_B).then_inc(tg_out, 1)
                act.wait_ge(p_gb, j + 1)
                nc.scalar.activation(tb[:], ps_gb[:], ACT.Tanh, scale=0.5).then_inc(tb_out, 1)
                act.wait_ge(p_gr, j + 1)
                act.wait_ge(parj_ready, j + 1)
                nc.scalar.activation(tr[:], ps_gate[:], ACT.Tanh, scale=0.5, bias=parj[:, 5:6]).then_inc(tr_out, 1)
                act.wait_ge(p_gi, j + 1)
                nc.scalar.activation(ti[:], ps_xl[:], ACT.Tanh, scale=0.5, bias=parj[:, 6:7]).then_inc(ti_out, 1)
                act.wait_ge(nla_ready, j + 1)
                nc.scalar.activation(av[:], tr[:], ACT.Exp, scale=-1.0).then_inc(a_out, 1)
                nc.scalar.activation(th[:], tr[:], ACT.Tanh).then_inc(th_out, 1)
                act.wait_ge(mu2_ready, j + 1)
                nc.scalar.activation(mu[:], mu[:], ACT.Sqrt, scale=2.0).then_inc(mu_root, 1)

        @block.tensor
        def _(pe):
            def ada_columns(n):
                pe.wait_ge(ada_ready, n + 1)
                pe.wait_ge(consts, 1)
                pe.wait_ge(mod_out, n)
                nc.tensor.matmul(ps_gate[:, 0:HALF], ones[:], ada_sum[:], start=True, stop=True).then_inc(ada_done, 1)

            with pe.Fori(0, 4) as n:
                ada_columns(n)
            with pe.Fori(0, TC) as c:
                pe.wait_ge(x_scaled, c + 1)
                pe.wait_ge(small_in, 64)
                pe.wait_ge(hT_out, c)
                for k in range(KC):
                    last = nc.tensor.transpose(ps_xl[:, k * P:(k + 1) * P], xn[:, k * P:(k + 1) * P], ident[:])
                last.then_inc(x_turned, 1)
            pe.wait_ge(hT_out, TC)

            def project(ps, slot, j, done, free, free_count):
                pe.wait_ge(w_in[slot], 16 * (j + 1))
                pe.wait_ge(free, free_count)
                for s in range(T // HALF):
                    for k in range(KC):
                        last = nc.tensor.matmul(ps[:, s * HALF:(s + 1) * HALF], wt[:, slot, k], hT[:, k, s * HALF:(s + 1) * HALF],
                                                start=(k == 0), stop=(k == KC - 1))
                last.then_inc(done, 1)

            with pe.Fori(0, KC) as j:
                project(ps_xl, 0, j, p_xl, ti_out, j)
                project(ps_xg, 1, j, p_xg, xg_out, j)
                pe.wait_ge(tr_out, j)
                ada_columns(j + 4)
                project(ps_gb, 2, j, p_gb, tb_out, j)
                pe.wait_ge(wg_in, 16 * (j + 1))
                pe.wait_ge(xc_ready, j + 1)
                pe.wait_ge(mod_out, j + 5)
                for s in range(T // HALF):
                    last = nc.tensor.matmul(ps_gate[:, s * HALF:(s + 1) * HALF], wgate[:, 0], xc[:, s * HALF:(s + 1) * HALF], start=True, stop=True)
                last.then_inc(p_gr, 1)
                pe.wait_ge(xl_out, j + 1)
                for s in range(T // HALF):
                    last = nc.tensor.matmul(ps_xl[:, s * HALF:(s + 1) * HALF], wgate[:, 1], xc[:, s * HALF:(s + 1) * HALF], start=True, stop=True)
                last.then_inc(p_gi, 1)

        @block.vector
        def _(dve):
            v = nc.vector
            step = Chain(dve, dve_step)

            def ada_sums(n):
                dve.wait_ge(ada_in, 32 * (n + 1))
                dve.wait_ge(ada_done, n)
                step(v.tensor_scalar(ada_sum[:], ada[:, 0], cact[:, 0:1], None, ALU.mult))
                for k in range(1, KC - 1):
                    step(v.scalar_tensor_tensor(ada_sum[:], ada[:, k], cact[:, k:k + 1], ada_sum[:], ALU.mult, ALU.add))
                ins = v.scalar_tensor_tensor(ada_sum[:], ada[:, KC - 1], cact[:, KC - 1:KC], ada_sum[:], ALU.mult, ALU.add)
                ins.then_inc(ada_ready, 1)
                dve.wait_ge(ada_ready, n + 1)
                dve.sem_inc(ada_used, 1)

            def mod_columns(n, dst, at):
                dve.wait_ge(ada_done, n + 1)
                v.tensor_tensor(dst[:, bass.ds(at * HALF, HALF)], ps_gate[:, 0:HALF], ada_bias[:], ALU.add).then_inc(mod_out, 1)
                dve.wait_ge(mod_out, n + 1)

            dve.wait_ge(small_in, 64)
            lam = par[:].rearrange("p (j q) -> p j q", q=NPAR)[:, :, 7]
            v.scalar_tensor_tensor(ptmp[:, 0], lam, -1.0, lam, ALU.mult, ALU.max).then_inc(par_abs, 1)
            dve.wait_ge(c_tanh, 1)
            step(v.tensor_scalar(cact[:], cact[:], 1.0, 0.5, ALU.add, ALU.mult))
            step(v.tensor_tensor(cact[:], cact[:], cT[:], ALU.mult))
            dve.wait_ge(par_exp, 1)
            step(v.tensor_scalar(ptmp[:, 2], ptmp[:, 1], 2.0, None, ALU.add))
            step(v.reciprocal(ptmp[:, 3], ptmp[:, 2]))
            step(v.tensor_tensor(ptmp[:, 2], ptmp[:, 1], ptmp[:, 3], ALU.mult))
            step(v.tensor_tensor(ptmp[:, 3], ptmp[:, 2], ptmp[:, 2], ALU.mult))
            step(v.tensor_scalar(ptmp[:, 4], ptmp[:, 3], 1.0 / 17, None, ALU.mult))
            for m in (15, 13, 11, 9, 7, 5, 3):
                step(v.scalar_tensor_tensor(ptmp[:, 4], ptmp[:, 4], 1.0 / m, ptmp[:, 3], ALU.add, ALU.mult))
            step(v.scalar_tensor_tensor(ptmp[:, 4], ptmp[:, 4], 1.0, ptmp[:, 2], ALU.add, ALU.mult))
            step(v.tensor_scalar(ptmp[:, 0], lam, -0.5 * SCAN_C, 0.0, ALU.mult, ALU.max))
            step(v.scalar_tensor_tensor(lam, ptmp[:, 4], SCAN_C, ptmp[:, 0], ALU.mult, ALU.add))
            halves = par[:].rearrange("p (j q) -> p j q", q=NPAR)[:, :, 5:7]
            step(v.tensor_scalar(halves, halves, 0.5, None, ALU.mult))

            step_in = step
            with dve.Fori(0, 4) as n:
                step.loop(n, KC - 1)
                ada_sums(n)
                mod_columns(n, mod1, n)
            step.end(4)
            for dst, m in ((S1, 0), (A1, 1)):
                step(v.tensor_tensor(diag[:].rearrange("p (k c) -> p k c", k=KC), mod1[:, m * D:(m + 1) * D].rearrange("p (k c) -> p k c", k=KC),
                                     ident[:].unsqueeze(1).broadcast_to([P, KC, P]), ALU.mult))
                step(v.tensor_reduce(dst[:], diag[:].rearrange("p (k c) -> p k c", k=KC), AX.X, ALU.add))
            step(v.scalar_tensor_tensor(A1[:], A1[:], 1.0, gain[:], ALU.add, ALU.mult))
            with dve.Fori(0, TC) as c:
                dve.wait_ge(x_root, c + 1)
                dve.wait_ge(x_scaled, c)
                v.reciprocal(rstd[:], ss[:]).then_inc(x_rstd, 1)
                dve.wait_ge(x_turned, c + 1)
                for k in range(KC):
                    last = v.tensor_scalar(hT[:, k, bass.ds(c * P, P)], ps_xl[:, k * P:(k + 1) * P], A1[:, k:k + 1], S1[:, k:k + 1], ALU.mult, ALU.add)
                last.then_inc(hT_out, 1)
            with dve.Fori(0, KC) as j:
                step.loop(j, (KC - 1) + 13)
                v.tensor_copy(parj[:], par[:, bass.ds(j * NPAR, NPAR)]).then_inc(parj_ready, 1)
                dve.wait_ge(xl_out, j + 1)
                dve.wait_ge(parj_ready, j + 1)
                step(v.tensor_scalar(xc[:], xlp[:, 3:3 + T], parj[:, 3:4], parj[:, 4:5], ALU.mult, ALU.add))
                step(v.scalar_tensor_tensor(xc[:], xlp[:, 2:2 + T], parj[:, 2:3], xc[:], ALU.mult, ALU.add))
                step(v.scalar_tensor_tensor(xc[:], xlp[:, 1:1 + T], parj[:, 1:2], xc[:], ALU.mult, ALU.add))
                v.scalar_tensor_tensor(xc[:], xlp[:, 0:T], parj[:, 0:1], xc[:], ALU.mult, ALU.add).then_inc(xc_ready, 1)
                ada_sums(j + 4)
                mod_columns(j + 4, mod, j)
                dve.wait_ge(xg_out, j + 1)
                step(v.scalar_tensor_tensor(pin[:], xg[:], GELU_A, xg[:], ALU.mult, ALU.mult))
                v.scalar_tensor_tensor(pin[:], pin[:], 1.0, xg[:], ALU.add, ALU.mult).then_inc(pin_ready, 1)
                dve.wait_ge(tr_out, j + 1)
                v.tensor_scalar(tr[:], tr[:], 1.0, parj[:, 7:8], ALU.add, ALU.mult).then_inc(nla_ready, 1)
                dve.wait_ge(th_out, j + 1)
                step(v.tensor_scalar(mu[:], th[:], 1.0, None, ALU.add))
                step(v.reciprocal(mu[:], mu[:]))
                v.scalar_tensor_tensor(mu[:], th[:], 0.0, mu[:], ALU.max, ALU.mult).then_inc(mu2_ready, 1)
                dve.wait_ge(ti_out, j + 1)
                step(v.scalar_tensor_tensor(ti[:], ti[:], 1.0, xc[:], ALU.add, ALU.mult))
                dve.wait_ge(mu_root, j + 1)
                step(v.scalar_tensor_tensor(mu[:], ti[:], 0.5, mu[:], ALU.mult, ALU.mult))
                dve.wait_ge(a_out, j + 1)
                step(v.tensor_tensor_scan(th[:], av[:], mu[:], 0.0, ALU.mult, ALU.add))
                dve.wait_ge(tg_out, j + 1)
                step(v.scalar_tensor_tensor(tg[:], tg[:], 1.0, xg[:], ALU.add, ALU.mult))
                dve.wait_ge(tb_out, j + 1)
                step(v.scalar_tensor_tensor(tg[:], tb[:], 1.0, tg[:], ALU.add, ALU.mult))
                step(v.tensor_scalar(tg[:], tg[:], 0.25, None, ALU.mult))
                step(v.tensor_tensor(merged[:, bass.ds(j * T, T)], th[:], tg[:], ALU.mult))
                dve.sem_inc(lru_out, 1)
            step.end(KC)


def gated_linear_attention(nc, ctx, keep, a, merged_dram):
    hT, merged, ident = keep["hT"], keep["merged"], keep["ident"]
    NL = LEVELS + 1
    with ExitStack() as scope:
        def sb(name, shape, dt=F32):
            return scope.enter_context(nc.sbuf_tensor(name, shape, dt))

        def sem(name):
            return ctx.enter_context(nc.semaphore(name))

        ps_a = scope.enter_context(nc.psum_tensor("ps_a", [P, T], F32))
        ps_b = scope.enter_context(nc.psum_tensor("ps_b", [P, T], F32))
        ps_s = scope.enter_context(nc.psum_tensor("ps_s", [P, NL * P], F32))
        ps_o = scope.enter_context(nc.psum_tensor("ps_o", [P, HALF], F32))
        ps_t = scope.enter_context(nc.psum_tensor("ps_t", [P, HALF], F32))
        s_banks = (ps_s, ps_b)
        o_banks = (ps_a[:, 0:DV], ps_a[:, HALF:HALF + DV])

        masks = sb("masks", [P, NL * P])
        restart = sb("restart", [P, T])
        eps = sb("eps2", [P, 1])
        w_al = sb("w_al", [P, KC, RANK])
        alow = sb("alow", [RANK, T])
        hpar = sb("hpar", [P, HEADS * 3])
        hp = sb("hp", [P, 3])
        w_alpha = sb("w_alpha", [RANK, DK])
        w_v = sb("w_v", [P, KC, DV])
        wr = sb("wr", [P, 3, KC, P])
        q = sb("q", [P, T])
        k = sb("k", [P, T])
        V = sb("V", [P, TC, DV])
        zl = sb("zl", [P, T])
        cum = sb("cum", [P, T])
        X = sb("X", [P, LEVELS, T])
        qe = sb("qe", [P, T])
        kd = sb("kd", [P, T])
        elast = sb("elast", [P, TC])
        gate = sb("gate", [P, 2, T])
        tnh = sb("tnh", [P, T])
        sm = sb("sm", [P, NL * P])
        S = sb("S", [P, 2, P])
        kdT = sb("kdT", [P, TC, DK])
        state = sb("state", [P, DV])
        junk = sb("junk2", [P, DV])
        ss = sb("ss2", [P, TC])
        rstd = sb("rstd2", [P, TC])
        on = sb("on", [P, 2, DV])
        oT = sb("oT", [P, 2, T])

        small_in, const = sem("small_in2"), sem("consts2")
        al_in, wal_in, wv_in = sem("al_in"), sem("walpha_in"), sem("wv_in")
        wr_in = [sem(f"wr_in{i}") for i in range(3)]
        al_done, al_out = sem("al_done"), sem("al_out")
        z_done, q_done, k_done, v_done = sem("z_done"), sem("q_done"), sem("k_done"), sem("v_done")
        rg_done = sem("rg_done")
        hp_ready = sem("hp_ready")
        z_abs, z_min, l_out = sem("z_abs"), sem("z_min"), sem("l_out")
        q_out, k_out, v_out = sem("q_out"), sem("k_out"), sem("v_out")
        diff_ready = sem("diff_ready")
        exp_out = sem("exp_out")
        x_ready = sem("x_ready")
        r_raw, rg_out = sem("r_raw"), sem("rg_out")
        gate_step = sem("gate_step")
        s_done, s_masked, s_ready = sem("s_done"), sem("s_masked"), sem("s_ready")
        kt_done, kt_out = sem("kt_done"), sem("kt_out")
        o_done, up_done, state_out = sem("o_done"), sem("up_done"), sem("state_out")
        o_sq, o_root, o_rstd, on_out = sem("o_sq"), sem("o_root"), sem("o_rstd"), sem("on_out")
        ot_done, ot_out = sem("ot_done"), sem("ot_out")
        head_out, merged_out = sem("head_out"), sem("merged_out")
        dve_step = sem("dve_step2")

        block = scope.enter_context(nc.Block())

        @block.sync
        def _(sp):
            sp.dma_start(w_al[:], a["w_al"]).then_inc(al_in, 16)
            sp.dma_start(masks[:], a["masks"]).then_inc(small_in, 16)
            sp.dma_start(hpar[:], a["head_par"]).then_inc(small_in, 16)

            def load_head(h, after):
                pick = (lambda t: t[bass.ds(h, 1)]) if after else (lambda t: t[0:1])
                if after:
                    sp.wait_ge(z_done, h)
                sp.dma_start(w_alpha[:], pick(a["w_alpha"]).rearrange("o r c -> (o r) c")).then_inc(wal_in, 16)
                before = ((rg_done, 4 * h - 2), (rg_done, 4 * h - 1), (rg_done, 4 * h), (q_done, h + 1), (k_done, h + 1), (rg_done, 4 * h + 1))
                for i, (used, count) in enumerate(before):
                    if i == 2:
                        if after:
                            sp.wait_ge(v_done, 2 * h)
                        sp.dma_start(w_v[:], pick(a["w_v"]).rearrange("o p k c -> p (o k) c")).then_inc(wv_in, 16)
                    if after or i >= 3:
                        sp.wait_ge(used, count)
                    sp.dma_start(wr[:, i % 3], pick(a["w_head"])[:, i].rearrange("o p k c -> p (o k) c")).then_inc(wr_in[i % 3], 16)

            load_head(0, False)
            with sp.Fori(1, HEADS) as h:
                load_head(h, True)
                sp.wait_ge(head_out, h)
                sp.dma_start(merged_dram[:, bass.ds(2 * (h - 1), 2), :], merged[:, bass.ds((h - 1) * 2 * T, 2 * T)].rearrange("p (j t) -> p j t", j=2)).then_inc(merged_out, 16)
            sp.wait_ge(head_out, HEADS)
            sp.dma_start(merged_dram[:, 2 * (HEADS - 1):, :], merged[:, (HEADS - 1) * 2 * T:].rearrange("p (j t) -> p j t", j=2)).then_inc(merged_out, 16)
            sp.wait_ge(merged_out, 16 * HEADS)

        @block.gpsimd
        def _(pool):
            nc.gpsimd.memset(eps[:], EPS).then_inc(const, 1)
            nc.gpsimd.memset(restart[:], 1.0).then_inc(const, 1)
            pool.wait_ge(const, 2)
            nc.gpsimd.memset(restart[:].rearrange("p (c t) -> p c t", t=P)[:, :, 0:1], 0.0).then_inc(const, 1)

        @block.scalar
        def _(act):
            act.wait_ge(const, 3)
            act.wait_ge(al_done, 1)
            nc.scalar.activation(alow[:], ps_a[0:RANK, :], ACT.Copy).then_inc(al_out, 1)
            with act.Fori(0, HEADS) as h:
                act.wait_ge(z_done, h + 1)
                act.wait_ge(hp_ready, h + 1)
                nc.scalar.activation(zl[:], ps_a[:], ACT.Abs, bias=hp[:, 0:1]).then_inc(z_abs, 1)
                act.wait_ge(z_abs, 2 * h + 1)
                nc.scalar.activation(zl[:], zl[:], ACT.Exp, scale=-1.0).then_inc(z_abs, 1)
                act.wait_ge(z_abs, 2 * h + 2)
                nc.scalar.activation(zl[:], zl[:], ACT.Ln, bias=1.0).then_inc(l_out, 1)
                act.wait_ge(q_done, h + 1)
                act.wait_ge(s_done, TC * h)
                nc.scalar.activation(q[:], ps_b[:], ACT.Copy, scale=DK ** -0.5).then_inc(q_out, 1)
                act.wait_ge(k_done, h + 1)
                nc.scalar.activation(k[:], ps_a[:], ACT.Copy).then_inc(k_out, 1)
                act.wait_ge(up_done, TC * h)
                for i, bank in enumerate((ps_b, ps_a)):
                    act.wait_ge(v_done, 2 * h + i + 1)
                    nc.scalar.activation(V[:, i * 4:(i + 1) * 4].rearrange("p c d -> p (c d)"), bank[:], ACT.Copy).then_inc(v_out, 1)
                for n in range(LEVELS):
                    half = P >> (n + 1)
                    pairs = X[:, n].rearrange("p (b w t) -> p b w t", w=2, t=half)
                    act.wait_ge(diff_ready, NL * h + n + 1)
                    nc.scalar.activation(pairs[:, :, 0], pairs[:, :, 0], ACT.Exp, scale=-1.0 / TAU)
                    nc.scalar.activation(pairs[:, :, 1], pairs[:, :, 1], ACT.Exp, scale=1.0 / TAU).then_inc(exp_out, 1)
                act.wait_ge(diff_ready, NL * h + NL)
                nc.scalar.activation(kd[:], kd[:], ACT.Exp, scale=-1.0 / TAU).then_inc(exp_out, 1)
                nc.scalar.activation(qe[:], cum[:], ACT.Exp, scale=1.0 / TAU).then_inc(exp_out, 1)
                nc.scalar.activation(elast[:], cum[:].rearrange("p (c t) -> p c t", t=P)[:, :, P - 1], ACT.Exp, scale=1.0 / TAU).then_inc(exp_out, 1)
                for i, bank in enumerate((ps_b, ps_a, ps_b, ps_a)):
                    act.wait_ge(rg_done, 4 * h + i + 1)
                    if i < 2:
                        act.wait_ge(head_out, h)
                        nc.scalar.activation(gate[:, i], bank[:], ACT.Copy).then_inc(r_raw, 1)
                    act.wait_ge(gate_step, 4 * h + i)
                    nc.scalar.activation(tnh[:], bank[:], ACT.Tanh, scale=0.5).then_inc(rg_out, 1)

                for i, bank in enumerate((ps_t, ps_o)):
                    act.wait_ge(kt_done, 2 * h + i + 1)
                    nc.scalar.activation(kdT[:, 4 * i:4 * i + 4].rearrange("p c d -> p (c d)"), bank[:], ACT.Copy).then_inc(kt_out, 1)

                def turned_out(c):
                    act.wait_ge(ot_done, TC * h + c + 1)
                    nc.scalar.activation(oT[:, :, c * P:(c + 1) * P], ps_t[:, 0:2 * P].rearrange("p (v t) -> p v t", v=2), ACT.Copy).then_inc(ot_out, 1)

                for c in range(TC):
                    n = TC * h + c
                    o = o_banks[c % 2]
                    act.wait_ge(o_done, n + 1)
                    nc.scalar.activation(junk[:], o, ACT.Square, scale=DV ** -0.5, accum_out=ss[:, c:c + 1]).then_inc(o_sq, 1)
                    act.wait_ge(o_sq, n + 1)
                    nc.scalar.activation(ss[:, c:c + 1], ss[:, c:c + 1], ACT.Sqrt, bias=eps[:]).then_inc(o_root, 1)
                    act.wait_ge(o_rstd, n + 1)
                    if c >= 2:
                        act.wait_ge(ot_done, n - 1)
                    nc.scalar.activation(on[:, c % 2], o, ACT.Copy, scale=rstd[:, c:c + 1]).then_inc(on_out, 1)
                    if c >= 1:
                        turned_out(c - 1)
                turned_out(TC - 1)

        @block.tensor
        def _(pe):
            def project(out, weights, rows=P):
                for s in range(T // HALF):
                    for kk in range(KC):
                        last = nc.tensor.matmul(out[0:rows, s * HALF:(s + 1) * HALF], weights[:, kk], hT[:, kk, s * HALF:(s + 1) * HALF],
                                                start=(kk == 0), stop=(kk == KC - 1))
                return last

            pe.wait_ge(al_in, 16)
            project(ps_a, w_al, RANK).then_inc(al_done, 1)
            pe.wait_ge(al_out, 1)
            with pe.Fori(0, HEADS) as h:
                pe.wait_ge(wal_in, 16 * (h + 1))
                pe.wait_ge(on_out, TC * h)
                pe.wait_ge(state_out, TC * h)
                pe.wait_ge(s_masked, TC * h)
                for s in range(T // HALF):
                    last = nc.tensor.matmul(ps_a[:, s * HALF:(s + 1) * HALF], w_alpha[:], alow[:, s * HALF:(s + 1) * HALF], start=True, stop=True)
                last.then_inc(z_done, 1)
                pe.wait_ge(wr_in[0], 16 * (2 * h + 1))
                project(ps_b, wr[:, 0]).then_inc(q_done, 1)
                pe.wait_ge(z_abs, 2 * h + 1)
                pe.wait_ge(z_min, h + 1)
                pe.wait_ge(wr_in[1], 16 * (2 * h + 1))
                project(ps_a, wr[:, 1]).then_inc(k_done, 1)
                pe.wait_ge(wv_in, 16 * (h + 1))
                for i, (bank, free) in enumerate(((ps_b, q_out), (ps_a, k_out))):
                    pe.wait_ge(free, h + 1)
                    for c in range(4 * i, 4 * i + 4):
                        for kk in range(KC):
                            last = nc.tensor.matmul(bank[:, (c % 4) * DV:(c % 4 + 1) * DV], hT[:, kk, c * P:(c + 1) * P], w_v[:, kk],
                                                    start=(kk == 0), stop=(kk == KC - 1))
                    last.then_inc(v_done, 1)
                for i, bank in enumerate((ps_b, ps_a, ps_b, ps_a)):
                    if i < 2:
                        pe.wait_ge(v_out, 2 * h + i + 1)
                    else:
                        pe.wait_ge(rg_out, 4 * h + i - 1)
                    pe.wait_ge(wr_in[(i + 2) % 3], 16 * (2 * h + (i + 2) // 3 + 1))
                    project(bank, wr[:, (i + 2) % 3]).then_inc(rg_done, 1)

                def scores(c):
                    cols = slice(c * P, (c + 1) * P)
                    bank = s_banks[c % 2]
                    if c >= 2:
                        pe.wait_ge(s_masked, TC * h + c - 1)
                    elif c == 1:
                        pe.wait_ge(rg_out, 4 * h + 4)
                    if c == 0:
                        pe.wait_ge(x_ready, (LEVELS + 2) * (h + 1))
                    for n in range(LEVELS):
                        nc.tensor.matmul(bank[:, n * P:(n + 1) * P], X[:, n, cols], X[:, n, cols], start=True, stop=True)
                    nc.tensor.matmul(bank[:, LEVELS * P:], k[:, cols], q[:, cols], start=True, stop=True).then_inc(s_done, 1)

                def turn(c):
                    pe.wait_ge(on_out, TC * h + c + 1)
                    pe.wait_ge(ot_out, TC * h + c)
                    for i in range(2):
                        last = nc.tensor.transpose(ps_t[:, i * P:(i + 1) * P], on[:, c % 2, i * P:(i + 1) * P], ident[:])
                    last.then_inc(ot_done, 1)

                scores(0)
                for i, bank in enumerate((ps_t, ps_o)):
                    for c in range(4):
                        last = nc.tensor.transpose(bank[:, c * P:(c + 1) * P], kd[:, (4 * i + c) * P:(4 * i + c + 1) * P], ident[:])
                    last.then_inc(kt_done, 1)
                for c in range(TC):
                    if c + 1 < TC:
                        scores(c + 1)
                    n = TC * h + c
                    bank = o_banks[c % 2]
                    pe.wait_ge(s_ready, n + 1)
                    if c >= 2:
                        pe.wait_ge(on_out, n - 1)
                    if c >= 1:
                        pe.wait_ge(rg_out, 4 * h + 4)
                    last = nc.tensor.matmul(bank, S[:, c % 2], V[:, c], start=True, stop=(c == 0))
                    if c == 0:
                        last.then_inc(o_done, 1)
                    else:
                        pe.wait_ge(state_out, n)
                        nc.tensor.matmul(bank, qe[:, c * P:(c + 1) * P], state[:], start=False, stop=True).then_inc(o_done, 1)
                    pe.wait_ge(kt_out, 2 * h + 2)
                    pe.wait_ge(state_out, n)
                    nc.tensor.matmul(ps_o[:, 0:DV], kdT[:, c], V[:, c], start=True, stop=True).then_inc(up_done, 1)
                    if c >= 1:
                        turn(c - 1)
                turn(TC - 1)

        @block.vector
        def _(dve):
            v = nc.vector
            step = Chain(dve, dve_step)
            dve.wait_ge(small_in, 32)
            dve.wait_ge(const, 3)
            with dve.Fori(0, HEADS) as h:
                step.loop(h, 6)
                v.tensor_copy(hp[:], hpar[:, bass.ds(h * 3, 3)]).then_inc(hp_ready, 1)
                dve.wait_ge(hp_ready, h + 1)
                dve.wait_ge(z_done, h + 1)
                dve.wait_ge(z_abs, 2 * h + 1)
                v.tensor_scalar(cum[:], ps_a[:], hp[:, 0:1], 0.0, ALU.add, ALU.min).then_inc(z_min, 1)
                dve.wait_ge(z_min, h + 1)
                dve.wait_ge(l_out, h + 1)
                step(v.tensor_tensor(zl[:], cum[:], zl[:], ALU.subtract))
                step(v.tensor_tensor_scan(cum[:], restart[:], zl[:], 0.0, ALU.mult, ALU.add))
                dve.wait_ge(o_done, TC * h)
                for n in range(LEVELS):
                    half = P >> (n + 1)
                    c4 = cum[:].rearrange("p (b w t) -> p b w t", w=2, t=half)
                    nb = T // (2 * half)
                    middle = c4[:, :, 0:1, half - 1:half].broadcast_to([P, nb, 2, half])
                    v.tensor_tensor(X[:, n].rearrange("p (b w t) -> p b w t", w=2, t=half), c4, middle, ALU.subtract).then_inc(diff_ready, 1)
                c3 = cum[:].rearrange("p (c t) -> p c t", t=P)
                v.tensor_tensor(kd[:].rearrange("p (c t) -> p c t", t=P), c3, c3[:, :, P - 1:P].broadcast_to([P, TC, P]), ALU.subtract).then_inc(diff_ready, 1)
                dve.wait_ge(q_out, h + 1)
                dve.wait_ge(k_out, h + 1)
                for n in range(LEVELS):
                    half = P >> (n + 1)
                    w4 = lambda t: t.rearrange("p (b w t) -> p b w t", w=2, t=half)
                    dve.wait_ge(exp_out, (LEVELS + 3) * h + n + 1)
                    v.tensor_tensor(w4(X[:, n])[:, :, 0], w4(X[:, n])[:, :, 0], w4(k[:])[:, :, 0], ALU.mult)
                    v.tensor_tensor(w4(X[:, n])[:, :, 1], w4(X[:, n])[:, :, 1], w4(q[:])[:, :, 1], ALU.mult).then_inc(x_ready, 1)
                dve.wait_ge(exp_out, (LEVELS + 3) * h + LEVELS + 3)
                v.tensor_tensor(kd[:], kd[:], k[:], ALU.mult).then_inc(x_ready, 1)
                v.tensor_tensor(qe[:], qe[:], q[:], ALU.mult).then_inc(x_ready, 1)
                for i in range(4):
                    dve.wait_ge(rg_out, 4 * h + i + 1)
                    dve.wait_ge(r_raw, 2 * h + min(i + 1, 2))
                    v.scalar_tensor_tensor(gate[:, i % 2], tnh[:], 1.0, gate[:, i % 2], ALU.add, ALU.mult).then_inc(gate_step, 1)
                    dve.wait_ge(gate_step, 4 * h + i + 1)

                def mask(c):
                    n = TC * h + c
                    dve.wait_ge(s_done, n + 1)
                    dve.wait_ge(s_ready, n)
                    v.tensor_tensor(sm[:], s_banks[c % 2][:], masks[:], ALU.mult).then_inc(s_masked, 1)
                    dve.wait_ge(s_masked, n + 1)
                    if c >= 2:
                        dve.wait_ge(o_done, n - 1)
                    v.tensor_reduce(S[:, c % 2], sm[:].rearrange("p (l t) -> p t l", l=NL), AX.X, ALU.add).then_inc(s_ready, 1)

                mask(0)
                for c in range(TC):
                    n = TC * h + c
                    if c + 1 < TC:
                        mask(c + 1)
                    dve.wait_ge(up_done, n + 1)
                    up = ps_o[:, 0:DV]
                    dve.wait_ge(o_done, n + 1)
                    if c == 0:
                        v.tensor_copy(state[:], up).then_inc(state_out, 1)
                    else:
                        dve.wait_ge(state_out, n)
                        v.scalar_tensor_tensor(state[:], state[:], elast[:, c:c + 1], up, ALU.mult, ALU.add).then_inc(state_out, 1)
                    dve.wait_ge(o_root, n + 1)
                    v.reciprocal(rstd[:, c:c + 1], ss[:, c:c + 1]).then_inc(o_rstd, 1)
                dve.wait_ge(ot_out, TC * (h + 1))
                for i in range(2):
                    step(v.scalar_tensor_tensor(gate[:, i], oT[:, i], hp[:, 1 + i:2 + i], gate[:, i], ALU.mult, ALU.mult))
                    dst = merged[:, bass.ds((2 * h + i) * T, T)]
                    step(v.scalar_tensor_tensor(dst, gate[:, i], 0.25, dst, ALU.mult, ALU.add))
                dve.sem_inc(head_out, 1)
            step.end(HEADS)


def peer_block(nc, ctx, keep, a, merged_dram, out):
    mod, ident = keep["mod"], keep["ident"]
    R = 8
    GROUPS = TOPK // R
    VR = ND = 4
    with ExitStack() as scope:
        def sb(name, shape, dt=F32):
            return scope.enter_context(nc.sbuf_tensor(name, shape, dt))

        def sem(name):
            return ctx.enter_context(nc.semaphore(name))

        def psum(name, cols):
            return scope.enter_context(nc.psum_tensor(name, [P, cols], F32))

        ps_acc, ps_y, ps_h, ps_sc = psum("ps_acc", D), psum("ps_y", D), psum("ps_h", D), psum("ps_sc", HALF)

        Wk = sb("Wk", [P, KC, 2 * PH * NK])
        w_out = sb("w_out", [P, KC, D])
        mT = sb("mT", [P, KC, P])
        x2n, x2c = sb("x2n", [P, D]), sb("x2c", [P, D])
        h2n, h2c = sb("h2n", [P, D]), sb("h2c", [P, D])
        h2T = sb("h2T", [P, KC, P])
        yf = sb("yf", [P, D])
        ur, vr = sb("ur", [P, R, D]), sb("vr", [P, VR, D])
        diag = sb("diag", [P, ND, P])
        zero = sb("zero", [P, P], mybir.dt.bfloat16)
        idx = sb("idx", [P, 2 * SLOTS], U32)
        gates = sb("gates", [P, 2 * SLOTS])
        uidx, vidx = sb("uidx", [P, 2, R], U32), sb("vidx", [P, 2, R], U32)
        sc2 = sb("sc2", [P, 2, NK])
        top = sb("top", [P, 2, TOPK])
        topi = sb("topi", [P, 2, TOPK], U32)
        topf = sb("topf", [P, 2, TOPK])
        best = sb("best", [P, TOPK])
        pos = sb("pos", [P, TOPK], U32)
        ab = sb("ab", [P, 2, TOPK], U32)
        abf = sb("abf", [P, 2, TOPK])
        iota = sb("iota", [P, TOPK])
        eq = sb("eq", [P, 2, TOPK, TOPK])
        pick = sb("pick", [P, 2, TOPK])
        negm = sb("negm", [P, 1])
        esum = sb("esum", [P, 1])
        ex = sb("ex", [P, TOPK])
        dots = sb("dots", [P, R])
        gel = sb("gel", [P, R])
        coef = sb("coef", [P, GROUPS, R])
        eps = sb("eps3", [P, 1])
        ss = sb("ss3", [P, 3])
        rstd = sb("rstd3", [P, 3])

        const, small_in = sem("consts3"), sem("small_in3")
        wout_in = sem("wout_in")
        wq_in = [sem("wq_in0"), sem("wq_in1")]
        wk_done, wk_out = sem("wk_done"), sem("wk_out")
        mod_ready = sem("mod_ready")
        x_in, m_in = sem("x_in3"), sem("m_in")
        y_done, y_sq, y_root, y_rstd, y_used = sem("y_done"), sem("y_sq"), sem("y_root"), sem("y_rstd"), sem("y_used")
        x2_ready, h2_ready, h2_turned, h2T_out, h2_copied = sem("x2_ready"), sem("h2_ready"), sem("h2_turned"), sem("h2T_out"), sem("h2_copied")
        sc_done, sc_used = sem("sc_done"), sem("sc_used")
        negm_ready, ex_out, sel_ready = sem("negm_ready"), sem("ex_out"), sem("sel_ready")
        ucopy, vcopy, pool_go = sem("ucopy"), sem("vcopy"), sem("pool_go3")
        u_in = [sem(f"u_in{r}") for r in range(R)]
        v_in = [sem(f"v_in{r}") for r in range(VR)]
        u_used, v_used = sem("u_used"), sem("v_used")
        gel_ready, tanh_out, coef_ready, diag_out = sem("gel_ready"), sem("tanh_out"), sem("coef_ready"), sem("diag_out")
        acc_done, acc_out, f_root, f_rstd, f_ready, out_done = (sem(n) for n in ("acc_done", "acc_out", "f_root", "f_rstd", "f_ready", "out_done"))
        dve_step, dve_go = sem("dve_step3"), sem("dve_go3")

        block = scope.enter_context(nc.Block())
        half = lambda s: slice(s * HALF, (s + 1) * HALF)

        def group_at(G):
            return bass.ds(G % (2 * SLOTS // R) * R, R)

        @block.sync
        def _(sp):
            for i, n in enumerate(("gain_post_mix", "gain_pre_ffn", "gain_post_ffn")):
                sp.dma_start(ur[:, 2 + i], a[n].broadcast_to([P, D])).then_inc(small_in, 16)

            def load_keys(g, s):
                sp.dma_start(vr[:, s], a["wqT"][g].rearrange("o p d -> (o p) d")).then_inc(wq_in[s], 16)
                sp.dma_start(vr[:, 2 + s, 0:NK], a["keysT"][g].rearrange("o p d -> (o p) d")).then_inc(wq_in[s], 16)

            def merged_tile(t):
                sp.dma_start(mT[:], merged_dram[:, :, bass.ds(t * P, P)]).then_inc(m_in, 16)

            def x_tile(t):
                sp.dma_start(x2n[:], a["x"][bass.ds(t, 1)].rearrange("o p d -> (o p) d")).then_inc(x_in, 16)

            def store_tile(t):
                sp.wait_ge(f_ready, t + 1)
                sp.dma_start(out[bass.ds(t, 1)].rearrange("o p d -> (o p) d"), yf[:]).then_inc(out_done, 16)

            merged_tile(0)
            sp.dma_start(w_out[:], a["w_out"]).then_inc(wout_in, 16)
            x_tile(0)
            for s in range(2):
                load_keys(slice(s, s + 1), s)
            with sp.Fori(0, PH - 1) as g:
                for s in range(2):
                    sp.wait_ge(wk_done, 2 * g + s + 1)
                    load_keys(bass.ds(2 * g + s + 2, 1), s)
            sp.wait_ge(y_done, 2)
            merged_tile(1)
            with sp.Fori(1, TC - 1) as t:
                sp.wait_ge(h2_copied, t)
                x_tile(t)
                sp.wait_ge(y_done, 2 * t + 2)
                merged_tile(t + 1)
                store_tile(t - 1)
            sp.wait_ge(h2_copied, TC - 1)
            x_tile(TC - 1)
            store_tile(TC - 2)
            store_tile(TC - 1)
            sp.wait_ge(out_done, 16 * TC)

        @block.gpsimd
        def _(pool):
            nc.gpsimd.memset(eps[:], EPS).then_inc(const, 1)
            nc.gpsimd.memset(zero[:], 0.0).then_inc(const, 1)
            nc.gpsimd.iota(iota[:], [[1, TOPK]], base=0, channel_multiplier=0, allow_small_or_imprecise_dtypes=True).then_inc(const, 1)

            def copy_indices(G, par, to, copied):
                pool.sem_inc(pool_go, 1)
                nc.gpsimd.tensor_copy(to[:, par], idx[:, group_at(G)]).then_inc(copied, 1)
                pool.wait_ge(copied, G + 1)

            def gather_u(G, par, r, first=False):
                if not first:
                    pool.wait_ge(u_used, R * (G - 1) + r + 1)
                pool.sem_inc(pool_go, 1)
                pool.indirect_dma_start(ur[:, r], None, a["u"], bass.IndirectOffsetOnAxis(ap=uidx[:, par, r:r + 1], axis=0)).then_inc(u_in[r], 16)

            def gather_v(G, par, r):
                pool.wait_ge(v_used, R * G + r + 1)
                pool.sem_inc(pool_go, 1)
                pool.indirect_dma_start(vr[:, r % VR], None, a["v"], bass.IndirectOffsetOnAxis(ap=vidx[:, par, r:r + 1], axis=0)).then_inc(v_in[r % VR], 16)

            def both(G, par):
                copy_indices(G + 1, 1 - par, uidx, ucopy)
                copy_indices(G, par, vidx, vcopy)
                for r in range(R):
                    gather_u(G + 1, 1 - par, r)
                    gather_v(G, par, r)

            pool.wait_ge(mod_ready, 1)
            pool.wait_ge(wk_done, 2 * PH)
            pool.wait_ge(sel_ready, 1)
            copy_indices(0, 0, uidx, ucopy)
            for r in range(R):
                gather_u(0, 0, r, first=True)
            with pool.Fori(0, TC * PH - 1) as H:
                both(2 * H, 0)
                pool.wait_ge(sel_ready, H + 2)
                both(2 * H + 1, 1)
            last = 2 * TC * PH - 1
            both(last - 1, 0)
            copy_indices(last, 1, vidx, vcopy)
            for r in range(R):
                gather_v(last, 1, r)

        @block.scalar
        def _(act):
            S = nc.scalar
            act.wait_ge(const, 3)
            act.sem_inc(diag_out, R)

            def tile_norms(t, stored):
                act.wait_ge(y_done, 2 * t + 2)
                if stored is not None:
                    act.wait_ge(out_done, 16 * stored)
                junk = yf[:]
                S.activation(junk, ps_y[:], ACT.Square, scale=D ** -0.5, accum_out=ss[:, 0:1]).then_inc(y_sq, 1)
                act.wait_ge(y_sq, 2 * t + 1)
                S.activation(ss[:, 0:1], ss[:, 0:1], ACT.Sqrt, bias=eps[:]).then_inc(y_root, 1)
                act.wait_ge(x2_ready, t + 1)
                S.activation(junk, x2n[:], ACT.Square, scale=D ** -0.5, accum_out=ss[:, 1:2]).then_inc(y_sq, 1)
                act.wait_ge(y_sq, 2 * t + 2)
                S.activation(ss[:, 1:2], ss[:, 1:2], ACT.Sqrt, bias=eps[:]).then_inc(y_root, 1)

            def tile_turned(t):
                act.wait_ge(h2_turned, t + 1)
                S.activation(h2T[:].rearrange("p k t -> p (k t)"), ps_h[:], ACT.Copy).then_inc(h2T_out, 1)

            def select_gates(n):
                act.wait_ge(negm_ready, n + 1)
                S.activation(ex[:], best[:], ACT.Exp, bias=negm[:], accum_out=esum[:]).then_inc(ex_out, 1)

            def experts(G, par):
                act.wait_ge(gel_ready, G + 1)
                S.activation(gel[:], gel[:], ACT.Tanh, scale=GELU_B).then_inc(tanh_out, 1)
                act.wait_ge(coef_ready, G + 1)
                for r in range(R):
                    act.wait_ge(v_used, R * G + r + 1)
                    S.activation(diag[:, r % ND], ident[:], ACT.Copy, scale=coef[:, par, r:r + 1]).then_inc(diag_out, 1)

            def finish(t):
                act.wait_ge(acc_done, t + 1)
                act.wait_ge(out_done, 16 * t)
                S.activation(yf[:], ps_acc[:], ACT.Square, scale=D ** -0.5, accum_out=ss[:, 2:3]).then_inc(f_root, 1)
                act.wait_ge(f_root, 2 * t + 1)
                S.activation(yf[:], ps_acc[:], ACT.Copy).then_inc(acc_out, 1)
                S.activation(ss[:, 2:3], ss[:, 2:3], ACT.Sqrt, bias=eps[:]).then_inc(f_root, 1)

            def take_tile(t):
                act.wait_ge(h2_ready, t + 1)
                act.wait_ge(f_ready, t)
                S.activation(x2c[:], x2n[:], ACT.Copy)
                act.wait_ge(u_used, SLOTS * t)
                S.activation(h2c[:], h2n[:], ACT.Copy).then_inc(h2_copied, 1)

            def head(H, select=True):
                for s in range(GROUPS):
                    experts(GROUPS * H + s, s)
                if select:
                    select_gates(H + 2)

            tile_norms(0, None)
            with act.Fori(0, 2 * PH) as g:
                act.wait_ge(wk_done, g + 1)
                S.activation(Wk[:, :, bass.ds(g * NK, NK)], ps_h[:].rearrange("p (k n) -> p k n", k=KC), ACT.Copy).then_inc(wk_out, 1)
            tile_turned(0)
            take_tile(0)
            for n in range(2):
                select_gates(n)
            with act.Fori(0, TC - 1) as t:
                with act.Fori(0, 2) as h:
                    head(PH * t + h)
                tile_norms(t + 1, t)
                with act.Fori(2, PH - 2) as h:
                    head(PH * t + h)
                tile_turned(t + 1)
                with act.Fori(PH - 2, PH) as h:
                    head(PH * t + h)
                finish(t)
                take_tile(t + 1)
            with act.Fori(PH * (TC - 1), PH * TC - 2) as H:
                head(H)
            for H in range(PH * TC - 2, PH * TC):
                head(H, select=False)
            finish(TC - 1)

        @block.tensor
        def _(pe):
            pe.sem_inc(v_used, VR)
            def tile_half(t, s):
                pe.wait_ge(m_in, 16 * (t + 1))
                pe.wait_ge(y_used, t)
                for k in range(KC):
                    last = nc.tensor.matmul(ps_y[:, bass.ds(s * HALF, HALF)], mT[:, k], w_out[:, k, bass.ds(s * HALF, HALF)], start=(k == 0), stop=(k == KC - 1))
                last.then_inc(y_done, 1)

            def tile_turn(t):
                pe.wait_ge(h2_ready, t + 1)
                pe.wait_ge(h2T_out, t)
                for k in range(KC):
                    last = nc.tensor.transpose(ps_h[:, k * P:(k + 1) * P], h2n[:, k * P:(k + 1) * P], ident[:])
                last.then_inc(h2_turned, 1)

            def scores(n, t, h):
                pe.wait_ge(h2T_out, t + 1)
                pe.wait_ge(sc_used, n)
                for k in range(KC):
                    last = nc.tensor.matmul(ps_sc[:, 0:2 * NK], h2T[:, k], Wk[:, k, bass.ds(h * 2 * NK, 2 * NK)], start=(k == 0), stop=(k == KC - 1))
                last.then_inc(sc_done, 1)

            def edge(start):
                for s in range(2):
                    last = nc.tensor.matmul(ps_acc[:, half(s)], zero[:], zero[:, 0:1].broadcast_to([P, HALF]), start=start, stop=not start, skip_group_check=True)
                return last

            def experts(G):
                for r in range(R):
                    pe.wait_ge(diag_out, R * (G + 1) + r + 1)
                    pe.wait_ge(v_in[r % VR], 16 * (R // VR * G + r // VR + 1))
                    for s in range(2):
                        last = nc.tensor.matmul(ps_acc[:, half(s)], diag[:, r % ND], vr[:, r % VR, half(s)], start=False, stop=False, skip_group_check=True)
                    last.then_inc(v_used, 1)

            def head(H):
                for s in range(GROUPS):
                    experts(GROUPS * H + s)

            pe.wait_ge(const, 3)
            pe.wait_ge(wout_in, 16)
            for s in range(2):
                tile_half(0, s)
            with pe.Fori(0, PH) as g:
                for s in range(2):
                    pe.wait_ge(wq_in[s], 32 * (g + 1))
                    pe.wait_ge(wk_out, 2 * g + s)
                    for k in range(KC):
                        last = nc.tensor.matmul(ps_h[:, k * P:(k + 1) * P], vr[:, s, k * P:(k + 1) * P], vr[:, 2 + s, 0:NK], start=True, stop=True)
                    last.then_inc(wk_done, 1)
            pe.wait_ge(wk_out, 2 * PH)
            tile_turn(0)
            for h in range(2):
                scores(h, 0, h)
            with pe.Fori(0, TC - 1) as t:
                pe.wait_ge(acc_out, t)
                edge(True)
                with pe.Fori(0, 2) as h:
                    scores(PH * t + h + 2, t, h + 2)
                    tile_half(t + 1, h)
                    head(PH * t + h)
                with pe.Fori(2, PH - 2) as h:
                    scores(PH * t + h + 2, t, h + 2)
                    head(PH * t + h)
                tile_turn(t + 1)
                with pe.Fori(PH - 2, PH) as h:
                    scores(PH * t + h + 2, t + 1, h - (PH - 2))
                    head(PH * t + h)
                edge(False).then_inc(acc_done, 1)
            pe.wait_ge(acc_out, TC - 1)
            edge(True)
            with pe.Fori(0, PH - 2) as h:
                scores(PH * (TC - 1) + h + 2, TC - 1, h + 2)
                head(PH * (TC - 1) + h)
            for H in range(PH * TC - 2, PH * TC):
                head(H)
            edge(False).then_inc(acc_done, 1)

        @block.vector
        def _(dve):
            v = nc.vector
            step = Chain(dve, dve_step)
            g1, shift2, scale2, g2 = (mod[:, i * D:(i + 1) * D] for i in range(4))
            dve.wait_ge(small_in, 48)
            dve.wait_ge(const, 3)
            step(v.tensor_tensor(g1, g1, ur[:, 2], ALU.mult))
            step(v.scalar_tensor_tensor(scale2, scale2, 1.0, ur[:, 3], ALU.add, ALU.mult))
            v.tensor_tensor(g2, g2, ur[:, 4], ALU.mult).then_inc(mod_ready, 1)
            dve.wait_ge(mod_ready, 1)

            def tile_norms(t):
                dve.wait_ge(y_root, 2 * t + 1)
                v.reciprocal(rstd[:, 0:1], ss[:, 0:1]).then_inc(y_rstd, 1)
                dve.wait_ge(y_rstd, 2 * t + 1)
                dve.wait_ge(h2_copied, t)
                v.scalar_tensor_tensor(h2n[:], ps_y[:], rstd[:, 0:1], g1, ALU.mult, ALU.mult).then_inc(y_used, 1)
                dve.wait_ge(y_used, t + 1)
                dve.wait_ge(x_in, 16 * (t + 1))
                v.tensor_tensor(x2n[:], x2n[:], h2n[:], ALU.add).then_inc(x2_ready, 1)
                dve.wait_ge(x2_ready, t + 1)
                dve.wait_ge(y_root, 2 * t + 2)
                v.reciprocal(rstd[:, 1:2], ss[:, 1:2]).then_inc(y_rstd, 1)
                dve.wait_ge(y_rstd, 2 * t + 2)
                step(v.scalar_tensor_tensor(h2n[:], x2n[:], rstd[:, 1:2], scale2, ALU.mult, ALU.mult))
                v.tensor_tensor(h2n[:], h2n[:], shift2, ALU.add).then_inc(h2_ready, 1)

            SELECT_STEPS = 8 + 1 + 4 + 10

            def alone():
                dve.sem_inc(dve_go, 1)

            def top16(values, spare, out, index):
                for n in range(2):
                    o, i = out[:, 8 * n:8 * n + 8], index[:, 8 * n:8 * n + 8]
                    alone()
                    step(v.max(o, values))
                    alone()
                    if n == 0:
                        v.max_index(i, o, values)
                        step(v.match_replace(spare, o, values, NEG))
                        values = spare
                    else:
                        step(v.max_index(i, o, values))

            def select_sides(n):
                dve.wait_ge(sc_done, n + 1)
                for p in range(2):
                    top16(ps_sc[:, p * NK:(p + 1) * NK], sc2[:, p], top[:, p], topi[:, p])
                dve.sem_inc(sc_used, 1)

            def select_pairs(n):
                cand = eq[:, 0]
                step(v.tensor_tensor(cand, top[:, 0].unsqueeze(2).broadcast_to([P, TOPK, TOPK]), top[:, 1].unsqueeze(1).broadcast_to([P, TOPK, TOPK]), ALU.add))
                dve.wait_ge(ex_out, n)
                top16(cand.rearrange("p a b -> p (a b)"), eq[:, 1].rearrange("p a b -> p (a b)"), best, pos)
                v.tensor_scalar(negm[:], best[:, 0:1], -1.0, None, ALU.mult).then_inc(negm_ready, 1)
                step(v.tensor_scalar(ab[:, 0], pos[:], 4, None, ALU.logical_shift_right))
                step(v.tensor_scalar(ab[:, 1], pos[:], TOPK - 1, None, ALU.bitwise_and))
                step(v.tensor_copy(abf[:], ab[:]))
                step(v.tensor_copy(topf[:], topi[:]))
                for p in range(2):
                    last = v.tensor_tensor(eq[:, p], abf[:, p].unsqueeze(2).broadcast_to([P, TOPK, TOPK]), iota[:].unsqueeze(1).broadcast_to([P, TOPK, TOPK]), ALU.is_equal)
                step(last)
                for p in range(2):
                    last = v.tensor_tensor(eq[:, p], eq[:, p], topf[:, p].unsqueeze(1).broadcast_to([P, TOPK, TOPK]), ALU.mult)
                step(last)
                step(v.tensor_reduce(pick[:], eq[:], AX.X, ALU.add))
                step(v.scalar_tensor_tensor(idx[:, bass.ds(n % (2 * PH) * TOPK, TOPK)], pick[:, 0], float(NK), pick[:, 1], ALU.mult, ALU.add))
                dve.wait_ge(ex_out, n + 1)
                step(v.reciprocal(esum[:], esum[:]))
                step(v.tensor_scalar(gates[:, bass.ds(n % (2 * PH) * TOPK, TOPK)], ex[:], esum[:], 0.5, ALU.mult, ALU.mult))
                dve.sem_inc(sel_ready, 1)

            def experts(G, par):
                for r in range(R):
                    dve.wait_ge(u_in[r], 16 * (G + 1))
                    last = v.scalar_tensor_tensor(ur[:, r], ur[:, r], 1.0, h2c[:], ALU.mult, ALU.mult, accum_out=dots[:, r:r + 1])
                    last.then_inc(u_used, 1)
                dve.wait_ge(u_used, R * (G + 1))
                step(v.scalar_tensor_tensor(gel[:], dots[:], GELU_A, dots[:], ALU.mult, ALU.mult))
                v.scalar_tensor_tensor(gel[:], gel[:], 1.0, dots[:], ALU.add, ALU.mult).then_inc(gel_ready, 1)
                dve.wait_ge(tanh_out, G + 1)
                step(v.scalar_tensor_tensor(gel[:], gel[:], 1.0, dots[:], ALU.add, ALU.mult))
                dve.wait_ge(diag_out, R * G)
                v.tensor_tensor(coef[:, par], gel[:], gates[:, group_at(G)], ALU.mult).then_inc(coef_ready, 1)

            def finish(t):
                dve.wait_ge(f_root, 2 * t + 2)
                v.reciprocal(rstd[:, 2:3], ss[:, 2:3]).then_inc(f_rstd, 1)
                dve.wait_ge(f_rstd, t + 1)
                dve.wait_ge(acc_out, t + 1)
                step(v.scalar_tensor_tensor(yf[:], yf[:], rstd[:, 2:3], g2, ALU.mult, ALU.mult))
                v.tensor_tensor(yf[:], yf[:], x2c[:], ALU.add).then_inc(f_ready, 1)

            HEAD_STEPS = 2 * GROUPS + SELECT_STEPS

            def head(H):
                experts(GROUPS * H, 0)
                select_sides(H + 2)
                experts(GROUPS * H + 1, 1)
                select_pairs(H + 2)

            tile_norms(0)
            for n in range(2):
                select_sides(n)
                select_pairs(n)
            dve.wait_ge(h2_copied, 1)
            alone()
            with dve.Fori(0, TC - 1) as t:
                step.loop(t, PH * HEAD_STEPS + 2)
                for first, last in ((0, 2), (2, PH - 2), (PH - 2, PH)):
                    with dve.Fori(first, last) as h:
                        step.loop(h - first, HEAD_STEPS)
                        head(PH * t + h)
                    step.end(last - first)
                    if first == 0:
                        tile_norms(t + 1)
                finish(t)
                dve.wait_ge(h2_copied, t + 2)
                alone()
            step.end(TC - 1)
            with dve.Fori(0, PH - 2) as h:
                step.loop(h, HEAD_STEPS)
                head(PH * (TC - 1) + h)
            step.end(PH - 2)
            for H in range(PH * TC - 2, PH * TC):
                for s in range(GROUPS):
                    experts(GROUPS * H + s, s)
            finish(TC - 1)


def build(nc, a, out):
    with ExitStack() as ctx:
        merged_dram = nc.dram_tensor("merged_scratch", (P, KC, T), F32, kind="Internal").ap()
        keep = {"mod": ctx.enter_context(nc.sbuf_tensor("mod", [P, 4 * D], F32)),
                "ident": ctx.enter_context(nc.sbuf_tensor("ident", [P, P], F32))}
        with nc.sbuf_tensor("hT", [P, KC, T], F32) as hT, nc.sbuf_tensor("merged", [P, KC * T], F32) as merged:
            keep["hT"], keep["merged"] = hT, merged
            conditioning_and_lru(nc, ctx, keep, a)
            gated_linear_attention(nc, ctx, keep, a, merged_dram)
        peer_block(nc, ctx, keep, a, merged_dram, out)


def layout(inputs):
    import numpy as np
    g = {k: np.asarray(v) for k, v in inputs.items()}
    ch = lambda w: w.reshape(KC, P, -1).transpose(1, 0, 2)
    col = lambda w: np.ascontiguousarray(w.reshape(KC, P).T)
    a = {}
    a["x"] = g["x"].reshape(TC, P, D)
    a["cT"] = col(g["c"][0])
    a["gain1"] = col(g["norm_pre_mix"][0])
    a["w_ada"] = ch(g["w_ada"][0]).reshape(P, KC, 2 * MODS, HALF).transpose(2, 0, 1, 3)
    a["b_ada"] = g["b_ada"][0].reshape(2 * MODS, HALF)
    a["ident"] = np.eye(P, dtype=np.float32)
    w = ch(g["w_in"][0])
    off = np.cumsum([0, 512, 512, 1024, 1024, RANK, D, D, D, D])
    q, k, v, r, al, xl, xg, ga, gb = (w[:, :, off[i]:off[i + 1]] for i in range(9))
    blocks = lambda m: m.reshape(P, KC, -1, P).transpose(2, 0, 1, 3)
    a["w_lru"] = np.stack([blocks(xl), blocks(xg), blocks(gb)], 1)
    par = np.stack([g["conv_w"][0][i] for i in range(4)] + [g["conv_b"][0], g["lru_b_a"][0].reshape(-1), g["lru_b_x"][0].reshape(-1), g["lru_lambda"][0]], -1)
    a["lru_par"] = par.reshape(KC, P, NPAR).transpose(1, 0, 2).reshape(P, KC * NPAR)
    a["lru_w"] = np.stack([g["lru_w_a"][0], g["lru_w_x"][0]], 2)
    a["w_v"] = v.reshape(P, KC, HEADS, DV).transpose(2, 0, 1, 3)
    pair = lambda m: blocks(m).reshape(HEADS, 2, P, KC, P)
    a["w_head"] = np.concatenate([blocks(q)[:, None], blocks(k)[:, None], pair(r), pair(ga)], 1)
    a["w_al"] = al
    a["w_alpha"] = g["w_alpha"][0].reshape(RANK, HEADS, DK).transpose(1, 0, 2)
    a["head_par"] = np.concatenate([g["b_alpha"][0].reshape(HEADS, DK).T.reshape(P, HEADS, 1), g["gla_norm"][0].reshape(HEADS, 2, P).transpose(2, 0, 1)], 2).reshape(P, HEADS * 3)
    s, t = np.arange(P)[:, None], np.arange(P)[None, :]
    halvings = [((s // b == t // b) & (s % b < b // 2) & (t % b >= b // 2)) for b in (P >> n for n in range(LEVELS))] + [s == t]
    a["masks"] = np.concatenate(halvings, 1).astype(np.float32)
    a["w_out"] = ch(g["w_out"][0])
    a["gain_post_mix"] = g["norm_post_mix"]
    a["gain_pre_ffn"] = g["norm_pre_ffn"]
    a["gain_post_ffn"] = g["norm_post_ffn"]
    a["wqT"] = g["peer_w_query"][0].reshape(D, PH * 2, P).transpose(1, 2, 0)
    a["keysT"] = g["peer_sub_keys"][0].reshape(PH * 2, NK, P).transpose(0, 2, 1)
    a["u"] = g["peer_u"][0]
    a["v"] = g["peer_v"][0]
    return {k: np.ascontiguousarray(v) for k, v in a.items()}


def kernel(**inputs):
    import numpy as np
    import concourse.bacc as bacc
    from concourse.bass_utils import run_bass_kernel_spmd

    arrays = {f"in_{k}": v for k, v in layout(inputs).items()}
    nc = bacc.Bacc("TRN2", target_bir_lowering=False, num_devices=1)
    a = {k[3:]: nc.dram_tensor(k, v.shape, mybir.dt.from_np(v.dtype), kind="ExternalInput").ap() for k, v in arrays.items()}
    out = nc.dram_tensor("out_y", (TC, P, D), F32, kind="ExternalOutput").ap()
    build(nc, a, out)
    r = run_bass_kernel_spmd(nc, [arrays], core_ids=[0])
    return np.asarray(r.results[0]["out_y"]).reshape(1, T, D)
```

```python
from contextlib import ExitStack

import concourse.bass as bass
from concourse import mybir

F32 = mybir.dt.float32
F32R = mybir.dt.float32r
U32 = mybir.dt.uint32
ALU = mybir.AluOpType
ACT = mybir.ActivationFunctionType
AX = mybir.AxisListType

P = 128
D = 1024
T = 1024
KC = D // P
TC = T // P
HALF = 512
EPS = 1e-6
HEADS, DK, DV, RANK = 4, 128, 256, 16
TAU = 16.0
LEVELS = 7
NPAR = 8
SCAN_C = 8.0
GELU_A, GELU_B = 0.044715, 0.7978845608028654
MODS = 6
PH, NK, TOPK = 8, 128, 16
SLOTS = PH * TOPK
NEG = -3.0e38


class Chain:

    def __init__(self, eng, sem, base=0):
        self.eng, self.sem, self.base, self.n, self.outer = eng, sem, base, 0, []

    def __call__(self, ins):
        self.n += 1
        ins.then_inc(self.sem, 1)
        self.eng.wait_ge(self.sem, self.base + self.n)

    def loop(self, i, per):
        self.outer.append((self.base, self.n, per))
        self.base, self.n = self.base + self.n + i * per, 0

    def end(self, count):
        base, n, per = self.outer.pop()
        assert self.n == per, (self.n, per)
        self.base, self.n = base, n + count * per


def split_product(nc, out, wh, wl, xh, xl, first, last):
    nc.tensor.matmul(out, wh, xh, start=first, stop=False)
    nc.tensor.matmul(out, wh, xl, start=False, stop=False)
    return nc.tensor.matmul(out, wl, xh, start=False, stop=last)


def conditioning_and_lru(nc, ctx, keep, a, mod_dram, merged_dram):
    hh, hl, ident = keep["hh"], keep["hl"], keep["ident"]
    Q = 256
    CQ = Q // P
    MOD1 = 2 * D // Q
    with ExitStack() as scope:
        def sb(name, shape, dt=F32):
            return scope.enter_context(nc.sbuf_tensor(name, shape, dt))

        def sem(name):
            return ctx.enter_context(nc.semaphore(name))

        ps_xl, ps_xg, ps_gb, ps_gate = (scope.enter_context(nc.psum_tensor(n, [P, T], F32)) for n in ("ps_xl", "ps_xg", "ps_gb", "ps_gate"))
        ada_banks = (ps_gate[:, 0:Q], ps_gate[:, HALF:HALF + Q])

        ada = sb("ada", [P, 2, KC, Q])
        ada_bias = sb("ada_bias", [P, 2, Q])
        ada_sum = sb("ada_sum", [P, 2, Q])
        mod = sb("mod_tile", [P, 2, Q])
        ones = sb("ones1", [P, P])
        eps = sb("eps1", [P, 1])
        cT, cact, gain = sb("cT", [P, KC]), sb("cact", [P, KC]), sb("gain1", [P, KC])
        cols = sb("cols1", [P, 2 * KC])
        par, parj = sb("par", [P, KC * NPAR]), sb("parj", [P, NPAR])
        ptmp = sb("ptmp", [P, 5, KC])
        ss, rstd = sb("ss1", [P, 2]), sb("rstd1", [P, 2])
        xt = sb("xt", [P, 2, D])
        wt = sb("wt", [P, 3, KC, P])
        wh, wl = sb("wh1", [P, 3, KC, P], F32R), sb("wl1", [P, 3, KC, P], F32R)
        wgate = sb("wgate", [P, 2, P])
        lru = sb("lru", [P, T])
        arena = sb("arena", [P, 11 * T + 3])
        raw = arena[:, 0:KC * T].rearrange("p (k t) -> p k t", k=KC)
        xn, junk = (arena[:, (KC + i) * T:(KC + i + 1) * T] for i in range(2))
        diag = arena[:, (KC + 2) * T:(KC + 2) * T + Q]
        xlp = arena[:, 0:T + 3]
        xc, xg, pin, tg, tb, tr, ti, av, th, mu = (arena[:, 3 + i * T:3 + (i + 1) * T] for i in range(1, 11))

        small_in, consts = sem("small_in"), sem("consts1")
        ada_in = [sem("ada_in0"), sem("ada_in1")]
        ada_ready = sem("ada_ready")
        ada_done = sem("ada_done")
        mod_out = sem("mod_out")
        mod_used = sem("mod_used")
        mod_stored = [sem("mod_stored0"), sem("mod_stored1")]
        c_tanh, par_abs, par_exp = sem("c_tanh"), sem("par_abs"), sem("par_exp")
        x_in = [sem("x_in0"), sem("x_in1")]
        x_sq, x_root, x_rstd, x_scaled, x_turned = (sem(n) for n in ("x_sq", "x_root", "x_rstd", "x_scaled", "x_turned"))
        raw_out = sem("raw_out")
        cols_ready, h_out, hi_out, lo_out = sem("cols_ready"), sem("h_out"), sem("hi_out"), sem("lo_out")
        w_in = [sem(f"w_in{i}") for i in range(3)]
        w_hi, w_split = sem("w_hi"), sem("w_split")
        wg_in = sem("wg_in")
        projected = [sem("p_xl"), sem("p_xg"), sem("p_gb")]
        p_gr, p_gi = sem("p_gr"), sem("p_gi")
        xl_out, xg_out, tb_out, tr_out, ti_out = (sem(n) for n in ("xl_out", "xg_out", "tb_out", "tr_out", "ti_out"))
        xc_ready, pin_ready, nla_ready, parj_ready = sem("xc_ready"), sem("pin_ready"), sem("nla_ready"), sem("parj_ready")
        tg_out, a_out, th_out = sem("tg_out"), sem("a_out"), sem("th_out")
        mu2_ready, mu_root = sem("mu2_ready"), sem("mu_root")
        lru_out, lru_stored = sem("lru_out"), sem("lru_stored")
        dve_step, pool_go = sem("dve_step1"), keep["pool_go"]

        block = scope.enter_context(nc.Block())

        @block.sync
        def _(sp):
            def load_ada(m, s):
                sp.dma_start(ada[:, s], a["w_ada"][bass.ds(m, 1)].rearrange("o p k c -> p (o k) c")).then_inc(ada_in[s], 16)
                sp.dma_start(ada_bias[:, s], a["b_ada"][bass.ds(m, 1), :].broadcast_to([P, Q])).then_inc(ada_in[s], 16)

            sp.dma_start(cT[:], a["cT"]).then_inc(small_in, 16)
            sp.dma_start(gain[:], a["gain1"]).then_inc(small_in, 16)
            sp.dma_start(par[:], a["lru_par"]).then_inc(small_in, 16)
            sp.dma_start(ident[:], a["ident"]).then_inc(small_in, 16)
            for s in range(2):
                load_ada(s, s)
            with sp.Fori(1, MOD1 // 2) as g:
                for s in range(2):
                    sp.wait_ge(ada_ready, 2 * g + s - 1)
                    sp.wait_ge(mod_out, 2 * g + s - 1)
                    load_ada(2 * g + s, s)
            for i in range(3):
                sp.dma_start(wt[:, i], a["w_lru"][0, i]).then_inc(w_in[i], 16)
            sp.dma_start(wgate[:], a["lru_w"][0]).then_inc(wg_in, 16)
            with sp.Fori(0, KC) as j:
                for s in range(2):
                    sp.wait_ge(ada_ready, MOD1 + 2 * j + s - 1)
                    sp.wait_ge(mod_out, MOD1 + 2 * j + s - 1)
                    load_ada(MOD1 + 2 * j + s, s)
                for i in range(3):
                    sp.wait_ge(w_split, 3 * j + i + 1)
                    sp.dma_start(wt[:, i], a["w_lru"][bass.ds(j + 1, 1), i].rearrange("o p k c -> p (o k) c")).then_inc(w_in[i], 16)
                sp.wait_ge(p_gi, j + 1)
                sp.dma_start(wgate[:], a["lru_w"][bass.ds(j + 1, 1)].rearrange("o p g c -> p (o g) c")).then_inc(wg_in, 16)
            for i in range(3):
                sp.wait_ge(w_in[i], 16 * (KC + 1))
            sp.wait_ge(wg_in, 16 * (KC + 1))

        @block.gpsimd
        def _(pool):
            g = nc.gpsimd
            g.memset(ones[:], 1.0).then_inc(consts, 1)
            g.memset(eps[:], EPS).then_inc(consts, 1)
            for s in range(2):
                pool.dma_start(xt[:, s], a["x"][s]).then_inc(x_in[s], 16)
            with pool.Fori(1, TC // 2) as q:
                for s in range(2):
                    pool.wait_ge(x_scaled, 2 * q + s - 1)
                    pool.sem_inc(pool_go, 1)
                    pool.dma_start(xt[:, s], a["x"][bass.ds(2 * q + s, 1)].rearrange("o p d -> (o p) d")).then_inc(x_in[s], 16)

            def split(i, j):
                pool.wait_ge(w_in[i], 16 * (j + 1))
                pool.wait_ge(projected[i], j)
                pool.sem_inc(pool_go, 1)
                g.tensor_copy(wh[:, i], wt[:, i]).then_inc(w_hi, 1)
                pool.wait_ge(w_hi, 3 * j + i + 1)
                g.tensor_tensor(wl[:, i], wt[:, i], wh[:, i], ALU.subtract).then_inc(w_split, 1)

            for i in range(3):
                split(i, 0)
            with pool.Fori(0, KC) as j:
                for i in range(3):
                    if i == 2:
                        for s in range(2):
                            pool.wait_ge(mod_out, MOD1 + 2 * j + s + 1)
                            pool.sem_inc(pool_go, 1)
                            pool.dma_start(mod_dram[:, bass.ds((2 * j + s) * Q, Q)], mod[:, s]).then_inc(mod_stored[s], 16)
                    split(i, j + 1)
                pool.wait_ge(lru_out, j + 1)
                pool.sem_inc(pool_go, 1)
                pool.dma_start(merged_dram[:, bass.ds(j, 1), :].rearrange("p o t -> p (o t)"), lru[:]).then_inc(lru_stored, 16)
            for s in range(2):
                pool.wait_ge(mod_stored[s], 16 * KC)
            pool.wait_ge(lru_stored, 16 * KC)

        @block.scalar
        def _(act):
            S = nc.scalar
            act.wait_ge(small_in, 64)
            S.activation(cact[:], cT[:], ACT.Tanh, scale=0.5).then_inc(c_tanh, 1)
            act.wait_ge(par_abs, 1)
            S.activation(ptmp[:, 1], ptmp[:, 0], ACT.Exp, scale=-1.0).then_inc(par_exp, 1)
            act.wait_ge(consts, 2)

            def turned(c, s):
                act.wait_ge(x_turned, c + 1)
                S.activation(raw[:, :, bass.ds(c * P, P)], (ps_xl, ps_xg)[s][:].rearrange("p (k t) -> p k t", k=KC), ACT.Copy).then_inc(raw_out, 1)

            with act.Fori(0, TC // 2) as q:
                for s in range(2):
                    c = 2 * q + s
                    act.wait_ge(x_in[s], 16 * (q + 1))
                    act.wait_ge(x_sq, c)
                    act.wait_ge(x_rstd, c)
                    S.activation(junk, xt[:, s], ACT.Square, scale=D ** -0.5, accum_out=ss[:, s:s + 1]).then_inc(x_sq, 1)
                    act.wait_ge(x_sq, c + 1)
                    S.activation(ss[:, s:s + 1], ss[:, s:s + 1], ACT.Sqrt, bias=eps[:]).then_inc(x_root, 1)
                    act.wait_ge(x_rstd, c + 1)
                    act.wait_ge(x_turned, c)
                    S.activation(xn, xt[:, s], ACT.Copy, scale=rstd[:, s:s + 1]).then_inc(x_scaled, 1)
                    turned(c, s)
            act.wait_ge(cols_ready, 1)
            act.wait_ge(raw_out, TC)
            for k in range(KC):
                S.activation(hh[:, k], raw[:, k], ACT.Identity, scale=cols[:, KC + k:KC + k + 1], bias=cols[:, k:k + 1]).then_inc(hi_out, 1)
            act.wait_ge(consts, 3)
            act.wait_ge(lo_out, KC)
            with act.Fori(0, KC) as j:
                act.wait_ge(projected[0], j + 1)
                act.wait_ge(xc_ready, j)
                S.activation(xlp[:, 3:3 + T], ps_xl[:], ACT.Copy).then_inc(xl_out, 1)
                act.wait_ge(projected[1], j + 1)
                act.wait_ge(lru_out, j)
                S.activation(xg, ps_xg[:], ACT.Copy).then_inc(xg_out, 1)
                act.wait_ge(pin_ready, j + 1)
                S.activation(tg, pin, ACT.Tanh, scale=GELU_B).then_inc(tg_out, 1)
                act.wait_ge(projected[2], j + 1)
                S.activation(tb, ps_gb[:], ACT.Tanh, scale=0.5).then_inc(tb_out, 1)
                act.wait_ge(p_gr, j + 1)
                act.wait_ge(parj_ready, j + 1)
                S.activation(tr, ps_gate[:], ACT.Tanh, scale=0.5, bias=parj[:, 5:6]).then_inc(tr_out, 1)
                act.wait_ge(p_gi, j + 1)
                S.activation(ti, ps_xl[:], ACT.Tanh, scale=0.5, bias=parj[:, 6:7]).then_inc(ti_out, 1)
                act.wait_ge(nla_ready, j + 1)
                S.activation(av, tr, ACT.Exp, scale=-1.0).then_inc(a_out, 1)
                S.activation(th, tr, ACT.Tanh).then_inc(th_out, 1)
                act.wait_ge(mu2_ready, j + 1)
                S.activation(mu, mu, ACT.Sqrt).then_inc(mu_root, 1)

        @block.tensor
        def _(pe):
            def ada_columns(m, s):
                pe.wait_ge(ada_ready, m + 1)
                nc.tensor.matmul(ada_banks[s], ones[:], ada_sum[:, s], start=True, stop=True).then_inc(ada_done, 1)

            pe.wait_ge(consts, 1)
            pe.wait_ge(small_in, 64)
            with pe.Fori(0, TC // 2) as q:
                for s in range(2):
                    c = 2 * q + s
                    pe.wait_ge(mod_out, c)
                    ada_columns(c, s)
                    pe.wait_ge(x_scaled, c + 1)
                    pe.wait_ge(raw_out, c)
                    for k in range(KC):
                        last = nc.tensor.transpose((ps_xl, ps_xg)[s][:, k * P:(k + 1) * P], xn[:, k * P:(k + 1) * P], ident[:])
                    last.then_inc(x_turned, 1)
            pe.wait_ge(raw_out, TC)
            pe.wait_ge(lo_out, KC)

            def project(ps, i, j, free):
                pe.wait_ge(w_split, 3 * j + i + 1)
                pe.wait_ge(free, j)
                for s in range(T // HALF):
                    cs = slice(s * HALF, (s + 1) * HALF)
                    for k in range(KC):
                        last = split_product(nc, ps[:, cs], wh[:, i, k], wl[:, i, k], hh[:, k, cs], hl[:, k, cs], k == 0, k == KC - 1)
                last.then_inc(projected[i], 1)

            with pe.Fori(0, KC) as j:
                project(ps_xl, 0, j, ti_out)
                project(ps_xg, 1, j, xg_out)
                pe.wait_ge(tr_out, j)
                pe.wait_ge(mod_out, MOD1 + 2 * j)
                for s in range(2):
                    ada_columns(MOD1 + 2 * j + s, s)
                project(ps_gb, 2, j, tb_out)
                pe.wait_ge(wg_in, 16 * (j + 1))
                pe.wait_ge(xc_ready, j + 1)
                pe.wait_ge(mod_out, MOD1 + 2 * j + 2)
                for s in range(T // HALF):
                    last = nc.tensor.matmul(ps_gate[:, s * HALF:(s + 1) * HALF], wgate[:, 0], xc[:, s * HALF:(s + 1) * HALF], start=True, stop=True)
                last.then_inc(p_gr, 1)
                pe.wait_ge(xl_out, j + 1)
                for s in range(T // HALF):
                    last = nc.tensor.matmul(ps_xl[:, s * HALF:(s + 1) * HALF], wgate[:, 1], xc[:, s * HALF:(s + 1) * HALF], start=True, stop=True)
                last.then_inc(p_gi, 1)

        @block.vector
        def _(dve):
            v = nc.vector
            step = Chain(dve, dve_step)
            SUMS = KC - 1

            def ada_sums(m, s, count):
                dve.wait_ge(ada_in[s], count)
                dve.wait_ge(ada_done, m)
                step(v.tensor_scalar(ada_sum[:, s], ada[:, s, 0], cact[:, 0:1], None, ALU.mult))
                for k in range(1, KC - 1):
                    step(v.scalar_tensor_tensor(ada_sum[:, s], ada[:, s, k], cact[:, k:k + 1], ada_sum[:, s], ALU.mult, ALU.add))
                v.scalar_tensor_tensor(ada_sum[:, s], ada[:, s, KC - 1], cact[:, KC - 1:KC], ada_sum[:, s], ALU.mult, ALU.add).then_inc(ada_ready, 1)

            def mod_tile(m, s):
                dve.wait_ge(ada_done, m + 1)
                v.tensor_tensor(mod[:, s], ada_banks[s], ada_bias[:, s], ALU.add).then_inc(mod_out, 1)
                dve.wait_ge(mod_out, m + 1)

            dve.wait_ge(small_in, 64)
            lam = par[:].rearrange("p (j q) -> p j q", q=NPAR)[:, :, 7]
            v.scalar_tensor_tensor(ptmp[:, 0], lam, -1.0, lam, ALU.mult, ALU.max).then_inc(par_abs, 1)
            dve.wait_ge(c_tanh, 1)
            step(v.tensor_scalar(cact[:], cact[:], 1.0, 0.5, ALU.add, ALU.mult))
            step(v.tensor_tensor(cact[:], cact[:], cT[:], ALU.mult))
            with dve.Fori(0, MOD1 // 2) as q:
                step.loop(q, 2 * (SUMS + 2))
                for s in range(2):
                    m = 2 * q + s
                    ada_sums(m, s, 32 * (q + 1))
                    dve.wait_ge(x_root, m + 1)
                    v.reciprocal(rstd[:, s:s + 1], ss[:, s:s + 1]).then_inc(x_rstd, 1)
                    mod_tile(m, s)
                    step(v.tensor_tensor(diag.rearrange("p (k c) -> p k c", k=CQ), mod[:, s].rearrange("p (k c) -> p k c", k=CQ),
                                         ident[:].unsqueeze(1).broadcast_to([P, CQ, P]), ALU.mult))
                    step(v.tensor_reduce(cols[:, bass.ds(m * CQ, CQ)], diag.rearrange("p (k c) -> p k c", k=CQ), AX.X, ALU.add))
            step.end(MOD1 // 2)
            v.scalar_tensor_tensor(cols[:, KC:], cols[:, KC:], 1.0, gain[:], ALU.add, ALU.mult).then_inc(cols_ready, 1)
            dve.wait_ge(cols_ready, 1)
            for k in range(KC):
                dve.wait_ge(hi_out, k + 1)
                v.tensor_scalar(raw[:, k], raw[:, k], cols[:, KC + k:KC + k + 1], cols[:, k:k + 1], ALU.mult, ALU.add).then_inc(h_out, 1)
                dve.wait_ge(h_out, k + 1)
                v.tensor_tensor(hl[:, k], raw[:, k], hh[:, k], ALU.subtract).then_inc(lo_out, 1)
            dve.wait_ge(par_exp, 1)
            step(v.tensor_scalar(ptmp[:, 2], ptmp[:, 1], 2.0, None, ALU.add))
            step(v.reciprocal(ptmp[:, 3], ptmp[:, 2]))
            step(v.tensor_tensor(ptmp[:, 2], ptmp[:, 1], ptmp[:, 3], ALU.mult))
            step(v.tensor_tensor(ptmp[:, 3], ptmp[:, 2], ptmp[:, 2], ALU.mult))
            step(v.tensor_scalar(ptmp[:, 4], ptmp[:, 3], 1.0 / 17, None, ALU.mult))
            for m in (15, 13, 11, 9, 7, 5, 3):
                step(v.scalar_tensor_tensor(ptmp[:, 4], ptmp[:, 4], 1.0 / m, ptmp[:, 3], ALU.add, ALU.mult))
            step(v.scalar_tensor_tensor(ptmp[:, 4], ptmp[:, 4], 1.0, ptmp[:, 2], ALU.add, ALU.mult))
            step(v.tensor_scalar(ptmp[:, 0], lam, -0.5 * SCAN_C, 0.0, ALU.mult, ALU.max))
            step(v.scalar_tensor_tensor(lam, ptmp[:, 4], SCAN_C, ptmp[:, 0], ALU.mult, ALU.add))
            halves = par[:].rearrange("p (j q) -> p j q", q=NPAR)[:, :, 5:7]
            step(v.tensor_scalar(halves, halves, 0.5, None, ALU.mult))
            dve.wait_ge(lo_out, KC)
            v.memset(xlp[:, 0:3], 0.0).then_inc(consts, 1)
            with dve.Fori(0, KC) as j:
                step.loop(j, 2 * SUMS + 3 + 1 + 4 + 3)
                v.tensor_copy(parj[:], par[:, bass.ds(j * NPAR, NPAR)]).then_inc(parj_ready, 1)
                dve.wait_ge(xl_out, j + 1)
                dve.wait_ge(parj_ready, j + 1)
                step(v.tensor_scalar(xc, xlp[:, 3:3 + T], parj[:, 3:4], parj[:, 4:5], ALU.mult, ALU.add))
                step(v.scalar_tensor_tensor(xc, xlp[:, 2:2 + T], parj[:, 2:3], xc, ALU.mult, ALU.add))
                step(v.scalar_tensor_tensor(xc, xlp[:, 1:1 + T], parj[:, 1:2], xc, ALU.mult, ALU.add))
                v.scalar_tensor_tensor(xc, xlp[:, 0:T], parj[:, 0:1], xc, ALU.mult, ALU.add).then_inc(xc_ready, 1)
                for s in range(2):
                    ada_sums(MOD1 + 2 * j + s, s, 32 * (MOD1 // 2 + j + 1))
                for s in range(2):
                    dve.wait_ge(mod_stored[s], 16 * j)
                    mod_tile(MOD1 + 2 * j + s, s)
                dve.wait_ge(xg_out, j + 1)
                step(v.scalar_tensor_tensor(pin, xg, GELU_A, xg, ALU.mult, ALU.mult))
                v.scalar_tensor_tensor(pin, pin, 1.0, xg, ALU.add, ALU.mult).then_inc(pin_ready, 1)
                dve.wait_ge(tr_out, j + 1)
                v.tensor_scalar(tr, tr, 1.0, parj[:, 7:8], ALU.add, ALU.mult).then_inc(nla_ready, 1)
                dve.wait_ge(a_out, j + 1)
                step(v.tensor_tensor(mu, av, av, ALU.mult))
                dve.wait_ge(th_out, j + 1)
                v.scalar_tensor_tensor(mu, mu, 1.0, th, ALU.add, ALU.mult).then_inc(mu2_ready, 1)
                dve.wait_ge(ti_out, j + 1)
                step(v.scalar_tensor_tensor(ti, ti, 1.0, xc, ALU.add, ALU.mult))
                dve.wait_ge(tg_out, j + 1)
                step(v.scalar_tensor_tensor(tg, tg, 1.0, xg, ALU.add, ALU.mult))
                dve.wait_ge(tb_out, j + 1)
                step(v.scalar_tensor_tensor(tg, tb, 1.0, tg, ALU.add, ALU.mult))
                dve.wait_ge(mu_root, j + 1)
                step(v.scalar_tensor_tensor(mu, ti, 0.5, mu, ALU.mult, ALU.mult))
                step(v.tensor_tensor_scan(th, av, mu, 0.0, ALU.mult, ALU.add))
                dve.wait_ge(lru_stored, 16 * j)
                step(v.scalar_tensor_tensor(lru[:], th, 0.25, tg, ALU.mult, ALU.mult))
                dve.sem_inc(lru_out, 1)
            step.end(KC)


def gated_linear_attention(nc, ctx, keep, a, merged_dram):
    hh, hl, ident = keep["hh"], keep["hl"], keep["ident"]
    TILES = 8
    NL = LEVELS + 1
    with ExitStack() as scope:
        def sb(name, shape, dt=F32):
            return scope.enter_context(nc.sbuf_tensor(name, shape, dt))

        def sem(name):
            return ctx.enter_context(nc.semaphore(name))

        ps_a = scope.enter_context(nc.psum_tensor("ps_a", [P, T], F32))
        ps_b = scope.enter_context(nc.psum_tensor("ps_b", [P, T], F32))
        ps_s = scope.enter_context(nc.psum_tensor("ps_s", [P, NL * P], F32))
        ps_o = scope.enter_context(nc.psum_tensor("ps_o", [P, HALF], F32))
        ps_t = scope.enter_context(nc.psum_tensor("ps_t", [P, HALF], F32))
        o_banks = (ps_a[:, 0:DV], ps_a[:, HALF:HALF + DV])

        masks = sb("masks", [P, NL * P])
        ones = sb("ones2", [P, P])
        eps = sb("eps2", [P, 1])
        w_alh, w_all = sb("w_alh", [P, KC, RANK], F32R), sb("w_all", [P, KC, RANK], F32R)
        alow = sb("alow", [RANK, T])
        hpar = sb("hpar", [P, HEADS * 3])
        hp = sb("hp", [P, 3])
        w_alpha = sb("w_alpha", [RANK, DK])
        wt = sb("wt2", [P, 2, KC, P])
        wh, wl = sb("wh2", [P, 4, KC, P], F32R), sb("wl2", [P, 4, KC, P], F32R)
        q = sb("q", [P, T])
        k = sb("k", [P, T])
        V = sb("V", [P, TC, DV])
        oT = sb("oT", [P, 2, T])
        zl, cum = oT[:, 0], oT[:, 1]
        X = sb("X", [P, LEVELS, T])
        qe = sb("qe", [P, T])
        kd = sb("kd", [P, T])
        elast = sb("elast", [P, TC])
        gate = sb("gate", [P, 2, T])
        tnh = sb("tnh", [P, 2, HALF])
        sm = sb("sm", [P, NL * P])
        S = sb("S", [P, 2, P])
        kdT = sb("kdT", [P, TC, DK])
        state = sb("state", [P, DV])
        junk = sb("junk2", [P, DV])
        ss = sb("ss2", [P, TC])
        rstd = sb("rstd2", [P, TC])
        on = sb("on", [P, 2, DV])
        w_al = on[:, 0, 0:KC * RANK].rearrange("p (k r) -> p k r", k=KC)
        mix = sb("mix", [P, 2, T])

        small_in, const = sem("small_in2"), sem("consts2")
        al_in, al_hi, al_split, wal_in = sem("al_in"), sem("al_hi"), sem("al_split"), sem("walpha_in")
        wt_in = [sem("wt_in0"), sem("wt_in1")]
        w_hi, w_split = sem("gla_w_hi"), sem("gla_w_split")
        mix_in = sem("mix_in")
        al_done, al_out = sem("al_done"), sem("al_out")
        z_done, q_done, k_done, v_done = sem("z_done"), sem("q_done"), sem("k_done"), sem("v_done")
        rg_done = sem("rg_done")
        hp_ready = sem("hp_ready")
        z_abs, z_min, l_out = sem("z_abs"), sem("z_min"), sem("l_out")
        q_out, k_out, v_out = sem("q_out"), sem("k_out"), sem("v_out")
        diff_ready = sem("diff_ready")
        exp_out = sem("exp_out")
        x_ready = sem("x_ready")
        r_raw, rg_out, pool_go = sem("r_raw"), sem("rg_out"), keep["pool_go"]
        gate_step = sem("gate_step")
        s_done, s_masked, s_ready = sem("s_done"), sem("s_masked"), sem("s_ready")
        kt_done, kt_out = sem("kt_done"), sem("kt_out")
        o_done, up_done, state_out = sem("o_done"), sem("up_done"), sem("state_out")
        o_sq, o_root, o_rstd, on_out = sem("o_sq"), sem("o_root"), sem("o_rstd"), sem("on_out")
        ot_done, ot_out = sem("ot_done"), sem("ot_out")
        head_out, merged_out = sem("head_out"), sem("merged_out")
        dve_step = sem("dve_step2")

        block = scope.enter_context(nc.Block())

        @block.sync
        def _(sp):
            sp.dma_start(w_al, a["w_al"]).then_inc(al_in, 16)
            sp.dma_start(masks[:], a["masks"]).then_inc(small_in, 16)
            sp.dma_start(hpar[:], a["head_par"]).then_inc(small_in, 16)

            def load_tile(n, s):
                sp.dma_start(wt[:, s], a["w_head"][bass.ds(n, 1)].rearrange("o p k c -> p (o k) c")).then_inc(wt_in[s], 16)

            def mix_at(h):
                return merged_dram[:, bass.ds(2 * h, 2), :]

            for s in range(2):
                load_tile(s, s)
            sp.dma_start(w_alpha[:], a["w_alpha"][0]).then_inc(wal_in, 16)
            sp.dma_start(mix[:], mix_at(0)).then_inc(mix_in, 16)

            def head(h, last):
                for i in range(2, TILES if last else TILES + 2):
                    sp.wait_ge(w_split, TILES * h + i - 1)
                    load_tile(TILES * h + i, i % 2)
                    if i == 3 and not last:
                        sp.wait_ge(z_done, h + 1)
                        sp.dma_start(w_alpha[:], a["w_alpha"][bass.ds(h + 1, 1)].rearrange("o r c -> (o r) c")).then_inc(wal_in, 16)
                sp.wait_ge(head_out, h + 1)
                sp.dma_start(mix_at(h), mix[:]).then_inc(merged_out, 16)
                sp.wait_ge(merged_out, 16 * (h + 1))
                if not last:
                    sp.dma_start(mix[:], mix_at(h + 1)).then_inc(mix_in, 16)

            with sp.Fori(0, HEADS - 1) as h:
                head(h, False)
            head(HEADS - 1, True)

        @block.gpsimd
        def _(pool):
            nc.gpsimd.memset(eps[:], EPS).then_inc(const, 1)
            g = nc.gpsimd
            g.memset(ones[:], 1.0).then_inc(const, 1)
            pool.wait_ge(al_in, 16)
            g.tensor_copy(w_alh[:], w_al).then_inc(al_hi, 1)
            pool.wait_ge(al_hi, 1)
            g.tensor_tensor(w_all[:], w_al, w_alh[:], ALU.subtract).then_inc(al_split, 1)
            def split(h, i):
                n = TILES * h + i
                pool.wait_ge(wt_in[i % 2], 16 * (TILES // 2 * h + i // 2 + 1))
                pool.sem_inc(pool_go, 1)
                g.tensor_copy(wh[:, i % 4], wt[:, i % 2]).then_inc(w_hi, 1)
                pool.wait_ge(w_hi, n + 1)
                g.tensor_tensor(wl[:, i % 4], wt[:, i % 2], wh[:, i % 4], ALU.subtract).then_inc(w_split, 1)

            def gate_tiles(h):
                for i, (used, count) in enumerate(((q_done, 1), (k_done, 1), (v_done, 2), (v_done, 2))):
                    pool.wait_ge(used, count * (h + 1))
                    split(h, 4 + i)

            for i in range(4):
                split(0, i)
            with pool.Fori(0, HEADS - 1) as h:
                gate_tiles(h)
                for i in range(4):
                    pool.wait_ge(rg_done, TC * h + 2 * (i + 1))
                    split(h + 1, i)
            gate_tiles(HEADS - 1)

        @block.scalar
        def _(act):
            act.wait_ge(const, 1)
            act.wait_ge(al_done, 1)
            nc.scalar.activation(alow[:], ps_a[0:RANK, :], ACT.Copy).then_inc(al_out, 1)
            with act.Fori(0, HEADS) as h:
                act.wait_ge(z_done, h + 1)
                act.wait_ge(hp_ready, h + 1)
                act.wait_ge(head_out, h)
                nc.scalar.activation(zl, ps_a[:], ACT.Abs, bias=hp[:, 0:1]).then_inc(z_abs, 1)
                act.wait_ge(z_abs, 2 * h + 1)
                nc.scalar.activation(zl, zl, ACT.Exp, scale=-1.0).then_inc(z_abs, 1)
                act.wait_ge(z_abs, 2 * h + 2)
                nc.scalar.activation(zl, zl, ACT.Ln, bias=1.0).then_inc(l_out, 1)
                act.wait_ge(q_done, h + 1)
                act.wait_ge(s_done, TC * h)
                nc.scalar.activation(q[:], ps_b[:], ACT.Copy, scale=DK ** -0.5).then_inc(q_out, 1)
                act.wait_ge(k_done, h + 1)
                nc.scalar.activation(k[:], ps_a[:], ACT.Copy).then_inc(k_out, 1)
                for n in range(LEVELS):
                    half = P >> (n + 1)
                    pairs = X[:, n].rearrange("p (b w t) -> p b w t", w=2, t=half)
                    act.wait_ge(diff_ready, NL * h + n + 1)
                    nc.scalar.activation(pairs[:, :, 0], pairs[:, :, 0], ACT.Exp, scale=-1.0 / TAU)
                    nc.scalar.activation(pairs[:, :, 1], pairs[:, :, 1], ACT.Exp, scale=1.0 / TAU).then_inc(exp_out, 1)
                act.wait_ge(diff_ready, NL * h + NL)
                nc.scalar.activation(kd[:], kd[:], ACT.Exp, scale=-1.0 / TAU).then_inc(exp_out, 1)
                nc.scalar.activation(qe[:], cum, ACT.Exp, scale=1.0 / TAU).then_inc(exp_out, 1)
                nc.scalar.activation(elast[:], cum.rearrange("p (c t) -> p c t", t=P)[:, :, P - 1], ACT.Exp, scale=1.0 / TAU).then_inc(exp_out, 1)
                act.wait_ge(up_done, TC * h)
                for i, bank in enumerate((ps_b, ps_a)):
                    act.wait_ge(v_done, 2 * h + i + 1)
                    nc.scalar.activation(V[:, i * 4:(i + 1) * 4].rearrange("p c d -> p (c d)"), bank[:], ACT.Copy).then_inc(v_out, 1)
                def gate_half(u):
                    i, s = u // 2, u % 2
                    bank = ps_b[:, s * HALF:(s + 1) * HALF]
                    act.wait_ge(rg_done, TC * h + u + 1)
                    if i < 2:
                        nc.scalar.activation(gate[:, i, s * HALF:(s + 1) * HALF], bank, ACT.Copy).then_inc(r_raw, 1)
                    if u >= 2:
                        act.wait_ge(gate_step, TC * h + u - 1)
                    nc.scalar.activation(tnh[:, s], bank, ACT.Tanh, scale=0.5).then_inc(rg_out, 1)

                for i, bank in enumerate((ps_t, ps_o)):
                    act.wait_ge(kt_done, 2 * h + i + 1)
                    nc.scalar.activation(kdT[:, 4 * i:4 * i + 4].rearrange("p c d -> p (c d)"), bank[:], ACT.Copy).then_inc(kt_out, 1)

                def turned_out(c):
                    act.wait_ge(ot_done, TC * h + c + 1)
                    nc.scalar.activation(oT[:, :, c * P:(c + 1) * P], ps_t[:, 0:2 * P].rearrange("p (v t) -> p v t", v=2), ACT.Copy).then_inc(ot_out, 1)

                for c in range(TC):
                    gate_half(c)
                    n = TC * h + c
                    o = o_banks[c % 2]
                    act.wait_ge(o_done, n + 1)
                    nc.scalar.activation(junk[:], o, ACT.Square, scale=DV ** -0.5, accum_out=ss[:, c:c + 1]).then_inc(o_sq, 1)
                    act.wait_ge(o_sq, n + 1)
                    nc.scalar.activation(ss[:, c:c + 1], ss[:, c:c + 1], ACT.Sqrt, bias=eps[:]).then_inc(o_root, 1)
                    act.wait_ge(o_rstd, n + 1)
                    if c >= 2:
                        act.wait_ge(ot_done, n - 1)
                    nc.scalar.activation(on[:, c % 2], o, ACT.Copy, scale=rstd[:, c:c + 1]).then_inc(on_out, 1)
                    if c >= 1:
                        turned_out(c - 1)
                turned_out(TC - 1)

        @block.tensor
        def _(pe):
            def project(out, w_h, w_l, halves=range(T // HALF)):
                for s in halves:
                    cs = slice(s * HALF, (s + 1) * HALF)
                    for kk in range(KC):
                        last = split_product(nc, out[:, cs], w_h[:, kk], w_l[:, kk], hh[:, kk, cs], hl[:, kk, cs], kk == 0, kk == KC - 1)
                return last

            pe.wait_ge(al_split, 1)
            project(ps_a[0:RANK], w_alh, w_all).then_inc(al_done, 1)
            pe.wait_ge(al_out, 1)
            with pe.Fori(0, HEADS) as h:
                pe.wait_ge(wal_in, 16 * (h + 1))
                pe.wait_ge(on_out, TC * h)
                pe.wait_ge(state_out, TC * h)
                pe.wait_ge(s_masked, TC * h)
                for s in range(T // HALF):
                    last = nc.tensor.matmul(ps_a[:, s * HALF:(s + 1) * HALF], w_alpha[:], alow[:, s * HALF:(s + 1) * HALF], start=True, stop=True)
                last.then_inc(z_done, 1)
                pe.wait_ge(w_split, TILES * h + 1)
                project(ps_b, wh[:, 0], wl[:, 0]).then_inc(q_done, 1)
                pe.wait_ge(z_abs, 2 * h + 1)
                pe.wait_ge(z_min, h + 1)
                pe.wait_ge(w_split, TILES * h + 2)
                project(ps_a, wh[:, 1], wl[:, 1]).then_inc(k_done, 1)
                pe.wait_ge(w_split, TILES * h + 4)
                for i, (bank, free) in enumerate(((ps_b, q_out), (ps_a, k_out))):
                    pe.wait_ge(free, h + 1)
                    for c in range(4 * i, 4 * i + 4):
                        ct = slice(c * P, (c + 1) * P)
                        for kk in range(KC):
                            last = split_product(nc, bank[:, (c % 4) * DV:(c % 4 + 1) * DV], hh[:, kk, ct], hl[:, kk, ct], wh[:, 2:4, kk], wl[:, 2:4, kk], kk == 0, kk == KC - 1)
                    last.then_inc(v_done, 1)

                def gate_half(u):
                    pe.wait_ge(w_split, TILES * h + 4 + u // 2 + 1)
                    if u < 2:
                        pe.wait_ge(v_out, 2 * h + 1)
                    else:
                        pe.wait_ge(rg_out, TC * h + u - 1)
                    project(ps_b, wh[:, u // 2], wl[:, u // 2], [u % 2]).then_inc(rg_done, 1)

                def scores(c):
                    cols = slice(c * P, (c + 1) * P)
                    bank = ps_s
                    if c >= 1:
                        pe.wait_ge(s_masked, TC * h + c)
                    if c == 0:
                        pe.wait_ge(x_ready, (LEVELS + 2) * (h + 1))
                    for n in range(LEVELS):
                        nc.tensor.matmul(bank[:, n * P:(n + 1) * P], X[:, n, cols], X[:, n, cols], start=True, stop=True)
                    nc.tensor.matmul(bank[:, LEVELS * P:], k[:, cols], q[:, cols], start=True, stop=True).then_inc(s_done, 1)

                def turn(c):
                    pe.wait_ge(on_out, TC * h + c + 1)
                    pe.wait_ge(ot_out, TC * h + c)
                    for i in range(2):
                        last = nc.tensor.transpose(ps_t[:, i * P:(i + 1) * P], on[:, c % 2, i * P:(i + 1) * P], ident[:])
                    last.then_inc(ot_done, 1)

                scores(0)
                for i, bank in enumerate((ps_t, ps_o)):
                    for c in range(4):
                        last = nc.tensor.transpose(bank[:, c * P:(c + 1) * P], kd[:, (4 * i + c) * P:(4 * i + c + 1) * P], ident[:])
                    last.then_inc(kt_done, 1)
                gate_half(0)
                for c in range(TC):
                    if c + 1 < TC:
                        scores(c + 1)
                    n = TC * h + c
                    bank = o_banks[c % 2]
                    pe.wait_ge(s_ready, n + 1)
                    if c >= 2:
                        pe.wait_ge(on_out, n - 1)
                    if c == 0:
                        pe.wait_ge(v_out, 2 * h + 2)
                    last = nc.tensor.matmul(bank, S[:, c % 2], V[:, c], start=True, stop=(c == 0))
                    if c == 0:
                        last.then_inc(o_done, 1)
                    else:
                        pe.wait_ge(state_out, n)
                        nc.tensor.matmul(bank, qe[:, c * P:(c + 1) * P], state[:], start=False, stop=True).then_inc(o_done, 1)
                    pe.wait_ge(kt_out, 2 * h + 2)
                    pe.wait_ge(state_out, n)
                    nc.tensor.matmul(ps_o[:, 0:DV], kdT[:, c], V[:, c], start=True, stop=True).then_inc(up_done, 1)
                    if c >= 1:
                        turn(c - 1)
                    if c + 1 < TC:
                        gate_half(c + 1)
                turn(TC - 1)

        @block.vector
        def _(dve):
            v = nc.vector
            step = Chain(dve, dve_step)
            dve.wait_ge(small_in, 32)
            dve.wait_ge(const, 2)
            with dve.Fori(0, HEADS) as h:
                step.loop(h, 2 + 4)
                v.tensor_copy(hp[:], hpar[:, bass.ds(h * 3, 3)]).then_inc(hp_ready, 1)
                dve.wait_ge(hp_ready, h + 1)
                dve.wait_ge(z_done, h + 1)
                dve.wait_ge(z_abs, 2 * h + 1)
                v.tensor_scalar(cum, ps_a[:], hp[:, 0:1], 0.0, ALU.add, ALU.min).then_inc(z_min, 1)
                dve.wait_ge(z_min, h + 1)
                dve.wait_ge(l_out, h + 1)
                step(v.tensor_tensor(zl, cum, zl, ALU.subtract))
                dve.wait_ge(z_min, h + 1)
                for c in range(TC):
                    ct = slice(c * P, (c + 1) * P)
                    last = v.tensor_tensor_scan(cum[:, ct], ones[:], zl[:, ct], 0.0, ALU.mult, ALU.add)
                step(last)
                dve.wait_ge(o_done, TC * h)
                for n in range(LEVELS):
                    half = P >> (n + 1)
                    c4 = cum.rearrange("p (b w t) -> p b w t", w=2, t=half)
                    nb = T // (2 * half)
                    middle = c4[:, :, 0:1, half - 1:half].broadcast_to([P, nb, 2, half])
                    v.tensor_tensor(X[:, n].rearrange("p (b w t) -> p b w t", w=2, t=half), c4, middle, ALU.subtract).then_inc(diff_ready, 1)
                c3 = cum.rearrange("p (c t) -> p c t", t=P)
                v.tensor_tensor(kd[:].rearrange("p (c t) -> p c t", t=P), c3, c3[:, :, P - 1:P].broadcast_to([P, TC, P]), ALU.subtract).then_inc(diff_ready, 1)
                dve.wait_ge(q_out, h + 1)
                dve.wait_ge(k_out, h + 1)
                for n in range(LEVELS):
                    half = P >> (n + 1)
                    w4 = lambda t: t.rearrange("p (b w t) -> p b w t", w=2, t=half)
                    dve.wait_ge(exp_out, (LEVELS + 3) * h + n + 1)
                    v.tensor_tensor(w4(X[:, n])[:, :, 0], w4(X[:, n])[:, :, 0], w4(k[:])[:, :, 0], ALU.mult)
                    v.tensor_tensor(w4(X[:, n])[:, :, 1], w4(X[:, n])[:, :, 1], w4(q[:])[:, :, 1], ALU.mult).then_inc(x_ready, 1)
                dve.wait_ge(exp_out, (LEVELS + 3) * h + LEVELS + 3)
                v.tensor_tensor(kd[:], kd[:], k[:], ALU.mult).then_inc(x_ready, 1)
                v.tensor_tensor(qe[:], qe[:], q[:], ALU.mult).then_inc(x_ready, 1)
                def gate_half(u):
                    part = gate[:, u // 2 % 2, u % 2 * HALF:(u % 2 + 1) * HALF]
                    dve.wait_ge(rg_out, TC * h + u + 1)
                    dve.wait_ge(r_raw, 4 * h + min(u + 1, 4))
                    if u >= 4:
                        dve.wait_ge(gate_step, TC * h + u - 3)
                    v.scalar_tensor_tensor(part, tnh[:, u % 2], 1.0, part, ALU.add, ALU.mult).then_inc(gate_step, 1)

                def mask(c):
                    n = TC * h + c
                    dve.wait_ge(s_done, n + 1)
                    dve.wait_ge(s_ready, n)
                    v.tensor_tensor(sm[:], ps_s[:], masks[:], ALU.mult).then_inc(s_masked, 1)
                    dve.wait_ge(s_masked, n + 1)
                    if c >= 2:
                        dve.wait_ge(o_done, n - 1)
                    v.tensor_reduce(S[:, c % 2], sm[:].rearrange("p (l t) -> p t l", l=NL), AX.X, ALU.add).then_inc(s_ready, 1)

                mask(0)
                for c in range(TC):
                    n = TC * h + c
                    if c + 1 < TC:
                        mask(c + 1)
                    dve.wait_ge(up_done, n + 1)
                    up = ps_o[:, 0:DV]
                    dve.wait_ge(o_done, n + 1)
                    if c == 0:
                        v.tensor_copy(state[:], up).then_inc(state_out, 1)
                    else:
                        dve.wait_ge(state_out, n)
                        v.scalar_tensor_tensor(state[:], state[:], elast[:, c:c + 1], up, ALU.mult, ALU.add).then_inc(state_out, 1)
                    gate_half(c)
                    dve.wait_ge(o_root, n + 1)
                    v.reciprocal(rstd[:, c:c + 1], ss[:, c:c + 1]).then_inc(o_rstd, 1)
                dve.wait_ge(ot_out, TC * (h + 1))
                dve.wait_ge(gate_step, TC * (h + 1))
                dve.wait_ge(mix_in, 16 * (h + 1))
                for i in range(2):
                    step(v.scalar_tensor_tensor(gate[:, i], oT[:, i], hp[:, 1 + i:2 + i], gate[:, i], ALU.mult, ALU.mult))
                    step(v.scalar_tensor_tensor(mix[:, i], gate[:, i], 0.25, mix[:, i], ALU.mult, ALU.add))
                dve.sem_inc(head_out, 1)
            step.end(HEADS)


def peer_block(nc, ctx, keep, a, mod_dram, merged_dram, out):
    ident = keep["ident"]
    R = 8
    GROUPS = TOPK // R
    VR = ND = 4
    with ExitStack() as scope:
        def sb(name, shape, dt=F32):
            return scope.enter_context(nc.sbuf_tensor(name, shape, dt))

        def sem(name):
            return ctx.enter_context(nc.semaphore(name))

        def psum(name, cols):
            return scope.enter_context(nc.psum_tensor(name, [P, cols], F32))

        ps_acc, ps_y, ps_h, ps_sc = psum("ps_acc", D), psum("ps_y", D), psum("ps_h", D), psum("ps_sc", HALF)

        Wk = sb("Wk", [P, KC, 2 * PH * NK])
        w_out = sb("w_out", [P, KC, D])
        mod = sb("mod", [P, 4 * D])
        mT = sb("mT", [P, KC, P])
        x2n, x2c = sb("x2n", [P, D]), sb("x2c", [P, D])
        h2n, h2c = sb("h2n", [P, D]), sb("h2c", [P, D])
        h2T = sb("h2T", [P, KC, P])
        yf = sb("yf", [P, D])
        ur, vr = sb("ur", [P, R, D]), sb("vr", [P, VR, D])
        diag = sb("diag", [P, ND, P])
        zero = sb("zero", [P, P], mybir.dt.bfloat16)
        idx = sb("idx", [P, 2 * SLOTS], U32)
        gates = sb("gates", [P, 2 * SLOTS])
        uidx, vidx = sb("uidx", [P, 2, R], U32), sb("vidx", [P, 2, R], U32)
        sc2 = sb("sc2", [P, 2, NK])
        top = sb("top", [P, 2, TOPK])
        topi = sb("topi", [P, 2, TOPK], U32)
        topf = sb("topf", [P, 2, TOPK])
        best = sb("best", [P, TOPK])
        pos = sb("pos", [P, TOPK], U32)
        ab = sb("ab", [P, 2, TOPK], U32)
        abf = sb("abf", [P, 2, TOPK])
        iota = sb("iota", [P, TOPK])
        eq = sb("eq", [P, 2, TOPK, TOPK])
        pick = sb("pick", [P, 2, TOPK])
        negm = sb("negm", [P, 1])
        esum = sb("esum", [P, 1])
        ex = sb("ex", [P, TOPK])
        dots = sb("dots", [P, R])
        gel = sb("gel", [P, R])
        coef = sb("coef", [P, GROUPS, R])
        eps = sb("eps3", [P, 1])
        ss = sb("ss3", [P, 3])
        rstd = sb("rstd3", [P, 3])

        const, small_in = sem("consts3"), sem("small_in3")
        wout_in = [sem("wout_in0"), sem("wout_in1")]
        wq_in = [sem("wq_in0"), sem("wq_in1")]
        wk_done, wk_out = sem("wk_done"), sem("wk_out")
        mod_ready = sem("mod_ready")
        x_in, m_in = sem("x_in3"), sem("m_in")
        y_done, y_sq, y_root, y_rstd, y_used = sem("y_done"), sem("y_sq"), sem("y_root"), sem("y_rstd"), sem("y_used")
        x2_ready, h2_ready, h2_turned, h2T_out, h2_copied = sem("x2_ready"), sem("h2_ready"), sem("h2_turned"), sem("h2T_out"), sem("h2_copied")
        sc_done, sc_used = sem("sc_done"), sem("sc_used")
        negm_ready, ex_out, sel_ready = sem("negm_ready"), sem("ex_out"), sem("sel_ready")
        ucopy, vcopy, pool_go = sem("ucopy"), sem("vcopy"), keep["pool_go"]
        u_in = [sem(f"u_in{r}") for r in range(R)]
        v_in = [sem(f"v_in{r}") for r in range(VR)]
        u_used, v_used = sem("u_used"), sem("v_used")
        gel_ready, tanh_out, coef_ready, diag_out = sem("gel_ready"), sem("tanh_out"), sem("coef_ready"), sem("diag_out")
        acc_done, acc_out, f_root, f_rstd, f_ready, out_done = (sem(n) for n in ("acc_done", "acc_out", "f_root", "f_rstd", "f_ready", "out_done"))
        dve_step, dve_go = sem("dve_step3"), sem("dve_go3")

        block = scope.enter_context(nc.Block())
        half = lambda s: slice(s * HALF, (s + 1) * HALF)
        wk_banks = (ps_h, ps_acc)

        def group_at(G):
            return bass.ds(G % (2 * SLOTS // R) * R, R)

        @block.sync
        def _(sp):
            def load_keys(g, s):
                sp.dma_start(vr[:, s], a["wqT"][g].rearrange("o p d -> (o p) d")).then_inc(wq_in[s], 16)
                sp.dma_start(vr[:, 2 + s, 0:NK], a["keysT"][g].rearrange("o p d -> (o p) d")).then_inc(wq_in[s], 16)

            def merged_tile(t):
                sp.dma_start(mT[:], merged_dram[:, :, bass.ds(t * P, P)]).then_inc(m_in, 16)

            def x_tile(t):
                sp.dma_start(x2n[:], a["x"][bass.ds(t, 1)].rearrange("o p d -> (o p) d")).then_inc(x_in, 16)

            def store_tile(t):
                sp.wait_ge(f_ready, t + 1)
                sp.dma_start(out[bass.ds(t, 1)].rearrange("o p d -> (o p) d"), yf[:]).then_inc(out_done, 16)

            for s in range(2):
                load_keys(slice(s, s + 1), s)
            merged_tile(0)
            for s in range(2):
                sp.dma_start(w_out[:, :, s * HALF:(s + 1) * HALF], a["w_out"][:, :, s * HALF:(s + 1) * HALF]).then_inc(wout_in[s], 16)
            x_tile(0)
            sp.dma_start(mod[:], mod_dram).then_inc(small_in, 16)
            for i, n in enumerate(("gain_post_mix", "gain_pre_ffn", "gain_post_ffn")):
                sp.dma_start(ur[:, 2 + i], a[n].broadcast_to([P, D])).then_inc(small_in, 16)
            with sp.Fori(0, PH - 1) as g:
                for s in range(2):
                    sp.wait_ge(wk_done, 2 * g + s + 1)
                    load_keys(bass.ds(2 * g + s + 2, 1), s)
            sp.wait_ge(y_done, 2)
            merged_tile(1)
            with sp.Fori(1, TC - 1) as t:
                sp.wait_ge(h2_copied, t)
                x_tile(t)
                sp.wait_ge(y_done, 2 * t + 2)
                merged_tile(t + 1)
                store_tile(t - 1)
            sp.wait_ge(h2_copied, TC - 1)
            x_tile(TC - 1)
            store_tile(TC - 2)
            store_tile(TC - 1)
            sp.wait_ge(out_done, 16 * TC)

        @block.gpsimd
        def _(pool):
            nc.gpsimd.memset(eps[:], EPS).then_inc(const, 1)
            nc.gpsimd.memset(zero[:], 0.0).then_inc(const, 1)
            nc.gpsimd.iota(iota[:], [[1, TOPK]], base=0, channel_multiplier=0, allow_small_or_imprecise_dtypes=True).then_inc(const, 1)

            def copy_indices(G, par, to, copied):
                pool.sem_inc(pool_go, 1)
                nc.gpsimd.tensor_copy(to[:, par], idx[:, group_at(G)]).then_inc(copied, 1)
                pool.wait_ge(copied, G + 1)

            def gather_u(G, par, r, first=False):
                if not first:
                    pool.wait_ge(u_used, R * (G - 1) + r + 1)
                pool.sem_inc(pool_go, 1)
                pool.indirect_dma_start(ur[:, r], None, a["u"], bass.IndirectOffsetOnAxis(ap=uidx[:, par, r:r + 1], axis=0)).then_inc(u_in[r], 16)

            def gather_v(G, par, r):
                pool.wait_ge(v_used, R * G + r + 1)
                pool.sem_inc(pool_go, 1)
                pool.indirect_dma_start(vr[:, r % VR], None, a["v"], bass.IndirectOffsetOnAxis(ap=vidx[:, par, r:r + 1], axis=0)).then_inc(v_in[r % VR], 16)

            def both(G, par):
                copy_indices(G + 1, 1 - par, uidx, ucopy)
                copy_indices(G, par, vidx, vcopy)
                for r in range(R):
                    gather_u(G + 1, 1 - par, r)
                    gather_v(G, par, r)

            pool.wait_ge(mod_ready, 1)
            pool.wait_ge(sel_ready, 1)
            copy_indices(0, 0, uidx, ucopy)
            for r in range(R):
                gather_u(0, 0, r, first=True)
            pool.wait_ge(wk_done, 2 * PH)
            with pool.Fori(0, TC * PH - 1) as H:
                both(2 * H, 0)
                pool.wait_ge(sel_ready, H + 2)
                both(2 * H + 1, 1)
            last = 2 * TC * PH - 1
            both(last - 1, 0)
            copy_indices(last, 1, vidx, vcopy)
            for r in range(R):
                gather_v(last, 1, r)

        @block.scalar
        def _(act):
            S = nc.scalar
            act.wait_ge(const, 3)
            act.sem_inc(diag_out, R)

            def tile_norms(t, stored):
                act.wait_ge(y_done, 2 * t + 2)
                if stored is not None:
                    act.wait_ge(out_done, 16 * stored)
                junk = yf[:]
                S.activation(junk, ps_y[:], ACT.Square, scale=D ** -0.5, accum_out=ss[:, 0:1]).then_inc(y_sq, 1)
                act.wait_ge(y_sq, 2 * t + 1)
                S.activation(ss[:, 0:1], ss[:, 0:1], ACT.Sqrt, bias=eps[:]).then_inc(y_root, 1)
                act.wait_ge(x2_ready, t + 1)
                S.activation(junk, x2n[:], ACT.Square, scale=D ** -0.5, accum_out=ss[:, 1:2]).then_inc(y_sq, 1)
                act.wait_ge(y_sq, 2 * t + 2)
                S.activation(ss[:, 1:2], ss[:, 1:2], ACT.Sqrt, bias=eps[:]).then_inc(y_root, 1)

            def tile_turned(t):
                act.wait_ge(h2_turned, t + 1)
                S.activation(h2T[:].rearrange("p k t -> p (k t)"), ps_h[:], ACT.Copy).then_inc(h2T_out, 1)

            def select_gates(n):
                act.wait_ge(negm_ready, n + 1)
                S.activation(ex[:], best[:], ACT.Exp, bias=negm[:], accum_out=esum[:]).then_inc(ex_out, 1)

            def experts(G, par):
                act.wait_ge(gel_ready, G + 1)
                S.activation(gel[:], gel[:], ACT.Tanh, scale=GELU_B).then_inc(tanh_out, 1)
                act.wait_ge(coef_ready, G + 1)
                for r in range(R):
                    act.wait_ge(v_used, R * G + r + 1)
                    S.activation(diag[:, r % ND], ident[:], ACT.Copy, scale=coef[:, par, r:r + 1]).then_inc(diag_out, 1)

            def finish(t):
                act.wait_ge(acc_done, t + 1)
                act.wait_ge(out_done, 16 * t)
                S.activation(yf[:], ps_acc[:], ACT.Square, scale=D ** -0.5, accum_out=ss[:, 2:3]).then_inc(f_root, 1)
                act.wait_ge(f_root, 2 * t + 1)
                S.activation(yf[:], ps_acc[:], ACT.Copy).then_inc(acc_out, 1)
                S.activation(ss[:, 2:3], ss[:, 2:3], ACT.Sqrt, bias=eps[:]).then_inc(f_root, 1)

            def take_tile(t):
                act.wait_ge(h2_ready, t + 1)
                act.wait_ge(f_ready, t)
                S.activation(x2c[:], x2n[:], ACT.Copy)
                act.wait_ge(u_used, SLOTS * t)
                S.activation(h2c[:], h2n[:], ACT.Copy).then_inc(h2_copied, 1)

            def head(H, select=True):
                for s in range(GROUPS):
                    experts(GROUPS * H + s, s)
                if select:
                    select_gates(H + 2)

            def keys_out(g):
                for s in range(2):
                    act.wait_ge(wk_done, 2 * g + s + 1)
                    S.activation(Wk[:, :, bass.ds((2 * g + s) * NK, NK)], wk_banks[s][:].rearrange("p (k n) -> p k n", k=KC), ACT.Copy).then_inc(wk_out, 1)

            keys_out(0)
            tile_norms(0, None)
            tile_turned(0)
            keys_out(1)
            take_tile(0)
            with act.Fori(2, 4) as g:
                keys_out(g)
            select_gates(0)
            with act.Fori(4, PH) as g:
                keys_out(g)
            select_gates(1)
            with act.Fori(0, TC - 1) as t:
                with act.Fori(0, 2) as h:
                    head(PH * t + h)
                tile_norms(t + 1, t)
                with act.Fori(2, PH - 2) as h:
                    head(PH * t + h)
                tile_turned(t + 1)
                with act.Fori(PH - 2, PH) as h:
                    head(PH * t + h)
                finish(t)
                take_tile(t + 1)
            with act.Fori(PH * (TC - 1), PH * TC - 2) as H:
                head(H)
            for H in range(PH * TC - 2, PH * TC):
                head(H, select=False)
            finish(TC - 1)

        @block.tensor
        def _(pe):
            pe.sem_inc(v_used, VR)
            def tile_half(t, s):
                pe.wait_ge(m_in, 16 * (t + 1))
                pe.wait_ge(y_used, t)
                for k in range(KC):
                    last = nc.tensor.matmul(ps_y[:, bass.ds(s * HALF, HALF)], mT[:, k], w_out[:, k, bass.ds(s * HALF, HALF)], start=(k == 0), stop=(k == KC - 1))
                last.then_inc(y_done, 1)

            def tile_turn(t):
                pe.wait_ge(h2_ready, t + 1)
                pe.wait_ge(h2T_out, t)
                for k in range(KC):
                    last = nc.tensor.transpose(ps_h[:, k * P:(k + 1) * P], h2n[:, k * P:(k + 1) * P], ident[:])
                last.then_inc(h2_turned, 1)

            def scores(n, t, h):
                pe.wait_ge(h2T_out, t + 1)
                pe.wait_ge(sc_used, n)
                for k in range(KC):
                    last = nc.tensor.matmul(ps_sc[:, 0:2 * NK], h2T[:, k], Wk[:, k, bass.ds(h * 2 * NK, 2 * NK)], start=(k == 0), stop=(k == KC - 1))
                last.then_inc(sc_done, 1)

            def edge(start):
                for s in range(2):
                    last = nc.tensor.matmul(ps_acc[:, half(s)], zero[:], zero[:, 0:1].broadcast_to([P, HALF]), start=start, stop=not start, skip_group_check=True)
                return last

            def experts(G):
                for r in range(R):
                    pe.wait_ge(diag_out, R * (G + 1) + r + 1)
                    pe.wait_ge(v_in[r % VR], 16 * (R // VR * G + r // VR + 1))
                    for s in range(2):
                        last = nc.tensor.matmul(ps_acc[:, half(s)], diag[:, r % ND], vr[:, r % VR, half(s)], start=False, stop=False, skip_group_check=True)
                    last.then_inc(v_used, 1)

            def head(H):
                for s in range(GROUPS):
                    experts(GROUPS * H + s)

            pe.wait_ge(const, 3)
            def keys(g, wait=True):
                for s in range(2):
                    pe.wait_ge(wq_in[s], 32 * (g + 1))
                    if wait:
                        pe.wait_ge(wk_out, 2 * g + s - 1)
                    for k in range(KC):
                        last = nc.tensor.matmul(wk_banks[s][:, k * P:(k + 1) * P], vr[:, s, k * P:(k + 1) * P], vr[:, 2 + s, 0:NK], start=True, stop=True)
                    last.then_inc(wk_done, 1)

            keys(0, wait=False)
            for s in range(2):
                pe.wait_ge(wout_in[s], 16)
                tile_half(0, s)
            pe.wait_ge(wk_out, 2)
            tile_turn(0)
            scores(0, 0, 0)
            pe.wait_ge(h2T_out, 1)
            keys(1)
            pe.wait_ge(wk_out, 4)
            scores(1, 0, 1)
            with pe.Fori(2, PH) as g:
                keys(g)
            pe.wait_ge(wk_out, 2 * PH)
            with pe.Fori(0, TC - 1) as t:
                pe.wait_ge(acc_out, t)
                edge(True)
                with pe.Fori(0, 2) as h:
                    scores(PH * t + h + 2, t, h + 2)
                    tile_half(t + 1, h)
                    head(PH * t + h)
                with pe.Fori(2, PH - 2) as h:
                    scores(PH * t + h + 2, t, h + 2)
                    head(PH * t + h)
                tile_turn(t + 1)
                with pe.Fori(PH - 2, PH) as h:
                    scores(PH * t + h + 2, t + 1, h - (PH - 2))
                    head(PH * t + h)
                edge(False).then_inc(acc_done, 1)
            pe.wait_ge(acc_out, TC - 1)
            edge(True)
            with pe.Fori(0, PH - 2) as h:
                scores(PH * (TC - 1) + h + 2, TC - 1, h + 2)
                head(PH * (TC - 1) + h)
            for H in range(PH * TC - 2, PH * TC):
                head(H)
            edge(False).then_inc(acc_done, 1)

        @block.vector
        def _(dve):
            v = nc.vector
            step = Chain(dve, dve_step)
            g1, shift2, scale2, g2 = (mod[:, i * D:(i + 1) * D] for i in range(4))
            dve.wait_ge(small_in, 64)
            dve.wait_ge(const, 3)
            step(v.tensor_tensor(g1, g1, ur[:, 2], ALU.mult))
            step(v.scalar_tensor_tensor(scale2, scale2, 1.0, ur[:, 3], ALU.add, ALU.mult))
            v.tensor_tensor(g2, g2, ur[:, 4], ALU.mult).then_inc(mod_ready, 1)
            dve.wait_ge(mod_ready, 1)

            def tile_norms(t):
                dve.wait_ge(y_root, 2 * t + 1)
                v.reciprocal(rstd[:, 0:1], ss[:, 0:1]).then_inc(y_rstd, 1)
                dve.wait_ge(y_rstd, 2 * t + 1)
                dve.wait_ge(h2_copied, t)
                v.scalar_tensor_tensor(h2n[:], ps_y[:], rstd[:, 0:1], g1, ALU.mult, ALU.mult).then_inc(y_used, 1)
                dve.wait_ge(y_used, t + 1)
                dve.wait_ge(x_in, 16 * (t + 1))
                v.tensor_tensor(x2n[:], x2n[:], h2n[:], ALU.add).then_inc(x2_ready, 1)
                dve.wait_ge(x2_ready, t + 1)
                dve.wait_ge(y_root, 2 * t + 2)
                v.reciprocal(rstd[:, 1:2], ss[:, 1:2]).then_inc(y_rstd, 1)
                dve.wait_ge(y_rstd, 2 * t + 2)
                step(v.scalar_tensor_tensor(h2n[:], x2n[:], rstd[:, 1:2], scale2, ALU.mult, ALU.mult))
                v.tensor_tensor(h2n[:], h2n[:], shift2, ALU.add).then_inc(h2_ready, 1)

            SELECT_STEPS = 8 + 1 + 4 + 10

            def alone():
                dve.sem_inc(dve_go, 1)

            def top16(values, spare, out, index):
                for n in range(2):
                    o, i = out[:, 8 * n:8 * n + 8], index[:, 8 * n:8 * n + 8]
                    alone()
                    step(v.max(o, values))
                    alone()
                    if n == 0:
                        v.max_index(i, o, values)
                        step(v.match_replace(spare, o, values, NEG))
                        values = spare
                    else:
                        step(v.max_index(i, o, values))

            def select_sides(n):
                dve.wait_ge(sc_done, n + 1)
                for p in range(2):
                    top16(ps_sc[:, p * NK:(p + 1) * NK], sc2[:, p], top[:, p], topi[:, p])
                dve.sem_inc(sc_used, 1)

            def select_pairs(n):
                cand = eq[:, 0]
                step(v.tensor_tensor(cand, top[:, 0].unsqueeze(2).broadcast_to([P, TOPK, TOPK]), top[:, 1].unsqueeze(1).broadcast_to([P, TOPK, TOPK]), ALU.add))
                dve.wait_ge(ex_out, n)
                top16(cand.rearrange("p a b -> p (a b)"), eq[:, 1].rearrange("p a b -> p (a b)"), best, pos)
                v.tensor_scalar(negm[:], best[:, 0:1], -1.0, None, ALU.mult).then_inc(negm_ready, 1)
                step(v.tensor_scalar(ab[:, 0], pos[:], 4, None, ALU.logical_shift_right))
                step(v.tensor_scalar(ab[:, 1], pos[:], TOPK - 1, None, ALU.bitwise_and))
                step(v.tensor_copy(abf[:], ab[:]))
                step(v.tensor_copy(topf[:], topi[:]))
                for p in range(2):
                    last = v.tensor_tensor(eq[:, p], abf[:, p].unsqueeze(2).broadcast_to([P, TOPK, TOPK]), iota[:].unsqueeze(1).broadcast_to([P, TOPK, TOPK]), ALU.is_equal)
                step(last)
                for p in range(2):
                    last = v.tensor_tensor(eq[:, p], eq[:, p], topf[:, p].unsqueeze(1).broadcast_to([P, TOPK, TOPK]), ALU.mult)
                step(last)
                step(v.tensor_reduce(pick[:], eq[:], AX.X, ALU.add))
                step(v.scalar_tensor_tensor(idx[:, bass.ds(n % (2 * PH) * TOPK, TOPK)], pick[:, 0], float(NK), pick[:, 1], ALU.mult, ALU.add))
                dve.wait_ge(ex_out, n + 1)
                step(v.reciprocal(esum[:], esum[:]))
                step(v.tensor_scalar(gates[:, bass.ds(n % (2 * PH) * TOPK, TOPK)], ex[:], esum[:], 0.5, ALU.mult, ALU.mult))
                dve.sem_inc(sel_ready, 1)

            def experts(G, par):
                for r in range(R):
                    dve.wait_ge(u_in[r], 16 * (G + 1))
                    last = v.scalar_tensor_tensor(ur[:, r], ur[:, r], 1.0, h2c[:], ALU.mult, ALU.mult, accum_out=dots[:, r:r + 1])
                    last.then_inc(u_used, 1)
                dve.wait_ge(u_used, R * (G + 1))
                step(v.scalar_tensor_tensor(gel[:], dots[:], GELU_A, dots[:], ALU.mult, ALU.mult))
                v.scalar_tensor_tensor(gel[:], gel[:], 1.0, dots[:], ALU.add, ALU.mult).then_inc(gel_ready, 1)
                dve.wait_ge(tanh_out, G + 1)
                step(v.scalar_tensor_tensor(gel[:], gel[:], 1.0, dots[:], ALU.add, ALU.mult))
                dve.wait_ge(diag_out, R * G)
                v.tensor_tensor(coef[:, par], gel[:], gates[:, group_at(G)], ALU.mult).then_inc(coef_ready, 1)

            def finish(t):
                dve.wait_ge(f_root, 2 * t + 2)
                v.reciprocal(rstd[:, 2:3], ss[:, 2:3]).then_inc(f_rstd, 1)
                dve.wait_ge(f_rstd, t + 1)
                dve.wait_ge(acc_out, t + 1)
                step(v.scalar_tensor_tensor(yf[:], yf[:], rstd[:, 2:3], g2, ALU.mult, ALU.mult))
                v.tensor_tensor(yf[:], yf[:], x2c[:], ALU.add).then_inc(f_ready, 1)

            HEAD_STEPS = 2 * GROUPS + SELECT_STEPS

            def head(H):
                experts(GROUPS * H, 0)
                select_sides(H + 2)
                experts(GROUPS * H + 1, 1)
                select_pairs(H + 2)

            tile_norms(0)
            for n in range(2):
                select_sides(n)
                select_pairs(n)
            dve.wait_ge(h2_copied, 1)
            alone()
            with dve.Fori(0, TC - 1) as t:
                step.loop(t, PH * HEAD_STEPS + 2)
                for first, last in ((0, 2), (2, PH - 2), (PH - 2, PH)):
                    with dve.Fori(first, last) as h:
                        step.loop(h - first, HEAD_STEPS)
                        head(PH * t + h)
                    step.end(last - first)
                    if first == 0:
                        tile_norms(t + 1)
                finish(t)
                dve.wait_ge(h2_copied, t + 2)
                alone()
            step.end(TC - 1)
            with dve.Fori(0, PH - 2) as h:
                step.loop(h, HEAD_STEPS)
                head(PH * (TC - 1) + h)
            step.end(PH - 2)
            for H in range(PH * TC - 2, PH * TC):
                for s in range(GROUPS):
                    experts(GROUPS * H + s, s)
            finish(TC - 1)


def build(nc, a, out):
    with ExitStack() as ctx:
        merged_dram = nc.dram_tensor("merged_scratch", (P, KC, T), F32, kind="Internal").ap()
        mod_dram = nc.dram_tensor("mod_scratch", (P, 4 * D), F32, kind="Internal").ap()
        keep = {"ident": ctx.enter_context(nc.sbuf_tensor("ident", [P, P], F32)),
                "pool_go": ctx.enter_context(nc.semaphore("pool_go"))}
        with nc.sbuf_tensor("hh", [P, KC, T], F32R) as hh, nc.sbuf_tensor("hl", [P, KC, T], F32R) as hl:
            keep["hh"], keep["hl"] = hh, hl
            conditioning_and_lru(nc, ctx, keep, a, mod_dram, merged_dram)
            gated_linear_attention(nc, ctx, keep, a, merged_dram)
        peer_block(nc, ctx, keep, a, mod_dram, merged_dram, out)


def layout(inputs):
    import numpy as np
    g = {k: np.asarray(v) for k, v in inputs.items()}
    ch = lambda w: w.reshape(KC, P, -1).transpose(1, 0, 2)
    col = lambda w: np.ascontiguousarray(w.reshape(KC, P).T)
    a = {}
    a["x"] = g["x"].reshape(TC, P, D)
    a["cT"] = col(g["c"][0])
    a["gain1"] = col(g["norm_pre_mix"][0])
    a["w_ada"] = ch(g["w_ada"][0]).reshape(P, KC, 4 * MODS, 256).transpose(2, 0, 1, 3)
    a["b_ada"] = g["b_ada"][0].reshape(4 * MODS, 256)
    a["ident"] = np.eye(P, dtype=np.float32)
    w = ch(g["w_in"][0])
    off = np.cumsum([0, 512, 512, 1024, 1024, RANK, D, D, D, D])
    q, k, v, r, al, xl, xg, ga, gb = (w[:, :, off[i]:off[i + 1]] for i in range(9))
    blocks = lambda m: m.reshape(P, KC, -1, P).transpose(2, 0, 1, 3)
    again = lambda m: np.concatenate([m, m[-1:]])
    a["w_lru"] = again(np.stack([blocks(xl), blocks(xg), blocks(gb)], 1))
    par = np.stack([g["conv_w"][0][i] for i in range(4)] + [g["conv_b"][0], g["lru_b_a"][0].reshape(-1), g["lru_b_x"][0].reshape(-1), g["lru_lambda"][0]], -1)
    a["lru_par"] = par.reshape(KC, P, NPAR).transpose(1, 0, 2).reshape(P, KC * NPAR)
    a["lru_w"] = again(np.stack([g["lru_w_a"][0], g["lru_w_x"][0]], 2))
    pair = lambda m: blocks(m).reshape(HEADS, 2, P, KC, P)
    a["w_head"] = np.concatenate([blocks(q)[:, None], blocks(k)[:, None], pair(v), pair(r), pair(ga)], 1).reshape(-1, P, KC, P)
    a["w_al"] = al
    a["w_alpha"] = g["w_alpha"][0].reshape(RANK, HEADS, DK).transpose(1, 0, 2)
    a["head_par"] = np.concatenate([g["b_alpha"][0].reshape(HEADS, DK).T.reshape(P, HEADS, 1), g["gla_norm"][0].reshape(HEADS, 2, P).transpose(2, 0, 1)], 2).reshape(P, HEADS * 3)
    s, t = np.arange(P)[:, None], np.arange(P)[None, :]
    halvings = [((s // b == t // b) & (s % b < b // 2) & (t % b >= b // 2)) for b in (P >> n for n in range(LEVELS))] + [s == t]
    a["masks"] = np.concatenate(halvings, 1).astype(np.float32)
    a["w_out"] = ch(g["w_out"][0])
    a["gain_post_mix"] = g["norm_post_mix"]
    a["gain_pre_ffn"] = g["norm_pre_ffn"]
    a["gain_post_ffn"] = g["norm_post_ffn"]
    a["wqT"] = g["peer_w_query"][0].reshape(D, PH * 2, P).transpose(1, 2, 0)
    a["keysT"] = g["peer_sub_keys"][0].reshape(PH * 2, NK, P).transpose(0, 2, 1)
    a["u"] = g["peer_u"][0]
    a["v"] = g["peer_v"][0]
    return {k: np.ascontiguousarray(v) for k, v in a.items()}


def kernel(**inputs):
    import numpy as np
    import concourse.bacc as bacc
    from concourse.bass_utils import run_bass_kernel_spmd

    arrays = {f"in_{k}": v for k, v in layout(inputs).items()}
    nc = bacc.Bacc("TRN2", target_bir_lowering=False, num_devices=1)
    a = {k[3:]: nc.dram_tensor(k, v.shape, mybir.dt.from_np(v.dtype), kind="ExternalInput").ap() for k, v in arrays.items()}
    out = nc.dram_tensor("out_y", (TC, P, D), F32, kind="ExternalOutput").ap()
    build(nc, a, out)
    r = run_bass_kernel_spmd(nc, [arrays], core_ids=[0])
    return np.asarray(r.results[0]["out_y"]).reshape(1, T, D)
```

```python
from contextlib import ExitStack

import concourse.bass as bass
from concourse import mybir

F32 = mybir.dt.float32
F32R = mybir.dt.float32r
U32 = mybir.dt.uint32
ALU = mybir.AluOpType
ACT = mybir.ActivationFunctionType
AX = mybir.AxisListType

P = 128
D = 1024
T = 1024
KC = D // P
TC = T // P
HALF = 512
EPS = 1e-6
HEADS, DK, DV, RANK = 4, 128, 256, 16
TAU = 16.0
LEVELS = 7
NPAR = 8
SCAN_C = 8.0
GELU_A, GELU_B = 0.044715, 0.7978845608028654
MODS = 6
PH, NK, TOPK = 8, 128, 16
SLOTS = PH * TOPK
NEG = -3.0e38


class Chain:

    def __init__(self, eng, sem, base=0):
        self.eng, self.sem, self.base, self.n, self.outer = eng, sem, base, 0, []

    def __call__(self, ins):
        self.n += 1
        ins.then_inc(self.sem, 1)
        self.eng.wait_ge(self.sem, self.base + self.n)

    def loop(self, i, per):
        self.outer.append((self.base, self.n, per))
        self.base, self.n = self.base + self.n + i * per, 0

    def end(self, count):
        base, n, per = self.outer.pop()
        assert self.n == per, (self.n, per)
        self.base, self.n = base, n + count * per


def split_product(nc, out, wh, wl, xh, xl, first, last):
    nc.tensor.matmul(out, wh, xh, start=first, stop=False)
    nc.tensor.matmul(out, wh, xl, start=False, stop=False)
    return nc.tensor.matmul(out, wl, xh, start=False, stop=last)


def conditioning_and_lru(nc, ctx, keep, a, mod_dram, merged_dram):
    hh, hl, alow, ident = keep["hh"], keep["hl"], keep["alow"], keep["ident"]
    Q = 256
    CQ = Q // P
    MOD1 = 2 * D // Q
    with ExitStack() as scope:
        def sb(name, shape, dt=F32):
            return scope.enter_context(nc.sbuf_tensor(name, shape, dt))

        def sem(name):
            return ctx.enter_context(nc.semaphore(name))

        ps_xl, ps_xg, ps_gb, ps_gate = (scope.enter_context(nc.psum_tensor(n, [P, T], F32)) for n in ("ps_xl", "ps_xg", "ps_gb", "ps_gate"))
        ada_banks = (ps_gate[:, 0:Q], ps_gate[:, HALF:HALF + Q])

        ada = sb("ada", [P, 2, KC, Q])
        ada_bias = sb("ada_bias", [P, 2, Q])
        ada_sum = sb("ada_sum", [P, 2, Q])
        mod = sb("mod_tile", [P, 2, Q])
        ones = sb("ones1", [P, P])
        eps = sb("eps1", [P, 1])
        cT, cact, gain = sb("cT", [P, KC]), sb("cact", [P, KC]), sb("gain1", [P, KC])
        cols = sb("cols1", [P, 2 * KC])
        par, parj = sb("par", [P, KC * NPAR]), sb("parj", [P, NPAR])
        ptmp = sb("ptmp", [P, 5, KC])
        ss, rstd = sb("ss1", [P, 2]), sb("rstd1", [P, 2])
        xt = sb("xt", [P, 2, D])
        wt = sb("wt", [P, 3, KC, P])
        wh, wl = sb("wh1", [P, 3, KC, P], F32R), sb("wl1", [P, 3, KC, P], F32R)
        wgate = sb("wgate", [P, 2, P])
        w_al, w_alh, w_all = sb("w_al", [P, KC, RANK]), sb("w_alh", [P, KC, RANK], F32R), sb("w_all", [P, KC, RANK], F32R)
        lru = sb("lru", [P, T])
        c_wide = lru[:].rearrange("p (k c) -> p k c", k=KC)
        arena = sb("arena", [P, 11 * T + 3])
        raw = arena[:, 0:KC * T].rearrange("p (k t) -> p k t", k=KC)
        xn, junk = (arena[:, (KC + i) * T:(KC + i + 1) * T] for i in range(2))
        diag = arena[:, (KC + 2) * T:(KC + 2) * T + Q]
        xlp = arena[:, 0:T + 3]
        xc, xg, pin, tg, tb, tr, ti, av, th, mu = (arena[:, 3 + i * T:3 + (i + 1) * T] for i in range(1, 11))

        small_in, consts = sem("small_in"), sem("consts1")
        ada_in = [sem("ada_in0"), sem("ada_in1")]
        ada_ready = sem("ada_ready")
        ada_done = sem("ada_done")
        mod_out = sem("mod_out")
        mod_stored = [sem("mod_stored0"), sem("mod_stored1")]
        c_ready, par_abs = sem("c_ready"), sem("par_abs")
        act_out = sem("act_out")
        x_in = [sem("x_in0"), sem("x_in1")]
        x_sq, x_root, x_rstd, x_scaled, x_turned = (sem(n) for n in ("x_sq", "x_root", "x_rstd", "x_scaled", "x_turned"))
        raw_out = sem("raw_out")
        cols_ready, h_out, hi_out, lo_out = sem("cols_ready"), sem("h_out"), sem("hi_out"), sem("lo_out")
        w_in = [sem(f"w_in{i}") for i in range(3)]
        w_hi, w_split = sem("w_hi"), sem("w_split")
        wg_in = sem("wg_in")
        al_in, al_split, al_done = sem("al_in"), sem("al_split"), sem("al_done")
        projected = [sem("p_xl"), sem("p_xg"), sem("p_gb")]
        p_gr, p_gi = sem("p_gr"), sem("p_gi")
        xl_out, xg_out, tb_out, tr_out, ti_out = (sem(n) for n in ("xl_out", "xg_out", "tb_out", "tr_out", "ti_out"))
        xc_ready, pin_ready, nla_ready, parj_ready = sem("xc_ready"), sem("pin_ready"), sem("nla_ready"), sem("parj_ready")
        tg_out, a_out, th_out = sem("tg_out"), sem("a_out"), sem("th_out")
        mu2_ready, mu_root = sem("mu2_ready"), sem("mu_root")
        lru_out, lru_stored = sem("lru_out"), sem("lru_stored")
        dve_step, pool_go = sem("dve_step1"), keep["go"]

        block = scope.enter_context(nc.Block())

        @block.sync
        def _(sp):
            def load_ada(m, s):
                sp.dma_start(ada[:, s], a["w_ada"][bass.ds(m, 1)].rearrange("o p k c -> p (o k) c")).then_inc(ada_in[s], 16)
                sp.dma_start(ada_bias[:, s], a["b_ada"][bass.ds(m, 1), :].broadcast_to([P, Q])).then_inc(ada_in[s], 16)

            sp.dma_start(cT[:], a["cT"]).then_inc(small_in, 16)
            sp.dma_start(gain[:], a["gain1"]).then_inc(small_in, 16)
            sp.dma_start(par[:], a["lru_par"]).then_inc(small_in, 16)
            sp.dma_start(ident[:], a["ident"]).then_inc(small_in, 16)
            for s in range(2):
                load_ada(s, s)
            with sp.Fori(1, MOD1 // 2) as g:
                for s in range(2):
                    sp.wait_ge(mod_out, 2 * g + s - 1)
                    load_ada(2 * g + s, s)
            for i in range(3):
                sp.dma_start(wt[:, i], a["w_lru"][0, i]).then_inc(w_in[i], 16)
            sp.dma_start(wgate[:], a["lru_w"][0]).then_inc(wg_in, 16)
            sp.dma_start(w_al[:], a["w_al"]).then_inc(al_in, 16)
            with sp.Fori(0, KC) as j:
                for s in range(2):
                    sp.wait_ge(mod_out, MOD1 + 2 * j + s - 1)
                    load_ada(MOD1 + 2 * j + s, s)
                for i in range(3):
                    sp.wait_ge(w_split, 3 * j + i + 1)
                    sp.dma_start(wt[:, i], a["w_lru"][bass.ds(j + 1, 1), i].rearrange("o p k c -> p (o k) c")).then_inc(w_in[i], 16)
                sp.wait_ge(p_gi, j + 1)
                sp.dma_start(wgate[:], a["lru_w"][bass.ds(j + 1, 1)].rearrange("o p g c -> p (o g) c")).then_inc(wg_in, 16)
            for i in range(3):
                sp.wait_ge(w_in[i], 16 * (KC + 1))
            sp.wait_ge(wg_in, 16 * (KC + 1))

        @block.gpsimd
        def _(pool):
            g = nc.gpsimd
            g.memset(ones[:], 1.0).then_inc(consts, 1)
            g.memset(eps[:], EPS).then_inc(consts, 1)
            for s in range(2):
                pool.dma_start(xt[:, s], a["x"][s]).then_inc(x_in[s], 16)
            with pool.Fori(1, TC // 2) as q:
                for s in range(2):
                    pool.wait_ge(x_scaled, 2 * q + s - 1)
                    pool.sem_inc(pool_go, 1)
                    pool.dma_start(xt[:, s], a["x"][bass.ds(2 * q + s, 1)].rearrange("o p d -> (o p) d")).then_inc(x_in[s], 16)

            def split(i, j):
                pool.wait_ge(w_in[i], 16 * (j + 1))
                pool.wait_ge(projected[i], j)
                pool.sem_inc(pool_go, 1)
                g.tensor_copy(wh[:, i], wt[:, i]).then_inc(w_hi, 1)
                pool.wait_ge(w_hi, 3 * j + i + 1)
                g.tensor_tensor(wl[:, i], wt[:, i], wh[:, i], ALU.subtract).then_inc(w_split, 1)

            for i in range(3):
                split(i, 0)
            pool.wait_ge(al_in, 16)
            g.tensor_copy(w_alh[:], w_al[:]).then_inc(al_split, 1)
            pool.wait_ge(al_split, 1)
            g.tensor_tensor(w_all[:], w_al[:], w_alh[:], ALU.subtract).then_inc(al_split, 1)
            with pool.Fori(0, KC) as j:
                for i in range(3):
                    if i == 2:
                        for s in range(2):
                            pool.wait_ge(mod_out, MOD1 + 2 * j + s + 1)
                            pool.sem_inc(pool_go, 1)
                            pool.dma_start(mod_dram[:, bass.ds((2 * j + s) * Q, Q)], mod[:, s]).then_inc(mod_stored[s], 16)
                    split(i, j + 1)
                pool.wait_ge(lru_out, j + 1)
                pool.sem_inc(pool_go, 1)
                pool.dma_start(merged_dram[:, bass.ds(j, 1), :].rearrange("p o t -> p (o t)"), lru[:]).then_inc(lru_stored, 16)
            for s in range(2):
                pool.wait_ge(mod_stored[s], 16 * KC)
            pool.wait_ge(lru_stored, 16 * KC)

        @block.scalar
        def _(act):
            S = nc.scalar
            act.wait_ge(small_in, 64)
            S.activation(cact[:], cT[:], ACT.Tanh, scale=0.5).then_inc(act_out, 1)
            act.wait_ge(par_abs, 1)
            S.activation(ptmp[:, 1], ptmp[:, 0], ACT.Exp, scale=-1.0).then_inc(act_out, 1)
            act.wait_ge(consts, 2)

            def turned(c, s):
                act.wait_ge(x_turned, c + 1)
                S.activation(raw[:, :, bass.ds(c * P, P)], (ps_xl, ps_xg)[s][:].rearrange("p (k t) -> p k t", k=KC), ACT.Copy).then_inc(raw_out, 1)

            def norm_tiles(q, first):
                for s in range(2):
                    c = 2 * q + s
                    act.wait_ge(x_in[s], 16 * (q + 1))
                    act.wait_ge(x_sq, c)
                    act.wait_ge(x_rstd, c)
                    S.activation(junk, xt[:, s], ACT.Square, scale=D ** -0.5, accum_out=ss[:, s:s + 1]).then_inc(x_sq, 1)
                    act.wait_ge(x_sq, c + 1)
                    S.activation(ss[:, s:s + 1], ss[:, s:s + 1], ACT.Sqrt, bias=eps[:]).then_inc(x_root, 1)
                    if not (first and s == 0):
                        turned(c - 1, 1 - s)
                    act.wait_ge(x_rstd, c + 1)
                    S.activation(xn, xt[:, s], ACT.Copy, scale=rstd[:, s:s + 1]).then_inc(x_scaled, 1)

            norm_tiles(0, True)
            with act.Fori(1, TC // 2) as q:
                norm_tiles(q, False)
            turned(TC - 1, 1)
            act.wait_ge(cols_ready, 1)
            act.wait_ge(raw_out, TC)
            for k in range(KC):
                S.activation(hh[:, k], raw[:, k], ACT.Identity, scale=cols[:, KC + k:KC + k + 1], bias=cols[:, k:k + 1]).then_inc(hi_out, 1)
            act.wait_ge(consts, 3)
            act.wait_ge(lo_out, KC)
            with act.Fori(0, KC) as j:
                act.wait_ge(projected[0], j + 1)
                act.wait_ge(xc_ready, j)
                S.activation(xlp[:, 3:3 + T], ps_xl[:], ACT.Copy).then_inc(xl_out, 1)
                act.wait_ge(projected[1], j + 1)
                act.wait_ge(lru_out, j)
                S.activation(xg, ps_xg[:], ACT.Copy).then_inc(xg_out, 1)
                act.wait_ge(pin_ready, j + 1)
                S.activation(tg, pin, ACT.Tanh, scale=GELU_B).then_inc(tg_out, 1)
                act.wait_ge(projected[2], j + 1)
                S.activation(tb, ps_gb[:], ACT.Tanh, scale=0.5).then_inc(tb_out, 1)
                act.wait_ge(p_gr, j + 1)
                act.wait_ge(parj_ready, j + 1)
                S.activation(tr, ps_gate[:], ACT.Tanh, scale=0.5, bias=parj[:, 5:6]).then_inc(tr_out, 1)
                act.wait_ge(p_gi, j + 1)
                S.activation(ti, ps_xl[:], ACT.Tanh, scale=0.5, bias=parj[:, 6:7]).then_inc(ti_out, 1)
                act.wait_ge(nla_ready, j + 1)
                S.activation(av, tr, ACT.Exp, scale=-1.0).then_inc(a_out, 1)
                S.activation(th, tr, ACT.Tanh).then_inc(th_out, 1)
                act.wait_ge(mu2_ready, j + 1)
                S.activation(mu, mu, ACT.Sqrt).then_inc(mu_root, 1)
            act.wait_ge(al_done, 1)
            S.activation(alow[:], ps_gb[0:RANK, :], ACT.Copy)

        @block.tensor
        def _(pe):
            def ada_products(q, s):
                pe.wait_ge(ada_in[s], 32 * (q + 1))
                for k in range(KC):
                    last = nc.tensor.matmul(ada_banks[s], c_wide[:, k], ada[:, s, k], start=(k == 0), stop=(k == KC - 1))
                last.then_inc(ada_done, 1)

            def ada_columns(n, s):
                pe.wait_ge(ada_ready, n + 1)
                nc.tensor.matmul(ada_banks[s], ones[:], ada_sum[:, s], start=True, stop=True).then_inc(ada_done, 1)

            pe.wait_ge(consts, 1)
            pe.wait_ge(small_in, 64)
            pe.wait_ge(c_ready, 1)
            with pe.Fori(0, TC // 2) as q:
                for s in range(2):
                    c = 2 * q + s
                    pe.wait_ge(mod_out, c)
                    ada_products(q, s)
                    pe.wait_ge(x_scaled, c + 1)
                    pe.wait_ge(raw_out, c)
                    for k in range(KC):
                        last = nc.tensor.transpose((ps_xl, ps_xg)[s][:, k * P:(k + 1) * P], xn[:, k * P:(k + 1) * P], ident[:])
                    last.then_inc(x_turned, 1)
            pe.wait_ge(raw_out, TC)

            def project(ps, i, j, free, first=False):
                pe.wait_ge(w_split, 3 * j + i + 1)
                if not first:
                    pe.wait_ge(free, j)
                order = [(k, s) for k in range(KC) for s in range(2)] if first else [(k, s) for s in range(2) for k in range(KC)]
                for k, s in order:
                    cs = slice(s * HALF, (s + 1) * HALF)
                    if first and s == 0:
                        pe.wait_ge(lo_out, k + 1)
                    last = split_product(nc, ps[:, cs], wh[:, i, k], wl[:, i, k], hh[:, k, cs], hl[:, k, cs], k == 0, k == KC - 1)
                last.then_inc(projected[i], 1)

            def lru_block(j, more):
                project(ps_xg, 1, j, xg_out)
                pe.wait_ge(tr_out, j)
                pe.wait_ge(mod_out, MOD1 + 2 * j)
                for s in range(2):
                    ada_columns(2 * j + s, s)
                project(ps_gb, 2, j, tb_out)
                pe.wait_ge(wg_in, 16 * (j + 1))
                pe.wait_ge(xc_ready, j + 1)
                pe.wait_ge(mod_out, MOD1 + 2 * j + 2)
                for s in range(T // HALF):
                    last = nc.tensor.matmul(ps_gate[:, s * HALF:(s + 1) * HALF], wgate[:, 0], xc[:, s * HALF:(s + 1) * HALF], start=True, stop=True)
                last.then_inc(p_gr, 1)
                pe.wait_ge(xl_out, j + 1)
                for s in range(T // HALF):
                    last = nc.tensor.matmul(ps_xl[:, s * HALF:(s + 1) * HALF], wgate[:, 1], xc[:, s * HALF:(s + 1) * HALF], start=True, stop=True)
                last.then_inc(p_gi, 1)
                if more:
                    project(ps_xl, 0, j + 1, ti_out)

            project(ps_xl, 0, 0, None, first=True)
            with pe.Fori(0, KC - 1) as j:
                lru_block(j, True)
            lru_block(KC - 1, False)
            pe.wait_ge(al_split, 2)
            pe.wait_ge(tb_out, KC)
            for s in range(T // HALF):
                cs = slice(s * HALF, (s + 1) * HALF)
                for k in range(KC):
                    last = split_product(nc, ps_gb[0:RANK, cs], w_alh[:, k], w_all[:, k], hh[:, k, cs], hl[:, k, cs], k == 0, k == KC - 1)
            last.then_inc(al_done, 1)

        @block.vector
        def _(dve):
            v = nc.vector
            step = Chain(dve, dve_step)
            SUMS = KC - 1

            def ada_sums(m, s, count, done):
                dve.wait_ge(ada_in[s], count)
                dve.wait_ge(ada_done, done)
                step(v.tensor_scalar(ada_sum[:, s], ada[:, s, 0], cact[:, 0:1], None, ALU.mult))
                for k in range(1, KC - 1):
                    step(v.scalar_tensor_tensor(ada_sum[:, s], ada[:, s, k], cact[:, k:k + 1], ada_sum[:, s], ALU.mult, ALU.add))
                v.scalar_tensor_tensor(ada_sum[:, s], ada[:, s, KC - 1], cact[:, KC - 1:KC], ada_sum[:, s], ALU.mult, ALU.add).then_inc(ada_ready, 1)

            def mod_tile(m, s):
                dve.wait_ge(ada_done, m + 1)
                v.tensor_tensor(mod[:, s], ada_banks[s], ada_bias[:, s], ALU.add).then_inc(mod_out, 1)
                dve.wait_ge(mod_out, m + 1)

            dve.wait_ge(small_in, 64)
            lam = par[:].rearrange("p (j q) -> p j q", q=NPAR)[:, :, 7]
            v.scalar_tensor_tensor(ptmp[:, 0], lam, -1.0, lam, ALU.mult, ALU.max).then_inc(par_abs, 1)
            dve.wait_ge(act_out, 1)
            step(v.tensor_scalar(cact[:], cact[:], 1.0, 0.5, ALU.add, ALU.mult))
            step(v.tensor_tensor(cact[:], cact[:], cT[:], ALU.mult))
            v.tensor_copy(c_wide, cact[:].unsqueeze(2).broadcast_to([P, KC, P])).then_inc(c_ready, 1)
            with dve.Fori(0, MOD1 // 2) as q:
                step.loop(q, 2 * 2)
                for s in range(2):
                    m = 2 * q + s
                    dve.wait_ge(x_root, m + 1)
                    v.reciprocal(rstd[:, s:s + 1], ss[:, s:s + 1]).then_inc(x_rstd, 1)
                    mod_tile(m, s)
                    step(v.tensor_tensor(diag.rearrange("p (k c) -> p k c", k=CQ), mod[:, s].rearrange("p (k c) -> p k c", k=CQ),
                                         ident[:].unsqueeze(1).broadcast_to([P, CQ, P]), ALU.mult))
                    step(v.tensor_reduce(cols[:, bass.ds(m * CQ, CQ)], diag.rearrange("p (k c) -> p k c", k=CQ), AX.X, ALU.add))
            step.end(MOD1 // 2)
            v.scalar_tensor_tensor(cols[:, KC:], cols[:, KC:], 1.0, gain[:], ALU.add, ALU.mult).then_inc(cols_ready, 1)
            dve.wait_ge(cols_ready, 1)
            for k in range(KC):
                dve.wait_ge(hi_out, k + 1)
                v.tensor_scalar(raw[:, k], raw[:, k], cols[:, KC + k:KC + k + 1], cols[:, k:k + 1], ALU.mult, ALU.add).then_inc(h_out, 1)
                dve.wait_ge(h_out, k + 1)
                v.tensor_tensor(hl[:, k], raw[:, k], hh[:, k], ALU.subtract).then_inc(lo_out, 1)
            dve.wait_ge(act_out, 2)
            step(v.tensor_scalar(ptmp[:, 2], ptmp[:, 1], 2.0, None, ALU.add))
            step(v.reciprocal(ptmp[:, 3], ptmp[:, 2]))
            step(v.tensor_tensor(ptmp[:, 2], ptmp[:, 1], ptmp[:, 3], ALU.mult))
            step(v.tensor_tensor(ptmp[:, 3], ptmp[:, 2], ptmp[:, 2], ALU.mult))
            step(v.tensor_scalar(ptmp[:, 4], ptmp[:, 3], 1.0 / 17, None, ALU.mult))
            for m in (15, 13, 11, 9, 7, 5, 3):
                step(v.scalar_tensor_tensor(ptmp[:, 4], ptmp[:, 4], 1.0 / m, ptmp[:, 3], ALU.add, ALU.mult))
            step(v.scalar_tensor_tensor(ptmp[:, 4], ptmp[:, 4], 1.0, ptmp[:, 2], ALU.add, ALU.mult))
            step(v.tensor_scalar(ptmp[:, 0], lam, -0.5 * SCAN_C, 0.0, ALU.mult, ALU.max))
            step(v.scalar_tensor_tensor(lam, ptmp[:, 4], SCAN_C, ptmp[:, 0], ALU.mult, ALU.add))
            halves = par[:].rearrange("p (j q) -> p j q", q=NPAR)[:, :, 5:7]
            step(v.tensor_scalar(halves, halves, 0.5, None, ALU.mult))
            dve.wait_ge(lo_out, KC)
            v.memset(xlp[:, 0:3], 0.0).then_inc(consts, 1)
            with dve.Fori(0, KC) as j:
                step.loop(j, 2 * SUMS + 3 + 1 + 4 + 3)
                for s in range(2):
                    ada_sums(MOD1 + 2 * j + s, s, 32 * (MOD1 // 2 + j + 1), MOD1 + 2 * j)
                v.tensor_copy(parj[:], par[:, bass.ds(j * NPAR, NPAR)]).then_inc(parj_ready, 1)
                dve.wait_ge(xl_out, j + 1)
                dve.wait_ge(parj_ready, j + 1)
                step(v.tensor_scalar(xc, xlp[:, 3:3 + T], parj[:, 3:4], parj[:, 4:5], ALU.mult, ALU.add))
                step(v.scalar_tensor_tensor(xc, xlp[:, 2:2 + T], parj[:, 2:3], xc, ALU.mult, ALU.add))
                step(v.scalar_tensor_tensor(xc, xlp[:, 1:1 + T], parj[:, 1:2], xc, ALU.mult, ALU.add))
                v.scalar_tensor_tensor(xc, xlp[:, 0:T], parj[:, 0:1], xc, ALU.mult, ALU.add).then_inc(xc_ready, 1)
                dve.wait_ge(xg_out, j + 1)
                step(v.scalar_tensor_tensor(pin, xg, GELU_A, xg, ALU.mult, ALU.mult))
                v.scalar_tensor_tensor(pin, pin, 1.0, xg, ALU.add, ALU.mult).then_inc(pin_ready, 1)
                for s in range(2):
                    dve.wait_ge(mod_stored[s], 16 * j)
                    mod_tile(MOD1 + 2 * j + s, s)
                dve.wait_ge(tr_out, j + 1)
                v.tensor_scalar(tr, tr, 1.0, parj[:, 7:8], ALU.add, ALU.mult).then_inc(nla_ready, 1)
                dve.wait_ge(a_out, j + 1)
                step(v.tensor_tensor(mu, av, av, ALU.mult))
                dve.wait_ge(th_out, j + 1)
                v.scalar_tensor_tensor(mu, mu, 1.0, th, ALU.add, ALU.mult).then_inc(mu2_ready, 1)
                dve.wait_ge(ti_out, j + 1)
                step(v.scalar_tensor_tensor(ti, ti, 1.0, xc, ALU.add, ALU.mult))
                dve.wait_ge(tg_out, j + 1)
                step(v.scalar_tensor_tensor(tg, tg, 1.0, xg, ALU.add, ALU.mult))
                dve.wait_ge(tb_out, j + 1)
                step(v.scalar_tensor_tensor(tg, tb, 1.0, tg, ALU.add, ALU.mult))
                dve.wait_ge(mu_root, j + 1)
                step(v.scalar_tensor_tensor(mu, ti, 0.5, mu, ALU.mult, ALU.mult))
                step(v.tensor_tensor_scan(th, av, mu, 0.0, ALU.mult, ALU.add))
                dve.wait_ge(lru_stored, 16 * j)
                step(v.scalar_tensor_tensor(lru[:], th, 0.25, tg, ALU.mult, ALU.mult))
                dve.sem_inc(lru_out, 1)
            step.end(KC)


def gated_linear_attention(nc, ctx, keep, a, merged_dram):
    hh, hl, alow, ident = keep["hh"], keep["hl"], keep["alow"], keep["ident"]
    TILES = 8
    NL = LEVELS + 1
    with ExitStack() as scope:
        def sb(name, shape, dt=F32):
            return scope.enter_context(nc.sbuf_tensor(name, shape, dt))

        def sem(name):
            return ctx.enter_context(nc.semaphore(name))

        ps_a = scope.enter_context(nc.psum_tensor("ps_a", [P, T], F32))
        ps_b = scope.enter_context(nc.psum_tensor("ps_b", [P, T], F32))
        ps_s = scope.enter_context(nc.psum_tensor("ps_s", [P, NL * P], F32))
        ps_o = scope.enter_context(nc.psum_tensor("ps_o", [P, HALF], F32))
        ps_t = scope.enter_context(nc.psum_tensor("ps_t", [P, HALF], F32))
        o_banks = (ps_a[:, 0:DV], ps_a[:, HALF:HALF + DV])

        masks = sb("masks", [P, NL * P])
        ones = sb("ones2", [P, P])
        eps = sb("eps2", [P, 1])
        hpar = sb("hpar", [P, HEADS * 3])
        hp = sb("hp", [P, 3])
        w_alpha = sb("w_alpha", [RANK, DK])
        wt = sb("wt2", [P, 2, KC, P])
        wh, wl = sb("wh2", [P, 4, KC, P], F32R), sb("wl2", [P, 4, KC, P], F32R)
        q = sb("q", [P, T])
        k = sb("k", [P, T])
        V = sb("V", [P, TC, DV])
        oT = sb("oT", [P, 2, T])
        zl, cum = oT[:, 0], oT[:, 1]
        X = sb("X", [P, LEVELS, T])
        qe = sb("qe", [P, T])
        kd = sb("kd", [P, T])
        elast = sb("elast", [P, TC])
        gate = sb("gate", [P, 2, T])
        tnh = sb("tnh", [P, 2, HALF])
        sm = sb("sm", [P, NL * P])
        S = sb("S", [P, 2, P])
        kdT = sb("kdT", [P, TC, DK])
        state = sb("state", [P, DV])
        junk = sb("junk2", [P, DV])
        ss = sb("ss2", [P, TC])
        rstd = sb("rstd2", [P, TC])
        on = sb("on", [P, 2, DV])
        mix = sb("mix", [P, 2, T])

        small_in, const = sem("small_in2"), sem("consts2")
        wal_in = sem("walpha_in")
        wt_in = [sem("wt_in0"), sem("wt_in1")]
        w_hi, w_split = sem("gla_w_hi"), sem("gla_w_split")
        mix_in = sem("mix_in")
        z_done, q_done, k_done, v_done = sem("z_done"), sem("q_done"), sem("k_done"), sem("v_done")
        rg_done = sem("rg_done")
        hp_ready = sem("hp_ready")
        z_abs, z_min, l_out = sem("z_abs"), sem("z_min"), sem("l_out")
        q_out, k_out, v_out = sem("q_out"), sem("k_out"), sem("v_out")
        diff_ready = sem("diff_ready")
        exp_out = sem("exp_out")
        x_ready = sem("x_ready")
        r_raw, rg_out, pool_go = sem("r_raw"), sem("rg_out"), keep["go"]
        gate_step = sem("gate_step")
        s_done, s_masked, s_ready = sem("s_done"), sem("s_masked"), sem("s_ready")
        kt_done, kt_out = sem("kt_done"), sem("kt_out")
        o_done, up_done, state_out = sem("o_done"), sem("up_done"), sem("state_out")
        o_sq, o_root, o_rstd, on_out = sem("o_sq"), sem("o_root"), sem("o_rstd"), sem("on_out")
        ot_done, ot_out = sem("ot_done"), sem("ot_out")
        head_out, merged_out = sem("head_out"), sem("merged_out")
        dve_step = sem("dve_step2")

        block = scope.enter_context(nc.Block())

        @block.sync
        def _(sp):

            def load_tile(n, s):
                sp.dma_start(wt[:, s], a["w_head"][bass.ds(n, 1)].rearrange("o p k c -> p (o k) c")).then_inc(wt_in[s], 16)

            def mix_at(h):
                return merged_dram[:, bass.ds(2 * h, 2), :]

            sp.dma_start(w_alpha[:], a["w_alpha"][0]).then_inc(wal_in, 16)
            for s in range(2):
                load_tile(s, s)
            sp.dma_start(hpar[:], a["head_par"]).then_inc(small_in, 16)
            sp.dma_start(masks[:], a["masks"]).then_inc(small_in, 16)
            sp.dma_start(mix[:], mix_at(0)).then_inc(mix_in, 16)

            def tiles(h, first, behind):
                for i in range(first, behind):
                    sp.wait_ge(w_split, TILES * h + i - 1)
                    load_tile(TILES * h + i, i % 2)

            tiles(0, 2, 4)

            def head(h, last):
                tiles(h, 4, TILES)
                if not last:
                    sp.wait_ge(z_done, h + 1)
                    sp.dma_start(w_alpha[:], a["w_alpha"][bass.ds(h + 1, 1)].rearrange("o r c -> (o r) c")).then_inc(wal_in, 16)
                    tiles(h, TILES, TILES + 4)
                sp.wait_ge(head_out, h + 1)
                sp.dma_start(mix_at(h), mix[:]).then_inc(merged_out, 16)
                sp.wait_ge(merged_out, 16 * (h + 1))
                if not last:
                    sp.dma_start(mix[:], mix_at(h + 1)).then_inc(mix_in, 16)

            with sp.Fori(0, HEADS - 1) as h:
                head(h, False)
            head(HEADS - 1, True)

        @block.gpsimd
        def _(pool):
            nc.gpsimd.memset(eps[:], EPS).then_inc(const, 1)
            g = nc.gpsimd
            g.memset(ones[:], 1.0).then_inc(const, 1)
            def split(h, i):
                n = TILES * h + i
                pool.wait_ge(wt_in[i % 2], 16 * (TILES // 2 * h + i // 2 + 1))
                pool.sem_inc(pool_go, 1)
                g.tensor_copy(wh[:, i % 4], wt[:, i % 2]).then_inc(w_hi, 1)
                pool.wait_ge(w_hi, n + 1)
                g.tensor_tensor(wl[:, i % 4], wt[:, i % 2], wh[:, i % 4], ALU.subtract).then_inc(w_split, 1)

            def gate_tiles(h):
                for i, (used, count) in enumerate(((q_done, 1), (k_done, 1), (v_done, 2), (v_done, 2))):
                    pool.wait_ge(used, count * (h + 1))
                    split(h, 4 + i)

            for i in range(4):
                split(0, i)
            with pool.Fori(0, HEADS - 1) as h:
                gate_tiles(h)
                for i in range(4):
                    pool.wait_ge(rg_done, TC * h + 2 * (i + 1))
                    split(h + 1, i)
            gate_tiles(HEADS - 1)

        @block.scalar
        def _(act):
            act.wait_ge(const, 1)
            with act.Fori(0, HEADS) as h:
                act.wait_ge(z_done, h + 1)
                act.wait_ge(hp_ready, h + 1)
                act.wait_ge(head_out, h)
                nc.scalar.activation(zl, ps_a[:], ACT.Abs, bias=hp[:, 0:1]).then_inc(z_abs, 1)
                act.wait_ge(z_abs, 2 * h + 1)
                nc.scalar.activation(zl, zl, ACT.Exp, scale=-1.0).then_inc(z_abs, 1)
                act.wait_ge(z_abs, 2 * h + 2)
                nc.scalar.activation(zl, zl, ACT.Ln, bias=1.0).then_inc(l_out, 1)
                act.wait_ge(q_done, h + 1)
                act.wait_ge(s_done, TC * h)
                nc.scalar.activation(q[:], ps_b[:], ACT.Copy, scale=DK ** -0.5).then_inc(q_out, 1)
                act.wait_ge(k_done, h + 1)
                nc.scalar.activation(k[:], ps_a[:], ACT.Copy).then_inc(k_out, 1)
                for n in range(LEVELS):
                    half = P >> (n + 1)
                    pairs = X[:, n].rearrange("p (b w t) -> p b w t", w=2, t=half)
                    act.wait_ge(diff_ready, NL * h + n + 1)
                    nc.scalar.activation(pairs[:, :, 0], pairs[:, :, 0], ACT.Exp, scale=-1.0 / TAU)
                    nc.scalar.activation(pairs[:, :, 1], pairs[:, :, 1], ACT.Exp, scale=1.0 / TAU).then_inc(exp_out, 1)
                act.wait_ge(diff_ready, NL * h + NL)
                nc.scalar.activation(kd[:], kd[:], ACT.Exp, scale=-1.0 / TAU).then_inc(exp_out, 1)
                nc.scalar.activation(qe[:], cum, ACT.Exp, scale=1.0 / TAU).then_inc(exp_out, 1)
                nc.scalar.activation(elast[:], cum.rearrange("p (c t) -> p c t", t=P)[:, :, P - 1], ACT.Exp, scale=1.0 / TAU).then_inc(exp_out, 1)
                act.wait_ge(up_done, TC * h)
                for i, bank in enumerate((ps_b, ps_a)):
                    act.wait_ge(v_done, 2 * h + i + 1)
                    nc.scalar.activation(V[:, i * 4:(i + 1) * 4].rearrange("p c d -> p (c d)"), bank[:], ACT.Copy).then_inc(v_out, 1)
                def gate_half(u):
                    i, s = u // 2, u % 2
                    bank = ps_b[:, s * HALF:(s + 1) * HALF]
                    act.wait_ge(rg_done, TC * h + u + 1)
                    if i < 2:
                        nc.scalar.activation(gate[:, i, s * HALF:(s + 1) * HALF], bank, ACT.Copy).then_inc(r_raw, 1)
                    if u >= 2:
                        act.wait_ge(gate_step, TC * h + u - 1)
                    nc.scalar.activation(tnh[:, s], bank, ACT.Tanh, scale=0.5).then_inc(rg_out, 1)

                for i, bank in enumerate((ps_t, ps_o)):
                    act.wait_ge(kt_done, 2 * h + i + 1)
                    nc.scalar.activation(kdT[:, 4 * i:4 * i + 4].rearrange("p c d -> p (c d)"), bank[:], ACT.Copy).then_inc(kt_out, 1)

                def turned_out(c):
                    act.wait_ge(ot_done, TC * h + c + 1)
                    nc.scalar.activation(oT[:, :, c * P:(c + 1) * P], ps_t[:, 0:2 * P].rearrange("p (v t) -> p v t", v=2), ACT.Copy).then_inc(ot_out, 1)

                for c in range(TC):
                    if c < TC - 1:
                        gate_half(c)
                    n = TC * h + c
                    o = o_banks[c % 2]
                    act.wait_ge(o_done, n + 1)
                    nc.scalar.activation(junk[:], o, ACT.Square, scale=DV ** -0.5, accum_out=ss[:, c:c + 1]).then_inc(o_sq, 1)
                    act.wait_ge(o_sq, n + 1)
                    nc.scalar.activation(ss[:, c:c + 1], ss[:, c:c + 1], ACT.Sqrt, bias=eps[:]).then_inc(o_root, 1)
                    act.wait_ge(o_rstd, n + 1)
                    if c >= 2:
                        act.wait_ge(ot_done, n - 1)
                    nc.scalar.activation(on[:, c % 2], o, ACT.Copy, scale=rstd[:, c:c + 1]).then_inc(on_out, 1)
                    if c == TC - 1:
                        gate_half(c)
                    if c >= 1:
                        turned_out(c - 1)
                turned_out(TC - 1)

        @block.tensor
        def _(pe):
            def project(out, w_h, w_l, halves=range(T // HALF), chunks=range(KC)):
                for s in halves:
                    cs = slice(s * HALF, (s + 1) * HALF)
                    for kk in chunks:
                        last = split_product(nc, out[:, cs], w_h[:, kk], w_l[:, kk], hh[:, kk, cs], hl[:, kk, cs], kk == 0, kk == KC - 1)
                return last

            with pe.Fori(0, HEADS) as h:
                pe.wait_ge(wal_in, 16 * (h + 1))
                pe.wait_ge(on_out, TC * h)
                pe.wait_ge(state_out, TC * h)
                pe.wait_ge(s_masked, TC * h)
                for s in range(T // HALF):
                    last = nc.tensor.matmul(ps_a[:, s * HALF:(s + 1) * HALF], w_alpha[:], alow[:, s * HALF:(s + 1) * HALF], start=True, stop=True)
                last.then_inc(z_done, 1)
                pe.wait_ge(w_split, TILES * h + 1)
                project(ps_b, wh[:, 0], wl[:, 0]).then_inc(q_done, 1)
                pe.wait_ge(z_abs, 2 * h + 1)
                pe.wait_ge(z_min, h + 1)
                pe.wait_ge(w_split, TILES * h + 2)
                project(ps_a, wh[:, 1], wl[:, 1]).then_inc(k_done, 1)
                pe.wait_ge(w_split, TILES * h + 4)
                for i, (bank, free) in enumerate(((ps_b, q_out), (ps_a, k_out))):
                    pe.wait_ge(free, h + 1)
                    for c in range(4 * i, 4 * i + 4):
                        ct = slice(c * P, (c + 1) * P)
                        for kk in range(KC):
                            last = split_product(nc, bank[:, (c % 4) * DV:(c % 4 + 1) * DV], hh[:, kk, ct], hl[:, kk, ct], wh[:, 2:4, kk], wl[:, 2:4, kk], kk == 0, kk == KC - 1)
                    last.then_inc(v_done, 1)

                def gate_half(u, chunks=range(KC)):
                    pe.wait_ge(w_split, TILES * h + 4 + u // 2 + 1)
                    if u < 2:
                        pe.wait_ge(v_out, 2 * h + 1)
                    else:
                        pe.wait_ge(rg_out, TC * h + u - 1)
                    last = project(ps_b, wh[:, u // 2], wl[:, u // 2], [u % 2], chunks)
                    if chunks[-1] == KC - 1:
                        last.then_inc(rg_done, 1)

                def scores(c):
                    cols = slice(c * P, (c + 1) * P)
                    bank = ps_s
                    if c >= 1:
                        pe.wait_ge(s_masked, TC * h + c)
                    if c == 0:
                        pe.wait_ge(x_ready, (LEVELS + 2) * (h + 1))
                    for n in range(LEVELS):
                        nc.tensor.matmul(bank[:, n * P:(n + 1) * P], X[:, n, cols], X[:, n, cols], start=True, stop=True)
                    nc.tensor.matmul(bank[:, LEVELS * P:], k[:, cols], q[:, cols], start=True, stop=True).then_inc(s_done, 1)

                def turn(c):
                    pe.wait_ge(on_out, TC * h + c + 1)
                    pe.wait_ge(ot_out, TC * h + c)
                    for i in range(2):
                        last = nc.tensor.transpose(ps_t[:, i * P:(i + 1) * P], on[:, c % 2, i * P:(i + 1) * P], ident[:])
                    last.then_inc(ot_done, 1)

                scores(0)
                for i, bank in enumerate((ps_t, ps_o)):
                    for c in range(4):
                        last = nc.tensor.transpose(bank[:, c * P:(c + 1) * P], kd[:, (4 * i + c) * P:(4 * i + c + 1) * P], ident[:])
                    last.then_inc(kt_done, 1)
                gate_half(0)
                for c in range(TC):
                    if c + 1 < TC:
                        scores(c + 1)
                    n = TC * h + c
                    bank = o_banks[c % 2]
                    pe.wait_ge(s_ready, n + 1)
                    if c >= 2:
                        pe.wait_ge(on_out, n - 1)
                    if c == 0:
                        pe.wait_ge(v_out, 2 * h + 2)
                    last = nc.tensor.matmul(bank, S[:, c % 2], V[:, c], start=True, stop=(c == 0))
                    if c == 0:
                        last.then_inc(o_done, 1)
                    else:
                        pe.wait_ge(state_out, n)
                        nc.tensor.matmul(bank, qe[:, c * P:(c + 1) * P], state[:], start=False, stop=True).then_inc(o_done, 1)
                    pe.wait_ge(kt_out, 2 * h + 2)
                    pe.wait_ge(state_out, n)
                    nc.tensor.matmul(ps_o[:, 0:DV], kdT[:, c], V[:, c], start=True, stop=True).then_inc(up_done, 1)
                    if c == TC - 1:
                        gate_half(c, range(KC // 2, KC))
                    if c >= 1:
                        turn(c - 1)
                    if c + 1 < TC:
                        gate_half(c + 1, range(KC // 2) if c + 2 == TC else range(KC))
                turn(TC - 1)

        @block.vector
        def _(dve):
            v = nc.vector
            step = Chain(dve, dve_step)
            dve.wait_ge(small_in, 32)
            dve.wait_ge(const, 2)
            with dve.Fori(0, HEADS) as h:
                step.loop(h, 2 + 4)
                v.tensor_copy(hp[:], hpar[:, bass.ds(h * 3, 3)]).then_inc(hp_ready, 1)
                dve.wait_ge(hp_ready, h + 1)
                dve.wait_ge(z_done, h + 1)
                dve.wait_ge(z_abs, 2 * h + 1)
                v.tensor_scalar(cum, ps_a[:], hp[:, 0:1], 0.0, ALU.add, ALU.min).then_inc(z_min, 1)
                dve.wait_ge(z_min, h + 1)
                dve.wait_ge(l_out, h + 1)
                step(v.tensor_tensor(zl, cum, zl, ALU.subtract))
                dve.wait_ge(z_min, h + 1)
                for c in range(TC):
                    ct = slice(c * P, (c + 1) * P)
                    last = v.tensor_tensor_scan(cum[:, ct], ones[:], zl[:, ct], 0.0, ALU.mult, ALU.add)
                step(last)
                dve.wait_ge(o_done, TC * h)
                for n in range(LEVELS):
                    half = P >> (n + 1)
                    c4 = cum.rearrange("p (b w t) -> p b w t", w=2, t=half)
                    nb = T // (2 * half)
                    middle = c4[:, :, 0:1, half - 1:half].broadcast_to([P, nb, 2, half])
                    v.tensor_tensor(X[:, n].rearrange("p (b w t) -> p b w t", w=2, t=half), c4, middle, ALU.subtract).then_inc(diff_ready, 1)
                c3 = cum.rearrange("p (c t) -> p c t", t=P)
                v.tensor_tensor(kd[:].rearrange("p (c t) -> p c t", t=P), c3, c3[:, :, P - 1:P].broadcast_to([P, TC, P]), ALU.subtract).then_inc(diff_ready, 1)
                dve.wait_ge(q_out, h + 1)
                dve.wait_ge(k_out, h + 1)
                for n in range(LEVELS):
                    half = P >> (n + 1)
                    w4 = lambda t: t.rearrange("p (b w t) -> p b w t", w=2, t=half)
                    dve.wait_ge(exp_out, (LEVELS + 3) * h + n + 1)
                    v.tensor_tensor(w4(X[:, n])[:, :, 0], w4(X[:, n])[:, :, 0], w4(k[:])[:, :, 0], ALU.mult)
                    v.tensor_tensor(w4(X[:, n])[:, :, 1], w4(X[:, n])[:, :, 1], w4(q[:])[:, :, 1], ALU.mult).then_inc(x_ready, 1)
                dve.wait_ge(exp_out, (LEVELS + 3) * h + LEVELS + 3)
                v.tensor_tensor(kd[:], kd[:], k[:], ALU.mult).then_inc(x_ready, 1)
                v.tensor_tensor(qe[:], qe[:], q[:], ALU.mult).then_inc(x_ready, 1)
                def gate_half(u):
                    part = gate[:, u // 2 % 2, u % 2 * HALF:(u % 2 + 1) * HALF]
                    dve.wait_ge(rg_out, TC * h + u + 1)
                    dve.wait_ge(r_raw, 4 * h + min(u + 1, 4))
                    if u >= 4:
                        dve.wait_ge(gate_step, TC * h + u - 3)
                    v.scalar_tensor_tensor(part, tnh[:, u % 2], 1.0, part, ALU.add, ALU.mult).then_inc(gate_step, 1)

                def mask(c):
                    n = TC * h + c
                    dve.wait_ge(s_done, n + 1)
                    dve.wait_ge(s_ready, n)
                    v.tensor_tensor(sm[:], ps_s[:], masks[:], ALU.mult).then_inc(s_masked, 1)
                    dve.wait_ge(s_masked, n + 1)
                    if c >= 2:
                        dve.wait_ge(o_done, n - 1)
                    v.tensor_reduce(S[:, c % 2], sm[:].rearrange("p (l t) -> p t l", l=NL), AX.X, ALU.add).then_inc(s_ready, 1)

                mask(0)
                for c in range(TC):
                    n = TC * h + c
                    if c + 1 < TC:
                        mask(c + 1)
                    dve.wait_ge(up_done, n + 1)
                    up = ps_o[:, 0:DV]
                    dve.wait_ge(o_done, n + 1)
                    if c == 0:
                        v.tensor_copy(state[:], up).then_inc(state_out, 1)
                    else:
                        dve.wait_ge(state_out, n)
                        v.scalar_tensor_tensor(state[:], state[:], elast[:, c:c + 1], up, ALU.mult, ALU.add).then_inc(state_out, 1)
                    if c < TC - 1:
                        gate_half(c)
                    dve.wait_ge(o_root, n + 1)
                    v.reciprocal(rstd[:, c:c + 1], ss[:, c:c + 1]).then_inc(o_rstd, 1)
                gate_half(TC - 1)
                dve.wait_ge(ot_out, TC * (h + 1))
                dve.wait_ge(gate_step, TC * (h + 1))
                dve.wait_ge(mix_in, 16 * (h + 1))
                for i in range(2):
                    step(v.scalar_tensor_tensor(gate[:, i], oT[:, i], hp[:, 1 + i:2 + i], gate[:, i], ALU.mult, ALU.mult))
                    step(v.scalar_tensor_tensor(mix[:, i], gate[:, i], 0.25, mix[:, i], ALU.mult, ALU.add))
                dve.sem_inc(head_out, 1)
            step.end(HEADS)


def peer_block(nc, ctx, keep, a, mod_dram, merged_dram, out):
    ident = keep["ident"]
    R = 8
    GROUPS = TOPK // R
    VR = ND = 4
    with ExitStack() as scope:
        def sb(name, shape, dt=F32):
            return scope.enter_context(nc.sbuf_tensor(name, shape, dt))

        def sem(name):
            return ctx.enter_context(nc.semaphore(name))

        def psum(name, cols):
            return scope.enter_context(nc.psum_tensor(name, [P, cols], F32))

        ps_acc, ps_y, ps_h, ps_sc = psum("ps_acc", D), psum("ps_y", D), psum("ps_h", D), psum("ps_sc", HALF)

        Wk = sb("Wk", [P, KC, 2 * PH * NK])
        w_out = sb("w_out", [P, KC, D])
        mod = sb("mod", [P, 4 * D])
        mT = sb("mT", [P, KC, P])
        x2n, x2c = sb("x2n", [P, D]), sb("x2c", [P, D])
        h2n, h2c = sb("h2n", [P, D]), sb("h2c", [P, D])
        h2T = sb("h2T", [P, KC, P])
        yf = sb("yf", [P, D])
        ur, vr = sb("ur", [P, R, D]), sb("vr", [P, VR, D])
        diag = sb("diag", [P, ND, P])
        zero = sb("zero", [P, P], mybir.dt.bfloat16)
        idx = sb("idx", [P, 2 * SLOTS], U32)
        gates = sb("gates", [P, 2 * SLOTS])
        uidx, vidx = sb("uidx", [P, 2, R], U32), sb("vidx", [P, 2, R], U32)
        sc2 = sb("sc2", [P, 2, NK])
        top = sb("top", [P, 2, TOPK])
        topi = sb("topi", [P, 2, TOPK], U32)
        topf = sb("topf", [P, 2, TOPK])
        best = sb("best", [P, TOPK])
        pos = sb("pos", [P, TOPK], U32)
        ab = sb("ab", [P, 2, TOPK], U32)
        abf = sb("abf", [P, 2, TOPK])
        iota = sb("iota", [P, TOPK])
        eq = sb("eq", [P, 2, TOPK, TOPK])
        pick = sb("pick", [P, 2, TOPK])
        negm = sb("negm", [P, 1])
        esum = sb("esum", [P, 1])
        ex = sb("ex", [P, TOPK])
        dots = sb("dots", [P, R])
        gel = sb("gel", [P, R])
        coef = sb("coef", [P, GROUPS, R])
        eps = sb("eps3", [P, 1])
        ss = sb("ss3", [P, 3])
        rstd = sb("rstd3", [P, 3])

        const, small_in = sem("consts3"), sem("small_in3")
        wout_in = [sem("wout_in0"), sem("wout_in1")]
        wq_in = [sem(f"wq_in{i}") for i in range(4)]
        wk_done, wk_out = sem("wk_done"), sem("wk_out")
        mod_ready = sem("mod_ready")
        x_in, m_in = sem("x_in3"), sem("m_in")
        y_done, y_sq, y_root, y_rstd, y_used = sem("y_done"), sem("y_sq"), sem("y_root"), sem("y_rstd"), sem("y_used")
        x2_ready, h2_ready, h2_turned, h2T_out = sem("x2_ready"), sem("h2_ready"), sem("h2_turned"), sem("h2T_out")
        x2_copied, h2_copied = sem("x2_copied"), sem("h2_copied")
        sc_done, sc_used = sem("sc_done"), sem("sc_used")
        negm_ready, ex_out, sel_ready = sem("negm_ready"), sem("ex_out"), sem("sel_ready")
        ucopy, vcopy, pool_go = sem("ucopy"), sem("vcopy"), keep["go"]
        u_in = [sem(f"u_in{r}") for r in range(R)]
        v_in = [sem(f"v_in{r}") for r in range(VR)]
        u_used, v_used = sem("u_used"), sem("v_used")
        gel_ready, tanh_out, coef_ready, diag_out = sem("gel_ready"), sem("tanh_out"), sem("coef_ready"), sem("diag_out")
        acc_done, acc_out, f_root, f_rstd, f_ready, out_done = (sem(n) for n in ("acc_done", "acc_out", "f_root", "f_rstd", "f_ready", "out_done"))
        dve_step, dve_go = sem("dve_step3"), keep["go"]

        block = scope.enter_context(nc.Block())
        half = lambda s: slice(s * HALF, (s + 1) * HALF)
        wk_banks = (ps_h, ps_acc)

        def group_at(G):
            return bass.ds(G % (2 * SLOTS // R) * R, R)

        @block.sync
        def _(sp):
            def load_keys(g, i):
                sp.dma_start(vr[:, i], a["wqT"][g].rearrange("o p d -> (o p) d")).then_inc(wq_in[i], 16)
                sp.dma_start(diag[:, i], a["keysT"][g].rearrange("o p d -> (o p) d")).then_inc(wq_in[i], 16)

            def merged_tile(t):
                sp.dma_start(mT[:], merged_dram[:, :, bass.ds(t * P, P)]).then_inc(m_in, 16)

            def x_tile(t):
                sp.dma_start(x2n[:], a["x"][bass.ds(t, 1)].rearrange("o p d -> (o p) d")).then_inc(x_in, 16)

            def store_tile(t):
                sp.wait_ge(f_ready, t + 1)
                sp.dma_start(out[bass.ds(t, 1)].rearrange("o p d -> (o p) d"), yf[:]).then_inc(out_done, 16)

            for s in range(2):
                load_keys(slice(s, s + 1), s)
            merged_tile(0)
            for s in range(2):
                sp.dma_start(w_out[:, :, s * HALF:(s + 1) * HALF], a["w_out"][:, :, s * HALF:(s + 1) * HALF]).then_inc(wout_in[s], 16)
            x_tile(0)
            sp.dma_start(mod[:], mod_dram).then_inc(small_in, 16)
            for i, n in enumerate(("gain_post_mix", "gain_pre_ffn", "gain_post_ffn")):
                sp.dma_start(ur[:, 2 + i], a[n].broadcast_to([P, D])).then_inc(small_in, 16)
            for i in range(2, 4):
                load_keys(slice(i, i + 1), i)
            with sp.Fori(0, PH // 2 - 1) as g:
                for i in range(4):
                    sp.wait_ge(wk_done, 4 * g + i + 1)
                    load_keys(bass.ds(4 * g + i + 4, 1), i)
            sp.wait_ge(y_done, 2)
            merged_tile(1)
            with sp.Fori(1, TC - 1) as t:
                sp.wait_ge(x2_copied, t)
                x_tile(t)
                sp.wait_ge(y_done, 2 * t + 2)
                merged_tile(t + 1)
                store_tile(t - 1)
            sp.wait_ge(x2_copied, TC - 1)
            x_tile(TC - 1)
            store_tile(TC - 2)
            store_tile(TC - 1)
            sp.wait_ge(out_done, 16 * TC)

        @block.gpsimd
        def _(pool):
            nc.gpsimd.memset(eps[:], EPS).then_inc(const, 1)
            nc.gpsimd.memset(zero[:], 0.0).then_inc(const, 1)
            nc.gpsimd.iota(iota[:], [[1, TOPK]], base=0, channel_multiplier=0, allow_small_or_imprecise_dtypes=True).then_inc(const, 1)

            def copy_indices(G, par, to, copied):
                pool.sem_inc(pool_go, 1)
                nc.gpsimd.tensor_copy(to[:, par], idx[:, group_at(G)]).then_inc(copied, 1)
                pool.wait_ge(copied, G + 1)

            def gather_u(G, par, r, first=False):
                if not first:
                    pool.wait_ge(u_used, R * (G - 1) + r + 1)
                pool.sem_inc(pool_go, 1)
                pool.indirect_dma_start(ur[:, r], None, a["u"], bass.IndirectOffsetOnAxis(ap=uidx[:, par, r:r + 1], axis=0)).then_inc(u_in[r], 16)

            def gather_v(G, par, r):
                pool.wait_ge(v_used, R * G + r + 1)
                pool.sem_inc(pool_go, 1)
                pool.indirect_dma_start(vr[:, r % VR], None, a["v"], bass.IndirectOffsetOnAxis(ap=vidx[:, par, r:r + 1], axis=0)).then_inc(v_in[r % VR], 16)

            def both(G, par):
                copy_indices(G + 1, 1 - par, uidx, ucopy)
                copy_indices(G, par, vidx, vcopy)
                for r in range(R):
                    gather_u(G + 1, 1 - par, r)
                    gather_v(G, par, r)

            pool.wait_ge(mod_ready, 1)
            pool.wait_ge(sel_ready, 1)
            copy_indices(0, 0, uidx, ucopy)
            for r in range(R):
                gather_u(0, 0, r, first=True)
            pool.wait_ge(wk_done, 2 * PH)
            with pool.Fori(0, TC * PH - 1) as H:
                both(2 * H, 0)
                pool.wait_ge(sel_ready, H + 2)
                both(2 * H + 1, 1)
            last = 2 * TC * PH - 1
            both(last - 1, 0)
            copy_indices(last, 1, vidx, vcopy)
            for r in range(R):
                gather_v(last, 1, r)

        @block.scalar
        def _(act):
            S = nc.scalar
            act.wait_ge(const, 3)
            act.sem_inc(diag_out, R)

            def mixer_norm(t, stored):
                act.wait_ge(y_done, 2 * t + 2)
                if stored is not None:
                    act.wait_ge(out_done, 16 * stored)
                S.activation(yf[:], ps_y[:], ACT.Square, scale=D ** -0.5, accum_out=ss[:, 0:1]).then_inc(y_sq, 1)
                act.wait_ge(y_sq, 2 * t + 1)
                S.activation(ss[:, 0:1], ss[:, 0:1], ACT.Sqrt, bias=eps[:]).then_inc(y_root, 1)

            def expert_norm(t):
                act.wait_ge(x2_ready, t + 1)
                S.activation(yf[:], x2n[:], ACT.Square, scale=D ** -0.5, accum_out=ss[:, 1:2]).then_inc(y_sq, 1)
                act.wait_ge(y_sq, 2 * t + 2)
                S.activation(ss[:, 1:2], ss[:, 1:2], ACT.Sqrt, bias=eps[:]).then_inc(y_root, 1)

            def tile_turned(t):
                act.wait_ge(h2_turned, t + 1)
                S.activation(h2T[:].rearrange("p k t -> p (k t)"), ps_h[:], ACT.Copy).then_inc(h2T_out, 1)

            def select_gates(n):
                act.wait_ge(negm_ready, n + 1)
                S.activation(ex[:], best[:], ACT.Exp, bias=negm[:], accum_out=esum[:]).then_inc(ex_out, 1)

            def experts(G, par):
                act.wait_ge(gel_ready, G + 1)
                S.activation(gel[:], gel[:], ACT.Tanh, scale=GELU_B).then_inc(tanh_out, 1)
                act.wait_ge(coef_ready, G + 1)
                for r in range(R):
                    act.wait_ge(v_used, R * G + r + 1)
                    S.activation(diag[:, r % ND], ident[:], ACT.Copy, scale=coef[:, par, r:r + 1]).then_inc(diag_out, 1)

            def finish(t):
                act.wait_ge(acc_done, t + 1)
                act.wait_ge(out_done, 16 * t)
                S.activation(yf[:], ps_acc[:], ACT.Square, scale=D ** -0.5, accum_out=ss[:, 2:3]).then_inc(f_root, 1)
                act.wait_ge(f_root, 2 * t + 1)
                S.activation(yf[:], ps_acc[:], ACT.Copy).then_inc(acc_out, 1)
                S.activation(ss[:, 2:3], ss[:, 2:3], ACT.Sqrt, bias=eps[:]).then_inc(f_root, 1)

            def take_h2(t):
                act.wait_ge(h2_ready, t + 1)
                act.wait_ge(u_used, SLOTS * t)
                S.activation(h2c[:], h2n[:], ACT.Copy).then_inc(h2_copied, 1)

            def take_x2(t):
                act.wait_ge(f_ready, t)
                S.activation(x2c[:], x2n[:], ACT.Copy).then_inc(x2_copied, 1)

            def head(H, select=True):
                for s in range(GROUPS):
                    experts(GROUPS * H + s, s)
                if select:
                    select_gates(H + 2)

            def keys_out(g, sides=range(2)):
                for s in sides:
                    act.wait_ge(wk_done, 2 * g + s + 1)
                    S.activation(Wk[:, :, bass.ds((2 * g + s) * NK, NK)], wk_banks[s][:].rearrange("p (k n) -> p k n", k=KC), ACT.Copy).then_inc(wk_out, 1)

            keys_out(0)
            mixer_norm(0, None)
            keys_out(1, [0])
            expert_norm(0)
            keys_out(1, [1])
            tile_turned(0)
            take_h2(0)
            take_x2(0)
            select_gates(0)
            with act.Fori(1, PH // 2) as g:
                keys_out(2 * g)
                keys_out(2 * g + 1)
            select_gates(1)
            with act.Fori(0, TC - 1) as t:
                with act.Fori(0, 2) as h:
                    head(PH * t + h)
                mixer_norm(t + 1, t)
                with act.Fori(2, 4) as h:
                    head(PH * t + h)
                expert_norm(t + 1)
                with act.Fori(4, PH - 2) as h:
                    head(PH * t + h)
                tile_turned(t + 1)
                with act.Fori(PH - 2, PH) as h:
                    head(PH * t + h)
                take_h2(t + 1)
                finish(t)
                take_x2(t + 1)
            with act.Fori(PH * (TC - 1), PH * TC - 2) as H:
                head(H)
            for H in range(PH * TC - 2, PH * TC):
                head(H, select=False)
            finish(TC - 1)

        @block.tensor
        def _(pe):
            pe.sem_inc(v_used, VR)
            def tile_half(t, s):
                pe.wait_ge(m_in, 16 * (t + 1))
                pe.wait_ge(y_used, t)
                for k in range(KC):
                    last = nc.tensor.matmul(ps_y[:, bass.ds(s * HALF, HALF)], mT[:, k], w_out[:, k, bass.ds(s * HALF, HALF)], start=(k == 0), stop=(k == KC - 1))
                last.then_inc(y_done, 1)

            def tile_turn(t):
                pe.wait_ge(h2_ready, t + 1)
                pe.wait_ge(h2T_out, t)
                for k in range(KC):
                    last = nc.tensor.transpose(ps_h[:, k * P:(k + 1) * P], h2n[:, k * P:(k + 1) * P], ident[:])
                last.then_inc(h2_turned, 1)

            def scores(n, t, h):
                pe.wait_ge(h2T_out, t + 1)
                pe.wait_ge(sc_used, n)
                for k in range(KC):
                    last = nc.tensor.matmul(ps_sc[:, 0:2 * NK], h2T[:, k], Wk[:, k, bass.ds(h * 2 * NK, 2 * NK)], start=(k == 0), stop=(k == KC - 1))
                last.then_inc(sc_done, 1)

            def edge(start):
                for s in range(2):
                    last = nc.tensor.matmul(ps_acc[:, half(s)], zero[:], zero[:, 0:1].broadcast_to([P, HALF]), start=start, stop=not start, skip_group_check=True)
                return last

            def experts(G):
                for r in range(R):
                    pe.wait_ge(diag_out, R * (G + 1) + r + 1)
                    pe.wait_ge(v_in[r % VR], 16 * (R // VR * G + r // VR + 1))
                    for s in range(2):
                        last = nc.tensor.matmul(ps_acc[:, half(s)], diag[:, r % ND], vr[:, r % VR, half(s)], start=False, stop=False, skip_group_check=True)
                    last.then_inc(v_used, 1)

            def head(H):
                for s in range(GROUPS):
                    experts(GROUPS * H + s)

            pe.wait_ge(const, 3)
            def keys(g, par, wait=True):
                for s in range(2):
                    i = 2 * par + s
                    pe.wait_ge(wq_in[i], 32 * (g + 1))
                    if wait:
                        pe.wait_ge(wk_out, 4 * g + i - 1)
                    for k in range(KC):
                        last = nc.tensor.matmul(wk_banks[s][:, k * P:(k + 1) * P], vr[:, i, k * P:(k + 1) * P], diag[:, i], start=True, stop=True)
                    last.then_inc(wk_done, 1)

            keys(0, 0, wait=False)
            for s in range(2):
                pe.wait_ge(wout_in[s], 16)
                tile_half(0, s)
            keys(0, 1)
            pe.wait_ge(wk_out, 4)
            tile_turn(0)
            for h in range(2):
                scores(h, 0, h)
            with pe.Fori(1, PH // 2) as g:
                for par in range(2):
                    keys(g, par)
            pe.wait_ge(wk_out, 2 * PH)
            with pe.Fori(0, TC - 1) as t:
                pe.wait_ge(acc_out, t)
                edge(True)
                with pe.Fori(0, 2) as h:
                    scores(PH * t + h + 2, t, h + 2)
                    tile_half(t + 1, h)
                    head(PH * t + h)
                with pe.Fori(2, PH - 2) as h:
                    scores(PH * t + h + 2, t, h + 2)
                    head(PH * t + h)
                tile_turn(t + 1)
                with pe.Fori(PH - 2, PH) as h:
                    scores(PH * t + h + 2, t + 1, h - (PH - 2))
                    head(PH * t + h)
                edge(False).then_inc(acc_done, 1)
            pe.wait_ge(acc_out, TC - 1)
            edge(True)
            with pe.Fori(0, PH - 2) as h:
                scores(PH * (TC - 1) + h + 2, TC - 1, h + 2)
                head(PH * (TC - 1) + h)
            for H in range(PH * TC - 2, PH * TC):
                head(H)
            edge(False).then_inc(acc_done, 1)

        @block.vector
        def _(dve):
            v = nc.vector
            step = Chain(dve, dve_step)
            g1, shift2, scale2, g2 = (mod[:, i * D:(i + 1) * D] for i in range(4))
            dve.wait_ge(small_in, 64)
            dve.wait_ge(const, 3)
            step(v.tensor_tensor(g1, g1, ur[:, 2], ALU.mult))
            step(v.scalar_tensor_tensor(scale2, scale2, 1.0, ur[:, 3], ALU.add, ALU.mult))
            v.tensor_tensor(g2, g2, ur[:, 4], ALU.mult).then_inc(mod_ready, 1)
            dve.wait_ge(mod_ready, 1)

            def mixer_norm(t):
                dve.wait_ge(y_root, 2 * t + 1)
                v.reciprocal(rstd[:, 0:1], ss[:, 0:1]).then_inc(y_rstd, 1)
                dve.wait_ge(y_rstd, 2 * t + 1)
                dve.wait_ge(h2_copied, t)
                v.scalar_tensor_tensor(h2n[:], ps_y[:], rstd[:, 0:1], g1, ALU.mult, ALU.mult).then_inc(y_used, 1)
                dve.wait_ge(y_used, t + 1)
                dve.wait_ge(x_in, 16 * (t + 1))
                v.tensor_tensor(x2n[:], x2n[:], h2n[:], ALU.add).then_inc(x2_ready, 1)

            def expert_norm(t):
                dve.wait_ge(x2_ready, t + 1)
                dve.wait_ge(y_root, 2 * t + 2)
                v.reciprocal(rstd[:, 1:2], ss[:, 1:2]).then_inc(y_rstd, 1)
                dve.wait_ge(y_rstd, 2 * t + 2)
                step(v.scalar_tensor_tensor(h2n[:], x2n[:], rstd[:, 1:2], scale2, ALU.mult, ALU.mult))
                v.tensor_tensor(h2n[:], h2n[:], shift2, ALU.add).then_inc(h2_ready, 1)

            SELECT_STEPS = 8 + 1 + 4 + 10

            def alone():
                dve.sem_inc(dve_go, 1)

            def top16(values, spare, out, index):
                for n in range(2):
                    o, i = out[:, 8 * n:8 * n + 8], index[:, 8 * n:8 * n + 8]
                    alone()
                    step(v.max(o, values))
                    alone()
                    if n == 0:
                        v.max_index(i, o, values)
                        step(v.match_replace(spare, o, values, NEG))
                        values = spare
                    else:
                        step(v.max_index(i, o, values))

            def select_sides(n):
                dve.wait_ge(sc_done, n + 1)
                for p in range(2):
                    top16(ps_sc[:, p * NK:(p + 1) * NK], sc2[:, p], top[:, p], topi[:, p])
                dve.sem_inc(sc_used, 1)

            def select_pairs(n):
                cand = eq[:, 0]
                step(v.tensor_tensor(cand, top[:, 0].unsqueeze(2).broadcast_to([P, TOPK, TOPK]), top[:, 1].unsqueeze(1).broadcast_to([P, TOPK, TOPK]), ALU.add))
                dve.wait_ge(ex_out, n)
                top16(cand.rearrange("p a b -> p (a b)"), eq[:, 1].rearrange("p a b -> p (a b)"), best, pos)
                v.tensor_scalar(negm[:], best[:, 0:1], -1.0, None, ALU.mult).then_inc(negm_ready, 1)
                step(v.tensor_scalar(ab[:, 0], pos[:], 4, None, ALU.logical_shift_right))
                step(v.tensor_scalar(ab[:, 1], pos[:], TOPK - 1, None, ALU.bitwise_and))
                step(v.tensor_copy(abf[:], ab[:]))
                step(v.tensor_copy(topf[:], topi[:]))
                for p in range(2):
                    last = v.tensor_tensor(eq[:, p], abf[:, p].unsqueeze(2).broadcast_to([P, TOPK, TOPK]), iota[:].unsqueeze(1).broadcast_to([P, TOPK, TOPK]), ALU.is_equal)
                step(last)
                for p in range(2):
                    last = v.tensor_tensor(eq[:, p], eq[:, p], topf[:, p].unsqueeze(1).broadcast_to([P, TOPK, TOPK]), ALU.mult)
                step(last)
                step(v.tensor_reduce(pick[:], eq[:], AX.X, ALU.add))
                step(v.scalar_tensor_tensor(idx[:, bass.ds(n % (2 * PH) * TOPK, TOPK)], pick[:, 0], float(NK), pick[:, 1], ALU.mult, ALU.add))
                dve.wait_ge(ex_out, n + 1)
                step(v.reciprocal(esum[:], esum[:]))
                step(v.tensor_scalar(gates[:, bass.ds(n % (2 * PH) * TOPK, TOPK)], ex[:], esum[:], 0.5, ALU.mult, ALU.mult))
                dve.sem_inc(sel_ready, 1)

            def products(G):
                for r in range(R):
                    dve.wait_ge(u_in[r], 16 * (G + 1))
                    last = v.scalar_tensor_tensor(ur[:, r], ur[:, r], 1.0, h2c[:], ALU.mult, ALU.mult, accum_out=dots[:, r:r + 1])
                    last.then_inc(u_used, 1)

            def coefficients(G, par):
                dve.wait_ge(u_used, R * (G + 1))
                step(v.scalar_tensor_tensor(gel[:], dots[:], GELU_A, dots[:], ALU.mult, ALU.mult))
                v.scalar_tensor_tensor(gel[:], gel[:], 1.0, dots[:], ALU.add, ALU.mult).then_inc(gel_ready, 1)
                dve.wait_ge(tanh_out, G + 1)
                step(v.scalar_tensor_tensor(gel[:], gel[:], 1.0, dots[:], ALU.add, ALU.mult))
                dve.wait_ge(diag_out, R * G)
                v.tensor_tensor(coef[:, par], gel[:], gates[:, group_at(G)], ALU.mult).then_inc(coef_ready, 1)

            def finish(t):
                dve.wait_ge(f_root, 2 * t + 2)
                v.reciprocal(rstd[:, 2:3], ss[:, 2:3]).then_inc(f_rstd, 1)
                dve.wait_ge(f_rstd, t + 1)
                dve.wait_ge(acc_out, t + 1)
                step(v.scalar_tensor_tensor(yf[:], yf[:], rstd[:, 2:3], g2, ALU.mult, ALU.mult))
                v.tensor_tensor(yf[:], yf[:], x2c[:], ALU.add).then_inc(f_ready, 1)

            HEAD_STEPS = 2 * GROUPS + SELECT_STEPS

            def head(H, take=None, select=True, more=True):
                coefficients(GROUPS * H, 0)
                if select:
                    select_sides(H + 2)
                products(GROUPS * H + 1)
                coefficients(GROUPS * H + 1, 1)
                if select:
                    select_pairs(H + 2)
                if take is not None:
                    dve.wait_ge(h2_copied, take + 1)
                    alone()
                if more:
                    products(GROUPS * (H + 1))

            mixer_norm(0)
            expert_norm(0)
            for n in range(2):
                select_sides(n)
                select_pairs(n)
            dve.wait_ge(h2_copied, 1)
            alone()
            products(0)
            with dve.Fori(0, TC - 1) as t:
                step.loop(t, PH * HEAD_STEPS + 2)
                for first, last in ((0, 3), (3, 5), (5, PH - 1)):
                    with dve.Fori(first, last) as h:
                        step.loop(h - first, HEAD_STEPS)
                        head(PH * t + h)
                    step.end(last - first)
                    if first == 0:
                        mixer_norm(t + 1)
                    if first == 3:
                        expert_norm(t + 1)
                head(PH * t + PH - 1, take=t + 1)
                finish(t)
            step.end(TC - 1)
            with dve.Fori(0, PH - 2) as h:
                step.loop(h, HEAD_STEPS)
                head(PH * (TC - 1) + h)
            step.end(PH - 2)
            for H in range(PH * TC - 2, PH * TC):
                head(H, select=False, more=H < PH * TC - 1)
            finish(TC - 1)


def build(nc, a, out):
    with ExitStack() as ctx:
        merged_dram = nc.dram_tensor("merged_scratch", (P, KC, T), F32, kind="Internal").ap()
        mod_dram = nc.dram_tensor("mod_scratch", (P, 4 * D), F32, kind="Internal").ap()
        keep = {"ident": ctx.enter_context(nc.sbuf_tensor("ident", [P, P], F32)),
                "go": ctx.enter_context(nc.semaphore("go"))}
        with nc.sbuf_tensor("hh", [P, KC, T], F32R) as hh, nc.sbuf_tensor("hl", [P, KC, T], F32R) as hl, nc.sbuf_tensor("alow", [RANK, T], F32) as alow:
            keep["hh"], keep["hl"], keep["alow"] = hh, hl, alow
            conditioning_and_lru(nc, ctx, keep, a, mod_dram, merged_dram)
            gated_linear_attention(nc, ctx, keep, a, merged_dram)
        peer_block(nc, ctx, keep, a, mod_dram, merged_dram, out)


def layout(inputs):
    import numpy as np
    g = {k: np.asarray(v) for k, v in inputs.items()}
    ch = lambda w: w.reshape(KC, P, -1).transpose(1, 0, 2)
    col = lambda w: np.ascontiguousarray(w.reshape(KC, P).T)
    a = {}
    a["x"] = g["x"].reshape(TC, P, D)
    a["cT"] = col(g["c"][0])
    a["gain1"] = col(g["norm_pre_mix"][0])
    a["w_ada"] = ch(g["w_ada"][0]).reshape(P, KC, 4 * MODS, 256).transpose(2, 0, 1, 3)
    a["b_ada"] = g["b_ada"][0].reshape(4 * MODS, 256)
    a["ident"] = np.eye(P, dtype=np.float32)
    w = ch(g["w_in"][0])
    off = np.cumsum([0, 512, 512, 1024, 1024, RANK, D, D, D, D])
    q, k, v, r, al, xl, xg, ga, gb = (w[:, :, off[i]:off[i + 1]] for i in range(9))
    blocks = lambda m: m.reshape(P, KC, -1, P).transpose(2, 0, 1, 3)
    again = lambda m: np.concatenate([m, m[-1:]])
    a["w_lru"] = again(np.stack([blocks(xl), blocks(xg), blocks(gb)], 1))
    par = np.stack([g["conv_w"][0][i] for i in range(4)] + [g["conv_b"][0], g["lru_b_a"][0].reshape(-1), g["lru_b_x"][0].reshape(-1), g["lru_lambda"][0]], -1)
    a["lru_par"] = par.reshape(KC, P, NPAR).transpose(1, 0, 2).reshape(P, KC * NPAR)
    a["lru_w"] = again(np.stack([g["lru_w_a"][0], g["lru_w_x"][0]], 2))
    pair = lambda m: blocks(m).reshape(HEADS, 2, P, KC, P)
    a["w_head"] = np.concatenate([blocks(q)[:, None], blocks(k)[:, None], pair(v), pair(r), pair(ga)], 1).reshape(-1, P, KC, P)
    a["w_al"] = al
    a["w_alpha"] = g["w_alpha"][0].reshape(RANK, HEADS, DK).transpose(1, 0, 2)
    a["head_par"] = np.concatenate([g["b_alpha"][0].reshape(HEADS, DK).T.reshape(P, HEADS, 1), g["gla_norm"][0].reshape(HEADS, 2, P).transpose(2, 0, 1)], 2).reshape(P, HEADS * 3)
    s, t = np.arange(P)[:, None], np.arange(P)[None, :]
    halvings = [((s // b == t // b) & (s % b < b // 2) & (t % b >= b // 2)) for b in (P >> n for n in range(LEVELS))] + [s == t]
    a["masks"] = np.concatenate(halvings, 1).astype(np.float32)
    a["w_out"] = ch(g["w_out"][0])
    a["gain_post_mix"] = g["norm_post_mix"]
    a["gain_pre_ffn"] = g["norm_pre_ffn"]
    a["gain_post_ffn"] = g["norm_post_ffn"]
    a["wqT"] = g["peer_w_query"][0].reshape(D, PH * 2, P).transpose(1, 2, 0)
    a["keysT"] = g["peer_sub_keys"][0].reshape(PH * 2, NK, P).transpose(0, 2, 1)
    a["u"] = g["peer_u"][0]
    a["v"] = g["peer_v"][0]
    return {k: np.ascontiguousarray(v) for k, v in a.items()}


def kernel(**inputs):
    import numpy as np
    import concourse.bacc as bacc
    from concourse.bass_utils import run_bass_kernel_spmd

    arrays = {f"in_{k}": v for k, v in layout(inputs).items()}
    nc = bacc.Bacc("TRN2", target_bir_lowering=False, num_devices=1)
    a = {k[3:]: nc.dram_tensor(k, v.shape, mybir.dt.from_np(v.dtype), kind="ExternalInput").ap() for k, v in arrays.items()}
    out = nc.dram_tensor("out_y", (TC, P, D), F32, kind="ExternalOutput").ap()
    build(nc, a, out)
    r = run_bass_kernel_spmd(nc, [arrays], core_ids=[0])
    return np.asarray(r.results[0]["out_y"]).reshape(1, T, D)
```
